# Optimizing a Trainium2 kernel written in Bass

```python
import math
import jax
import jax.numpy as jnp
from jax import lax
import numpy as np

D_MODEL = 1024
BATCH = 1
SEQ = 512
DEPTH = 2

NORM_EPS = 1e-6
PLE_DIM = 256
D_FF = 2816
FFN_HALF = 0.5
BRANCH_WIDTH = D_MODEL // 2
N_BRANCHES = 3
MASK_VALUE = -1e30

ATTN_HEAD_DIM = 64
ATTN_HEADS = BRANCH_WIDTH // ATTN_HEAD_DIM
ATTN_KV_HEADS = ATTN_HEADS // 4
ATTN_GROUP = ATTN_HEADS // ATTN_KV_HEADS
WINDOW = 128
ATTN_BLOCK = 128
ATTN_SCALE = ATTN_HEAD_DIM ** -0.5
ATTN_IN = (ATTN_HEADS + 2 * ATTN_KV_HEADS) * ATTN_HEAD_DIM

RWKV_HEAD_DIM = 64
RWKV_HEADS = BRANCH_WIDTH // RWKV_HEAD_DIM
RWKV_W_RANK = 64
RWKV_A_RANK = 64
RWKV_G_RANK = 128
RWKV_GN_EPS = 64e-5
RWKV_DECAY_SCALE = math.exp(-0.5)
RWKV_WIDTHS = (BRANCH_WIDTH, BRANCH_WIDTH, BRANCH_WIDTH, RWKV_W_RANK, RWKV_A_RANK, RWKV_G_RANK)
RWKV_OFFSETS = tuple(int(o) for o in np.cumsum(RWKV_WIDTHS)[:-1])
RWKV_IN = sum(RWKV_WIDTHS)

HGRN_KEY_DIM = 128
HGRN_HEADS = BRANCH_WIDTH // HGRN_KEY_DIM
HGRN_VAL_DIM = BRANCH_WIDTH // HGRN_HEADS
HGRN_CHUNK = 64
HGRN_IN = 4 * BRANCH_WIDTH

GATE_IN = N_BRANCHES * D_MODEL
GROUP_WIDTHS = (ATTN_IN, RWKV_IN, HGRN_IN, GATE_IN)
GROUP_OFFSETS = tuple(int(o) for o in np.cumsum(GROUP_WIDTHS)[:-1])
IN_WIDTH = sum(GROUP_WIDTHS)

kernel_name = 'hybrid_gated_swa_rwkv7_hgrn2_block'

def rmsnorm(x, g, eps=NORM_EPS):
    xf = x.astype(jnp.float32)
    y = xf * lax.rsqrt(jnp.mean(xf * xf, axis=-1, keepdims=True) + eps)
    return (y * g.astype(jnp.float32)).astype(x.dtype)

def swiglu(x, w_gate, w_up, w_down):
    return (jax.nn.silu(x @ w_gate) * (x @ w_up)) @ w_down

def sliding_window_attention(q, k, v, sinks):
    B, L, _ = q.shape
    nb = L // ATTN_BLOCK
    qb = q.reshape(B, nb, ATTN_BLOCK, ATTN_KV_HEADS, ATTN_GROUP, ATTN_HEAD_DIM)

    def band(t):
        t = t.reshape(B, nb, ATTN_BLOCK, ATTN_KV_HEADS, ATTN_HEAD_DIM)
        prev = jnp.pad(t, ((0, 0), (1, 0), (0, 0), (0, 0), (0, 0)))[:, :-1]
        return jnp.concatenate([prev, t], axis=2)

    kb, vb = band(k), band(v)
    scores = jnp.einsum('bnqhgd,bnkhd->bnhgqk', qb, kb).astype(jnp.float32) * ATTN_SCALE
    qi = jnp.arange(ATTN_BLOCK)[:, None]
    kj = jnp.arange(2 * ATTN_BLOCK)[None, :]
    rel = ATTN_BLOCK + qi - kj
    in_band = (rel >= 0) & (rel < WINDOW)
    not_pad = (jnp.arange(nb)[:, None, None] > 0) | (kj[None] >= ATTN_BLOCK)
    mask = in_band[None] & not_pad
    scores = jnp.where(mask[None, :, None, None], scores, MASK_VALUE)
    sink = sinks.astype(jnp.float32).reshape(ATTN_KV_HEADS, ATTN_GROUP)[None, None, :, :, None, None]
    m = jnp.maximum(jnp.max(scores, axis=-1, keepdims=True), sink)
    pr = jnp.exp(scores - m)
    denom = jnp.sum(pr, axis=-1, keepdims=True) + jnp.exp(sink - m)
    out = jnp.einsum('bnhgqk,bnkhd->bnqhgd', (pr / denom).astype(v.dtype), vb)
    return out.reshape(B, L, ATTN_HEADS * ATTN_HEAD_DIM)

def rwkv7_mix(z, mu, w0, w_up, a0, a_up, g_up, k_k, k_a, r_k, ln_w, ln_b):
    B, L, _ = z.shape
    f32 = jnp.float32
    z = z.astype(f32)
    z_prev = jnp.pad(z, ((0, 0), (1, 0), (0, 0)))[:, :-1]
    z = z + mu * (z_prev - z)
    r, k, v, xw, xa, xg = jnp.split(z, RWKV_OFFSETS, axis=-1)
    d = w0 + jnp.tanh(xw) @ w_up
    decay = jnp.exp(-RWKV_DECAY_SCALE * jax.nn.sigmoid(d))
    a = jax.nn.sigmoid(a0 + xa @ a_up)
    g = jax.nn.sigmoid(xg) @ g_up
    heads = lambda t: t.reshape(B, L, RWKV_HEADS, RWKV_HEAD_DIM)
    kk = heads(k * k_k)
    kk = kk * lax.rsqrt(jnp.maximum(jnp.sum(kk * kk, axis=-1, keepdims=True), 1e-24))
    k = k * (1.0 + (a - 1.0) * k_a)
    r_h, k_h, v_h, a_h, w_h = heads(r), heads(k), heads(v), heads(a), heads(decay)
    b_h = kk * a_h

    def step(S, inp):
        r_t, w_t, k_t, v_t, kk_t, b_t = inp
        sa = jnp.einsum('bhvk,bhk->bhv', S, -kk_t)
        S = S * w_t[:, :, None, :] + sa[..., None] * b_t[:, :, None, :] + v_t[..., None] * k_t[:, :, None, :]
        return S, jnp.einsum('bhvk,bhk->bhv', S, r_t)

    xs = tuple(jnp.moveaxis(t, 1, 0) for t in (r_h, w_h, k_h, v_h, kk, b_h))
    S0 = jnp.zeros((B, RWKV_HEADS, RWKV_HEAD_DIM, RWKV_HEAD_DIM), f32)
    _, y = lax.scan(step, S0, xs)
    y = jnp.moveaxis(y, 0, 1)
    mean = jnp.mean(y, axis=-1, keepdims=True)
    var = jnp.mean(jnp.square(y - mean), axis=-1, keepdims=True)
    y = ((y - mean) * lax.rsqrt(var + RWKV_GN_EPS)).reshape(B, L, BRANCH_WIDTH) * ln_w + ln_b
    bonus = jnp.sum(r_h * k_h * r_k, axis=-1, keepdims=True) * v_h
    y = y + bonus.reshape(B, L, BRANCH_WIDTH)
    return y * g

def hgrn2_mix(z, lb, norm_g):
    B, L, _ = z.shape
    f32 = jnp.float32
    z = z.astype(f32)
    q, f, i, og = jnp.split(z, 4, axis=-1)
    lb = lb.astype(f32)
    forget = lb + (1.0 - lb) * jax.nn.sigmoid(f)
    log_f = jnp.log(forget)
    key = 1.0 - forget
    q = jax.nn.silu(q)
    nc = L // HGRN_CHUNK

    def chunks(t, dim):
        return t.reshape(B, nc, HGRN_CHUNK, HGRN_HEADS, dim).transpose(1, 0, 3, 2, 4)

    xs = (chunks(q, HGRN_KEY_DIM), chunks(key, HGRN_KEY_DIM), chunks(i, HGRN_VAL_DIM), chunks(log_f, HGRN_KEY_DIM))
    causal = jnp.tril(jnp.ones((HGRN_CHUNK, HGRN_CHUNK), bool))[:, :, None]

    def step(S, inp):
        q_c, k_c, v_c, g_c = inp
        b = jnp.cumsum(g_c, axis=-2)
        rel = b[..., :, None, :] - b[..., None, :, :]
        dec = jnp.where(causal, jnp.exp(jnp.where(causal, rel, 0.0)), 0.0)
        attn = jnp.einsum('bhtk,bhsk,bhtsk->bhts', q_c, k_c, dec)
        o = attn @ v_c + jnp.einsum('bhtk,bhkv->bhtv', q_c * jnp.exp(b), S)
        b_last = b[..., -1:, :]
        S = jnp.exp(b_last[..., 0, :])[..., None] * S + jnp.einsum('bhsk,bhsv->bhkv', k_c * jnp.exp(b_last - b), v_c)
        return S, o

    S0 = jnp.zeros((B, HGRN_HEADS, HGRN_KEY_DIM, HGRN_VAL_DIM), f32)
    _, o = lax.scan(step, S0, xs)
    o = o.transpose(1, 0, 3, 2, 4).reshape(B, L, HGRN_HEADS, HGRN_VAL_DIM)
    o = rmsnorm(o, norm_g).reshape(B, L, BRANCH_WIDTH)
    return o * jax.nn.silu(og)

def token_mixer(u, w_in, attn_sinks, rwkv_mu, rwkv_w0, rwkv_w_up, rwkv_a0, rwkv_a_up, rwkv_g_up,
                rwkv_k_k, rwkv_k_a, rwkv_r_k, rwkv_ln_w, rwkv_ln_b, lb, hgrn_norm, w_branch, w_o):
    B, L, _ = u.shape
    z = u @ w_in
    z_attn, z_rwkv, z_hgrn, z_gate = jnp.split(z, GROUP_OFFSETS, axis=-1)
    q_w = ATTN_HEADS * ATTN_HEAD_DIM
    kv_w = ATTN_KV_HEADS * ATTN_HEAD_DIM
    q, k, v = jnp.split(z_attn, [q_w, q_w + kv_w], axis=-1)
    y_a = sliding_window_attention(q, k, v, attn_sinks).astype(jnp.float32)
    y_b = rwkv7_mix(z_rwkv, rwkv_mu, rwkv_w0, rwkv_w_up, rwkv_a0, rwkv_a_up, rwkv_g_up,
                    rwkv_k_k, rwkv_k_a, rwkv_r_k, rwkv_ln_w, rwkv_ln_b)
    y_c = hgrn2_mix(z_hgrn, lb, hgrn_norm)
    ys = jnp.stack([y_a, y_b, y_c], axis=2).astype(u.dtype)
    up = jnp.einsum('blnw,nwd->blnd', ys, w_branch)
    gates = jax.nn.sigmoid(z_gate).reshape(B, L, N_BRANCHES, D_MODEL)
    merged = jnp.sum(gates * up, axis=2)
    return merged @ w_o

def _normal(key, shape, scale):
    return jax.random.normal(key, shape, jnp.float32) * scale

def setup_inputs(seed: int = 0) -> dict:
    key = jax.random.key(seed)
    ks = iter(jax.random.split(key, 40))
    gain = lambda shape: 1.0 + _normal(next(ks), shape, 0.05)
    Dp = DEPTH
    inp = {}
    inp['x'] = _normal(next(ks), (BATCH, SEQ, D_MODEL), 1.0)
    inp['p'] = _normal(next(ks), (DEPTH, BATCH, SEQ, PLE_DIM), 1.0)
    inp['ffn1_norm'] = gain((Dp, D_MODEL))
    inp['ffn1_w_gate'] = _normal(next(ks), (Dp, D_MODEL, D_FF), D_MODEL ** -0.5)
    inp['ffn1_w_up'] = _normal(next(ks), (Dp, D_MODEL, D_FF), D_MODEL ** -0.5)
    inp['ffn1_w_down'] = _normal(next(ks), (Dp, D_FF, D_MODEL), D_FF ** -0.5)
    inp['mix_norm'] = gain((Dp, D_MODEL))
    inp['w_in'] = _normal(next(ks), (Dp, D_MODEL, IN_WIDTH), D_MODEL ** -0.5)
    inp['attn_sinks'] = _normal(next(ks), (Dp, ATTN_HEADS), 0.5)
    inp['rwkv_mu'] = jax.random.uniform(next(ks), (Dp, RWKV_IN), jnp.float32)
    inp['rwkv_w0'] = _normal(next(ks), (Dp, BRANCH_WIDTH), 0.5)
    inp['rwkv_w_up'] = _normal(next(ks), (Dp, RWKV_W_RANK, BRANCH_WIDTH), RWKV_W_RANK ** -0.5)
    inp['rwkv_a0'] = _normal(next(ks), (Dp, BRANCH_WIDTH), 0.1)
    inp['rwkv_a_up'] = _normal(next(ks), (Dp, RWKV_A_RANK, BRANCH_WIDTH), RWKV_A_RANK ** -0.5)
    inp['rwkv_g_up'] = _normal(next(ks), (Dp, RWKV_G_RANK, BRANCH_WIDTH), RWKV_G_RANK ** -0.5)
    inp['rwkv_k_k'] = 0.85 + _normal(next(ks), (Dp, BRANCH_WIDTH), 0.05)
    inp['rwkv_k_a'] = gain((Dp, BRANCH_WIDTH))
    inp['rwkv_r_k'] = _normal(next(ks), (Dp, RWKV_HEADS, RWKV_HEAD_DIM), 0.1)
    inp['rwkv_ln_w'] = gain((Dp, BRANCH_WIDTH))
    inp['rwkv_ln_b'] = _normal(next(ks), (Dp, BRANCH_WIDTH), 0.01)
    inp['hgrn_lb'] = _normal(next(ks), (Dp, HGRN_HEADS * HGRN_KEY_DIM), 1.0)
    inp['hgrn_norm'] = gain((Dp, HGRN_VAL_DIM))
    inp['w_branch'] = _normal(next(ks), (Dp, N_BRANCHES, BRANCH_WIDTH, D_MODEL), BRANCH_WIDTH ** -0.5)
    inp['w_o'] = _normal(next(ks), (Dp, D_MODEL, D_MODEL), D_MODEL ** -0.5)
    inp['ffn2_norm'] = gain((Dp, D_MODEL))
    inp['ffn2_w_gate'] = _normal(next(ks), (Dp, D_MODEL, D_FF), D_MODEL ** -0.5)
    inp['ffn2_w_up'] = _normal(next(ks), (Dp, D_MODEL, D_FF), D_MODEL ** -0.5)
    inp['ffn2_w_down'] = _normal(next(ks), (Dp, D_FF, D_MODEL), D_FF ** -0.5)
    inp['ple_norm'] = gain((Dp, D_MODEL))
    inp['ple_w_gate'] = _normal(next(ks), (Dp, D_MODEL, D_MODEL), D_MODEL ** -0.5)
    inp['ple_w_proj'] = _normal(next(ks), (Dp, PLE_DIM, D_MODEL), PLE_DIM ** -0.5)
    inp['final_norm'] = gain((D_MODEL,))
    return inp

def reference(x, p, ffn1_norm, ffn1_w_gate, ffn1_w_up, ffn1_w_down, mix_norm, w_in, attn_sinks,
              rwkv_mu, rwkv_w0, rwkv_w_up, rwkv_a0, rwkv_a_up, rwkv_g_up, rwkv_k_k, rwkv_k_a, rwkv_r_k,
              rwkv_ln_w, rwkv_ln_b, hgrn_lb, hgrn_norm, w_branch, w_o, ffn2_norm, ffn2_w_gate, ffn2_w_up,
              ffn2_w_down, ple_norm, ple_w_gate, ple_w_proj, final_norm):
    lb_all = jax.nn.softmax(hgrn_lb.astype(jnp.float32), axis=0)
    lb_layers = jnp.clip(jnp.cumsum(lb_all, axis=0) - lb_all[0:1], 0.0, 1.0 - 1e-6)
    for i in range(DEPTH):
        h = rmsnorm(x, ffn1_norm[i])
        x = x + FFN_HALF * swiglu(h, ffn1_w_gate[i], ffn1_w_up[i], ffn1_w_down[i])
        u = rmsnorm(x, mix_norm[i])
        x = x + token_mixer(u, w_in[i], attn_sinks[i], rwkv_mu[i], rwkv_w0[i], rwkv_w_up[i], rwkv_a0[i],
                            rwkv_a_up[i], rwkv_g_up[i], rwkv_k_k[i], rwkv_k_a[i], rwkv_r_k[i], rwkv_ln_w[i],
                            rwkv_ln_b[i], lb_layers[i], hgrn_norm[i], w_branch[i], w_o[i]).astype(x.dtype)
        h = rmsnorm(x, ffn2_norm[i])
        x = x + FFN_HALF * swiglu(h, ffn2_w_gate[i], ffn2_w_up[i], ffn2_w_down[i])
        gate = jax.nn.sigmoid(rmsnorm(x, ple_norm[i]) @ ple_w_gate[i])
        x = x + gate * (p[i] @ ple_w_proj[i])
    return rmsnorm(x, final_norm)


_drawn_inputs = setup_inputs


def setup_inputs(seed=0):
    import zlib

    import numpy as np

    out = dict(_drawn_inputs(seed))
    spreads = {}
    factors = {'attn_sinks': 8.0,
     'rwkv_a0': 3.501,
     'rwkv_k_k': 160.681,
     'rwkv_k_a': 2.739,
     'rwkv_ln_w': 3.614,
     'rwkv_ln_b': 8.0,
     'hgrn_lb': 2.836,
     'hgrn_norm': 3.146,
     'ple_norm': 21.561,
     'ffn2_norm': 2.981}
    for name, (base, spread) in spreads.items():
        noise = np.random.default_rng([zlib.crc32(name.encode()), seed]).standard_normal(out[name].shape)
        drawn = base * np.exp(spread * noise) if base else spread * noise
        out[name] = jnp.asarray(drawn.astype(out[name].dtype))
    for name, factor in factors.items():
        out[name] = (out[name] * factor).astype(out[name].dtype)
    return out
```

```python
from contextlib import ExitStack

import numpy as np
import concourse.bass as bass
from concourse import mybir

F32 = mybir.dt.float32
F32R = mybir.dt.float32r
I32 = mybir.dt.int32
ALU = mybir.AluOpType
ACT = mybir.ActivationFunctionType
AX = mybir.AxisListType

P = 128
SEQ = 512
D = 1024
DEPTH = 2
D_FF = 2816
PLE = 256
KD = D // P
TT = SEQ // P
HALF_TILES = (10, 12)
EPS = 1e-6

HD = 64
C = SEQ // HD
PAIRS = 4
Y_RAW = 6
LEVELS = 7
WIDTH = PAIRS * P
DECAY = float(np.exp(-0.5))
GN_EPS = 64e-5
MASKED = -1e30
LN_MIN = 2.0 ** -60

Z_Q, Z_K, Z_V = 0, 4, 5
Z_R, Z_RK, Z_RV, Z_WA, Z_G = 6, 10, 14, 18, 19
Z_HQ, Z_HF, Z_HI, Z_HO = 20, 24, 28, 32
Z_GATE, Z_TILES = 36, 60
Y_A, Y_B, Y_C = 0, 4, 8

W_BUF = KD * P


class Signal:

    def __init__(self, sem, ahead=1):
        self.sem, self.ahead = sem, ahead

    def at(self, n):
        return n + self.ahead


class Turns:

    def __init__(self, sections):
        self.base, self.per, self.total = {}, {}, 0
        for name, laps, uses in sections:
            self.base[name], self.per[name] = self.total, uses
            self.total += laps * uses

    def nth(self, layer, section, lap, k=1):
        return layer * self.total + lap * self.per[section] + (self.base[section] + k)


SECTIONS = [("f1a_up", HALF_TILES[0], 1, (1, 1)), ("f1a_down", 4, 2, (1, 1)), ("f1b_up", HALF_TILES[1], 1, (1, 1)), ("f1b_down", 4, 2, (1, 1)),
            ("in_ab", 10, 1, (1, 1)), ("in_c", 4, 2, (1, 1, 1, 1)), ("in_gates", 4, 3, (2, 2, 1, 1)),
            ("merge", 4, 3, (1, 1, 1, 1, 1, 1)), ("w_o", 4, 1, (1, 1)),
            ("f2a_up", HALF_TILES[0], 1, (1, 1)), ("f2a_down", 4, 2, (1, 1)), ("f2b_up", HALF_TILES[1], 1, (1, 1)), ("f2b_down", 4, 2, (1, 1)),
            ("ple", 4, 2, (1, 1, 1, 1))]
SLOT = Turns([(n, laps, u) for n, laps, u, _ in SECTIONS])
BANK = [Turns([(n, laps, (b[i] if i < len(b) else 0)) for n, laps, _, b in SECTIONS]) for i in range(6)]

STAGE = [Turns([(n, laps, b[i] if i < len(b) else 0) for n, laps, _, b in SECTIONS if n.startswith("in_")])
         for i in range(4)]

ROWS = [("ffn1_norm", 8), ("mix_norm", 8), ("ffn2_norm", 8), ("ple_norm", 8), ("rwkv_mu", 14), ("rwkv_w0", 4),
        ("rwkv_a0", 4), ("rwkv_k_k", 4), ("rwkv_k_a", 4), ("rwkv_r_k", 4), ("rwkv_ln_w", 4), ("rwkv_ln_b", 4),
        ("hgrn_lb", 4), ("hgrn_norm", 1)]
COL = {}
_at = 0
for _name, _n in ROWS:
    COL[_name] = _at
    _at += _n
LAYER_COLS = _at
NEXT_GAIN = LAYER_COLS


_LV = range(1, LEVELS - 1)
RW_PE = (["d", "a", "g", "kk_norm", "bonus", "turn_v", "turn_kq", "turn_bh", "turn_kh",
          "A1T_0", "A1T_1", "A1_0", "A1_1", "A2T_0", "A2T_1", "A2v"]
         + [f"{w}{l}_{h}" for l in _LV for w in "TX" for h in (0, 1)]
         + ["PG_0", "PG_1", "B1T_0", "B1T_1", "B2T_0", "B2T_1", "R2", "state_0", "state_1"]
         + [f"Z{c}" for c in range(2, C)] + ["y_0", "y_1", "mean", "var"])
RW_ACT = ["w", "a", "g", "kk_raw", "kk_sq", "dec", "inc", "kk_root", "kq0", "rk", "v_tok", "kq_tok", "b_tok", "k_tok",
          "A2v_tok", "PG_0", "PG_1", "NZ_0", "NZ_1", "y_0", "y_sq", "y_sd", "y_ln"]
RW_POOL = ["lora_wa", "lora_g", "b", "rk", "bt", "rt", "kt", "ediag", "XTm_0", "XTm_1", "X_0", "X_1", "XT_0", "XT_1",
           "y_b", "y"]
RW_DVE = (["dr", "r", "dk", "k", "dv", "v", "cs", "kmax", "krs", "kk", "ka", "kp", "kq", "bh", "kh", "bonus",
           "NT_0", "NT_1", "X_0", "X_1", "A2T_0", "A2T_1"]
          + [f"{w}{l}_{h}" for l in _LV[:-1] for w in ("T", "XT", "X") for h in (0, 1)]
          + [f"{w}{LEVELS - 2}_{h}" for w in ("T", "XT") for h in (0, 1)]
          + ["B1T_0", "B1T_1", "B2T_0", "B2T_1", "R2", "M00", "M01", "M10", "MT"] + [f"Z{c}" for c in range(1, C)]
          + ["y_1", "yc", "yrs", "yn"])
HG_PE = (["scores_00", "scores_01", "scores_10", "scores_11", "probT_00", "probT_01", "probT_10", "probT_11", "att", "hv"]
         + [f"att{l}" for l in range(LEVELS + 1)] + ["hk", "dS", "o", "o_norm"])
HG_ACT = (["sig_f", "sig_q", "sig_o", "qs", "logf", "exp_0", "esink_0", "exp_1", "esink_1"]
          + ["probT_00", "probT_01", "probT_10", "probT_11", "yatt", "hv_tok"]
          + [f"ex{l}" for l in range(LEVELS - 2)] + ["eb", f"ex{LEVELS - 2}", f"ex{LEVELS - 1}", "ed", "hk_tok", "o", "o_sq", "o_sd"])
HG_POOL = ["kcur", "vcur", "key", "hq", "hog"] + [f"qk{l}" for l in range(LEVELS)] + ["kd"]
HG_DVE = (["fl", "f", "bsum"] + [f"{x}_{j}" for j in (0, 1) for x in ("m0", "m1", "mx", "max")]
          + [f"{x}_{j}" for j in (0, 1) for x in ("den", "rec", "probs")] + ["d0", "d1"]
          + [x for l in range(LEVELS) for x in (f"d{l + 2}" if l + 2 < LEVELS else ("qb", "dend")[l + 2 - LEVELS], f"att{l}")]
          + ["S1", f"att{LEVELS}", "S2", "S3", "orec", "on", "y"])
LY_DVE = ["zero", "mt_zero", "dwa", "wa", "dg", "g", "att_zero"]
LY_ACT = ["tanh", "sigmoid", "k00", "k01", "k10", "k11", "v"]
LY_PE = ["v"]
MASK_STEPS = 53


def step(table, n, name):
    return n * len(table) + (table.index(name) + 1)


def pe_mark(ins, signal, table, name, order):
    order.append(name)
    return ins.then_inc(signal.sem, 1)


def build_trunk(nc, d, out):
    ctx = ExitStack()
    with ctx:
        def sb(name, shape, dt=F32, scope=ctx):
            return scope.enter_context(nc.sbuf_tensor(name, shape, dt))

        def signal(name, ahead=1):
            return Signal(ctx.enter_context(nc.semaphore(name)), ahead)

        def dma_signal(name):
            return ctx.enter_context(nc.semaphore(name))

        x = sb("x", [P, KD, SEQ])
        ghi = sb("ghi", [P, KD, SEQ], F32R)
        glo = sb("glo", [P, KD, SEQ], F32R)
        wraw = sb("wraw", [P, 2, W_BUF])
        whi = sb("whi", [P, 2, W_BUF], F32R)
        wlo = sb("wlo", [P, 2, W_BUF], F32R)
        ident = sb("ident", [P, P])
        ones = sb("ones", [P, P])
        rows = sb("rows", [P, DEPTH, P])
        cols = sb("cols", [P, DEPTH * LAYER_COLS + 8])
        lc = sb("lc", [P, LAYER_COLS + 8])
        xsq = sb("xsq", [P, 2, SEQ])
        ssum = sb("ssum", [P, SEQ])
        eps_col = sb("eps_col", [P, 1])
        zero = sb("zero", [P, 1])
        table_set = sb("table_set", [P, 1])
        rstd = sb("rstd", [P, SEQ])

        low = sb("low", [P, LEVELS - 1, P])
        up0 = sb("up0", [P, P])
        before = sb("before", [P, P])
        upto = sb("upto", [P, P])
        pair_mask = sb("pair_mask", [P, LEVELS + 1, P], I32)
        band = sb("band", [P, 4, P])
        seg64 = sb("seg64", [P, SEQ])
        seg128 = sb("seg128", [P, SEQ])
        head_ones = sb("head_ones", [P, P])
        eye64 = sb("eye64", [P, HD])
        sinks = sb("sinks", [P, DEPTH * 8])
        lb = sb("lb", [P, DEPTH * PAIRS])
        lb_rest = sb("lb_rest", [P, DEPTH * PAIRS])
        gn_eps = sb("gn_eps", [P, 1])

        rw = ExitStack()
        stage = sb("stage", [P, 4, SEQ], F32, rw)
        zr = sb("zr", [P, 3, SEQ + 1], F32, rw)
        lora_wa = sb("lora_wa", [P, WIDTH], F32, rw)
        lora_g = sb("lora_g", [P, WIDTH], F32, rw)
        xwa = sb("xwa", [P, SEQ], F32, rw)
        xgs = sb("xgs", [P, SEQ], F32, rw)
        lwa = sb("lwa", [P, P], F32, rw)
        lg = sb("lg", [P, P], F32, rw)
        shift = sb("shift", [P, SEQ], F32, rw)
        r_ = sb("r", [P, SEQ], F32, rw)
        k_ = sb("k", [P, SEQ], F32, rw)
        v_ = sb("v", [P, SEQ], F32, rw)
        w_ = sb("w", [P, SEQ], F32, rw)
        a_ = sb("a", [P, SEQ], F32, rw)
        g_ = sb("g", [P, SEQ], F32, rw)
        cs = sb("cs", [P, SEQ], F32, rw)
        dec = sb("dec", [P, SEQ], F32, rw)
        inc = sb("inc", [P, SEQ], F32, rw)
        kk = sb("kk", [P, SEQ], F32, rw)
        tmp = sb("tmp", [P, SEQ], F32, rw)
        kp = sb("kp", [P, SEQ], F32, rw)
        bb = sb("bb", [P, SEQ], F32, rw)
        kq = sb("kq", [P, SEQ], F32, rw)
        rk = sb("rk", [P, SEQ], F32, rw)
        bh = sb("bh", [P, SEQ], F32, rw)
        kh = sb("kh", [P, SEQ], F32, rw)
        bonus = sb("bonus", [P, SEQ], F32, rw)
        v_tok = sb("v_tok", [P, TT, P], F32, rw)
        b_tok = sb("b_tok", [P, TT, P], F32, rw)
        k_tok = sb("k_tok", [P, TT, P], F32, rw)
        rhs = sb("rhs", [P, TT, 2, 2, HD], F32, rw)
        NT = sb("NT", [P, 2, TT, P], F32, rw)
        X = sb("X", [P, 2, TT, P], F32, rw)
        XT = sb("XT", [P, 2, TT, P], F32, rw)
        T1 = sb("T1", [P, 2, TT, P], F32, rw)
        PG = sb("PG", [P, 2, TT, P], F32, rw)
        MT = sb("MT", [P, C, P], F32, rw)
        ediag = sb("ediag", [P, C, HD], F32, rw)
        NZ = sb("NZ", [P, C, HD], F32, rw)
        Z = sb("Z", [P, C, HD], F32, rw)
        rw.close()
        zwag = NT[:].rearrange("p a t c -> p (a t c)")
        y_ = w_

        hg = ExitStack()
        stage_ = sb("stage_again", [P, 4, SEQ], F32, hg)
        kvraw = sb("kvraw", [P, 2, SEQ], F32, hg)
        krep = sb("krep", [P, 2, SEQ], F32, hg)
        vtok2 = sb("vtok2", [P, 2, TT, HD], F32, hg)
        kcur = sb("kcur", [P, SEQ], F32, hg)
        vcur = sb("vcur", [P, TT, HD], F32, hg)
        zq = sb("zq", [P, SEQ], F32, hg)
        qs = sb("qs", [P, SEQ], F32, hg)
        sc = sb("sc", [P, 2, TT, 2 * P], F32, hg)
        pT_ = sb("probT", [P, 2, TT, 2, P], F32, hg)
        small = sb("small", [P, 2, 6, TT], F32, hg)
        yatt = sb("yatt", [P, SEQ], F32, hg)
        hz = sb("hz", [P, 4, SEQ], F32, hg)
        fg = sb("fg", [P, SEQ], F32, hg)
        logf = sb("logf", [P, SEQ], F32, hg)
        key = sb("key", [P, SEQ], F32, hg)
        bsum = sb("bsum", [P, SEQ], F32, hg)
        hq = sb("hq", [P, SEQ], F32, hg)
        hog = sb("hog", [P, SEQ], F32, hg)
        dd = sb("dd", [P, 2, SEQ], F32, hg)
        ex = sb("ex", [P, 2, SEQ], F32, hg)
        qk = sb("qk", [P, 2, SEQ], F32, hg)
        attT = sb("attT", [P, TT, P], F32, hg)
        qb = sb("qb", [P, SEQ], F32, hg)
        hv_tok = sb("hv_tok", [P, TT, P], F32, hg)
        hk_tok = sb("hk_tok", [P, TT, P], F32, hg)
        S = sb("S", [P, TT, P], F32, hg)
        ho = sb("ho", [P, SEQ], F32, hg)
        hsq = sb("hsq", [P, SEQ], F32, hg)
        hg.close()

        mg = ExitStack()
        yhi = sb("yhi", [P, 12, SEQ], F32R, mg)
        ylo = sb("ylo", [P, 12, SEQ], F32R, mg)
        mhi = sb("mhi", [P, KD, SEQ], F32R, mg)
        mlo = sb("mlo", [P, KD, SEQ], F32R, mg)
        yraw = sb("yraw", [P, Y_RAW, SEQ], F32, mg)
        gates = sb("gates", [P, 2, 3, SEQ], F32, mg)
        acc = sb("acc", [P, 2, SEQ], F32, mg)
        mg.close()

        ffn = ExitStack()
        fhi = sb("fhi", [P, KD, SEQ], F32R, ffn)
        flo = sb("flo", [P, KD, SEQ], F32R, ffn)
        ple_scope = ExitStack()
        praw = sb("praw", [P, TT, PLE], F32, ple_scope)
        pT = sb("pT", [P, 2, SEQ], F32, ple_scope)
        phi = sb("phi", [P, 2, SEQ], F32R, ple_scope)
        plo = sb("plo", [P, 2, SEQ], F32R, ple_scope)
        pgate = sb("pgate", [P, 2, SEQ], F32, ple_scope)
        pprod = sb("pprod", [P, 2, SEQ], F32, ple_scope)
        ple_scope.close()
        hhi = sb("hhi", [P, max(HALF_TILES), SEQ], F32R, ffn)
        hlo = sb("hlo", [P, max(HALF_TILES), SEQ], F32R, ffn)
        gate_in = sb("gate_in", [P, SEQ], F32, ffn)
        gate_sig = sb("gate_sig", [P, SEQ], F32, ffn)
        gate_act = sb("gate_act", [P, SEQ], F32, ffn)
        up = sb("up", [P, SEQ], F32, ffn)
        h = sb("h", [P, SEQ], F32, ffn)
        ffn.close()
        ends = ExitStack()
        _skip = sb("skip_fhi_flo", [P, 2 * KD, SEQ], F32, ends)
        xin = sb("xin", [P, TT, D], F32, ends)
        fin = sb("fin", [P, KD, SEQ], F32, ends)
        fout = sb("fout", [P, TT, D], F32, ends)
        ends.close()

        zd = nc.dram_tensor("z_scratch", (Z_TILES, P, SEQ), F32, kind="Internal").ap()
        yd = nc.dram_tensor("y_scratch", (12, P, SEQ), F32, kind="Internal").ap()
        primer = nc.dram_tensor("primer_scratch", (7, P, P), F32, kind="Internal").ap()

        bank = [ctx.enter_context(nc.psum_tensor(f"bank{i}", [P, SEQ], F32)) for i in range(8)]

        landed = [dma_signal(f"chunk_landed{s}") for s in (0, 1)]
        w_hi = [signal(f"chunk_hi{s}") for s in (0, 1)]
        w_lo = [signal(f"chunk_lo{s}") for s in (0, 1)]
        used = [signal(f"chunk_used{s}") for s in (0, 1)]
        read = [signal(f"bank_read{i}") for i in range(6)]
        rows_in = dma_signal("rows_in")
        x_in = dma_signal("x_in")
        p_in = dma_signal("p_in")
        stored = dma_signal("stored")
        const = signal("constants", 0)
        turned = signal("transposes_done", 0)
        cols_ready = signal("cols_ready", 0)
        lc_ready = signal("layer_cols_ready", 0)
        x_new = signal("x_tile_loaded", 0)
        g_hi = signal("x_gain_hi")
        g_sq = signal("x_square")
        g_lo = signal("x_gain_lo")
        g_sum = signal("squares_summed", 2)
        n_sum = signal("norm_sum")
        n_rms = signal("norm_rms")
        n_rstd = signal("norm_rstd")
        f_sig = signal("gate_sigmoid")
        f_act = signal("gate_silu")
        f_h = signal("hidden")
        f_hi = signal("hidden_hi")
        f_lo = signal("hidden_lo")
        p_turned = signal("p_turned")
        p_copied = signal("p_copied")
        p_hi = signal("p_hi")
        p_lo = signal("p_lo")
        p_sig = signal("ple_sigmoid")
        p_mul = signal("ple_product")
        p_add = signal("ple_added")
        stage_out = [dma_signal(f"stage{i}_out") for i in range(4)]
        lora_in = dma_signal("lora_in")
        wag_in = dma_signal("wag_in")
        rkv_in = dma_signal("rkv_in")
        kv_in = dma_signal("kv_in")
        hz_in = dma_signal("hz_in")
        zq_in = dma_signal("zq_in")
        ya_out, yb_out, yc_out = dma_signal("ya_out"), dma_signal("yb_out"), dma_signal("yc_out")
        acc_step = signal("branch_sum_step")
        y_in = [dma_signal(f"y_in{i}") for i in range(Y_RAW)]
        gates_in = [dma_signal(f"gates_in{i}") for i in (0, 1)]
        sinks_in = dma_signal("sinks_in")
        lb_step = signal("lb_step", 0)
        lb_ready = signal("lb_ready", 0)
        lb_sig = signal("lb_sigmoid", 0)
        masks = signal("masks", 0)
        w_pe = signal("rwkv_products", len(RW_PE))
        w_act = signal("rwkv_scalar", len(RW_ACT))
        w_pool = signal("rwkv_pool", len(RW_POOL))
        w_dve = signal("rwkv_vector", len(RW_DVE))
        h_pe = signal("hgrn_products", len(HG_PE))
        h_act = signal("hgrn_scalar", len(HG_ACT))
        h_pool = signal("hgrn_pool", len(HG_POOL))
        h_dve = signal("hgrn_vector", len(HG_DVE))
        l_dve = signal("layer_vector", len(LY_DVE))
        l_act = signal("layer_scalar", len(LY_ACT))
        l_pe = signal("layer_products", len(LY_PE))
        m_hi = signal("y_hi")
        m_lo = signal("y_lo", Y_RAW)
        m_sig = signal("gates_sigmoid")
        m_sum = signal("merged")
        m_mhi = signal("merged_hi")
        m_mlo = signal("merged_lo")
        sum_clear = signal("ssum_cleared", 0)
        eps_set = signal("eps_set", 0)
        zero_set = signal("zero_set", 0)
        col_copy = signal("cols_copied", 0)
        lc_copied = signal("layer_cols_copied", 0)
        out_new = signal("out_tile", 0)
        out_copied = signal("out_copied", 0)

        def kview(w, k0, nk):
            return w[k0 * P:(k0 + nk) * P, :].rearrange("(k p) n -> p k n", p=P)

        block = ctx.enter_context(nc.Block())

        @block.sync
        def _(sp):
            for L in range(DEPTH):
                for name, n in ROWS:
                    src = d[name][L] if name != "rwkv_r_k" else d[name][L].rearrange("h k -> (h k)")
                    sp.dma_start(rows[COL[name]:COL[name] + n, L, :],
                                 src.rearrange("(r c) -> r c", c=P)).then_inc(rows_in, 16)
                sp.dma_start(rows[LAYER_COLS:LAYER_COLS + 8, L, :],
                             d["final_norm"].rearrange("(r c) -> r c", c=P)).then_inc(rows_in, 16)
            sp.dma_start(sinks[:], d["attn_sinks"].rearrange("l h -> (l h)").partition_broadcast(P)).then_inc(sinks_in, 16)
            sp.dma_start(xin[:], d["x"][0].rearrange("(t p) c -> p t c", p=P)).then_inc(x_in, 16)

            def load(L, section, lap, k, slot, src, n):
                use = SLOT.nth(L, section, lap, k)
                dst = wraw[:, slot, 0:n].rearrange("p (k c) -> p k c", c=P)
                before = sp.snap(w_lo[slot].at(use - 1))
                sp.wait_ge(w_lo[slot].sem, before)
                sp.dma_start(dst, src).then_inc(landed[slot], 16)

            def ffn_loads(L, f):
                tile0 = 0
                for half, tiles in zip("ab", HALF_TILES):
                    with sp.Fori(0, tiles) as j:
                        cols_j = bass.ds(sp.snap(j * P + tile0 * P), P)
                        load(L, f"f{f}{half}_up", j, 1, 0, kview(d[f"ffn{f}_w_gate"][L], 0, KD)[:, :, cols_j], W_BUF)
                        load(L, f"f{f}{half}_up", j, 1, 1, kview(d[f"ffn{f}_w_up"][L], 0, KD)[:, :, cols_j], W_BUF)
                    nk = tiles // 2
                    with sp.Fori(0, KD // 2) as lap:
                        for i in range(2):
                            cols_m = bass.ds(sp.snap(lap * (2 * P) + i * P), P)
                            for s in (0, 1):
                                load(L, f"f{f}{half}_down", lap, i + 1, s,
                                     kview(d[f"ffn{f}_w_down"][L], tile0 + s * nk, nk)[:, :, cols_m], nk * P)
                    tile0 += tiles

            def mixer_loads(L):
                win = kview(d["w_in"][L], 0, KD)

                def in_tile(section, lap, q, tile):
                    load(L, section, lap, q // 2 + 1, q % 2, win[:, :, bass.ds(sp.snap(tile * P), P)], W_BUF)

                with sp.Fori(0, 10) as lap:
                    for q in range(2):
                        in_tile("in_ab", lap, q, lap * 2 + q)
                sp.wait_ge(used[1].sem, used[1].at(SLOT.nth(L, "f1b_down", 3, 2)))
                sp.dma_start(lora_wa[0:64, :], d["rwkv_w_up"][L]).then_inc(lora_in, 16)
                sp.dma_start(lora_wa[64:P, :], d["rwkv_a_up"][L]).then_inc(lora_in, 16)
                sp.dma_start(lora_g[:], d["rwkv_g_up"][L]).then_inc(lora_in, 16)
                with sp.Fori(0, PAIRS) as lap:
                    for q in range(4):
                        in_tile("in_c", lap, q, lap * 4 + (Z_HQ + q))
                with sp.Fori(0, PAIRS) as lap:
                    for q in range(6):
                        in_tile("in_gates", lap, q, lap * 6 + (Z_GATE + q))
                with sp.Fori(0, KD // 2) as lap:
                    for q in range(6):
                        cols_m = bass.ds(sp.snap(lap * (2 * P) + (q // 3) * P), P)
                        load(L, "merge", lap, q // 2 + 1, q % 2, kview(d["w_branch"][L, q % 3], 0, PAIRS)[:, :, cols_m], PAIRS * P)
                with sp.Fori(0, KD // 2) as lap:
                    for q in range(2):
                        cols_m = bass.ds(sp.snap(lap * (2 * P) + q * P), P)
                        load(L, "w_o", lap, 1, q, kview(d["w_o"][L], 0, KD)[:, :, cols_m], W_BUF)

            with sp.Fori(0, DEPTH) as L:
                ffn_loads(L, 1)
                mixer_loads(L)
                ffn_loads(L, 2)
                sp.wait_ge(used[1].sem, used[1].at(SLOT.nth(L, "f2b_down", 3, 2)))
                sp.dma_start(praw[:], d["p"][L, 0].rearrange("(t p) c -> p t c", p=P)).then_inc(p_in, 16)
                with sp.Fori(0, KD // 2) as lap:
                    for i in range(2):
                        cols_m = bass.ds(sp.snap(lap * (2 * P) + i * P), P)
                        load(L, "ple", lap, i + 1, 0, kview(d["ple_w_gate"][L], 0, KD)[:, :, cols_m], W_BUF)
                        load(L, "ple", lap, i + 1, 1, kview(d["ple_w_proj"][L], 0, 2)[:, :, cols_m], 2 * P)

            for t in range(TT):
                sp.wait_ge(out_copied.sem, 2 * t + 2)
                sp.dma_start(out[0, t * P:(t + 1) * P, :], fout[:, t, :]).then_inc(stored, 16)
            sp.wait_ge(stored, 16 * TT)

        @block.tensor
        def _(pe):
            for s in (*used, n_sum, p_turned, w_pe, h_pe, l_pe):
                pe.sem_inc(s.sem, s.ahead)
            pe.wait_ge(const.sem, 3)
            pe.wait_ge(rows_in, 16 * DEPTH * (len(ROWS) + 1))
            for L in range(DEPTH):
                pe.transpose(bank[6][:, L * P:L * P + LAYER_COLS + 8], rows[0:LAYER_COLS + 8, L, :],
                             ident[0:LAYER_COLS + 8, 0:LAYER_COLS + 8]).then_inc(turned.sem, 1)
            pe.wait_ge(x_in, 16)
            for m in range(KD):
                if m >= 2:
                    pe.wait_ge(x_new.sem, m - 1)
                for t in range(TT):
                    mm = pe.transpose(bank[m % 2][:, t * P:(t + 1) * P], xin[:, t, m * P:(m + 1) * P], ident[:])
                mm.then_inc(turned.sem, 1)

            def norm(e):
                pe.wait_ge(g_sum.sem, g_sum.at(8 * e + 8))
                pe.wait_ge(n_rms.sem, n_rms.at(e))
                pe.matmul(bank[7][:], ones[:], ssum[:], start=True, stop=True).then_inc(n_sum.sem, 1)

            def chunk(L, section, lap, k, slot, nk, hi, lo, k0, b, first, last, between=None):
                use = SLOT.nth(L, section, lap, k)
                pe.wait_ge(w_lo[slot].sem, w_lo[slot].at(use))
                for i in range(nk):
                    wh = whi[:, slot, i * P:(i + 1) * P]
                    wl = wlo[:, slot, i * P:(i + 1) * P]
                    pe.matmul(bank[b][:], wh, hi[:, k0 + i, :], start=first and i == 0, stop=False)
                    pe.matmul(bank[b][:], wh, lo[:, k0 + i, :], start=False, stop=False)
                    mm = pe.matmul(bank[b][:], wl, hi[:, k0 + i, :], start=False, stop=last and i == nk - 1)
                    if between is not None and i < nk - 1:
                        between(i)
                mm.then_inc(used[slot].sem, 1)

            def bank_free(L, section, lap, b, k=1):
                pe.wait_ge(read[b].sem, read[b].at(BANK[b].nth(L, section, lap, k) - 1))

            def ffn(L, f, event, hi, lo):
                done = L * (2 * sum(HALF_TILES)) + (f - 1) * sum(HALF_TILES)
                for half, tiles in zip("ab", HALF_TILES):
                    if half == "a":
                        pe.wait_ge(g_lo.sem, g_lo.at(8 * event + 8))
                        norm(event)
                    with pe.Fori(0, tiles) as j:
                        for s in (0, 1):
                            bank_free(L, f"f{f}{half}_up", j, s)
                            chunk(L, f"f{f}{half}_up", j, 1, s, KD, hi, lo, 0, s, True, True)
                    nk = tiles // 2
                    with pe.Fori(0, KD // 2) as lap:
                        for i in range(2):
                            bank_free(L, f"f{f}{half}_down", lap, i)
                            for s in (0, 1):
                                pe.wait_ge(f_lo.sem, f_lo.at(done + (s + 1) * nk))
                                chunk(L, f"f{f}{half}_down", lap, i + 1, s, nk, hhi, hlo, s * nk, i, s == 0, s == 1)
                    done = done + tiles

            def in_tile(L, section, lap, q, b, k=1, between=None):
                bank_free(L, section, lap, b, k)
                chunk(L, section, lap, q // 2 + 1, q % 2, KD, ghi, glo, 0, b, True, True, between)

            def rwkv_lap(L, lap):
                n = pe.snap(L * PAIRS + lap)
                done = lambda ins, name: pe_mark(ins, w_pe, RW_PE, name, order)
                order = []
                G = lambda q, between=None: in_tile(L, "in_c", lap, q, q, 1, between)
                W = lambda sig, table, name: pe.wait_ge(sig.sem, sig.at(step(table, n, name)))

                pe.wait_ge(l_act.sem, l_act.at(step(LY_ACT, L, "sigmoid")))
                W(w_pool, RW_POOL, "lora_g")
                pe.wait_ge(w_act.sem, w_act.at(step(RW_ACT, n - 1, "y_sd")))
                pe.wait_ge(w_dve.sem, w_dve.at(step(RW_DVE, n - 1, "yc")))
                for b, w, x_, name in ((4, lwa[0:64, :], xwa[0:64, :], "d"), (5, lwa[64:P, :], xwa[64:P, :], "a"),
                                       (6, lg[:], xgs[:], "g")):
                    done(pe.matmul(bank[b][:], w, x_, start=True, stop=True), name)
                G(0)
                W(w_act, RW_ACT, "kk_sq")
                done(pe.matmul(bank[4][:], head_ones[:], tmp[:], start=True, stop=True), "kk_norm")
                G(1)
                W(w_act, RW_ACT, "rk")
                done(pe.matmul(bank[5][:], head_ones[:], rk[:], start=True, stop=True), "bonus")
                for src, b, sig, table, name in ((v_, 6, w_dve, RW_DVE, "v"), (kq, 7, w_dve, RW_DVE, "kq"),
                                                 (bh, 4, w_dve, RW_DVE, "bh"), (kh, 5, w_dve, RW_DVE, "kh")):
                    W(sig, table, name)
                    if name == "kq":
                        W(w_act, RW_ACT, "kq0")
                    if name == "kh":
                        W(w_dve, RW_DVE, "bonus")
                    for t in range(TT):
                        mm = pe.transpose(bank[b][:, t * P:(t + 1) * P], src[:, t * P:(t + 1) * P], ident[:])
                    done(mm, "turn_" + name)

                def gram(l_, r__, b, h):
                    for t in range(TT):
                        mm = pe.matmul(bank[b][:, t * P:(t + 1) * P], l_[h * 64:h * 64 + 64, t * P:(t + 1) * P],
                                       r__[h * 64:h * 64 + 64, t * P:(t + 1) * P], start=True, stop=True)
                    return mm

                W(w_pool, RW_POOL, "bt")
                W(w_act, RW_ACT, "v_tok")
                done(gram(bb, kq, 6, 0), "A1T_0")
                W(w_act, RW_ACT, "kq_tok")
                done(gram(bb, kq, 7, 1), "A1T_1")
                W(w_act, RW_ACT, "b_tok")
                done(gram(kq, bb, 4, 0), "A1_0")
                W(w_act, RW_ACT, "k_tok")
                done(gram(kq, bb, 5, 1), "A1_1")
                W(w_pool, RW_POOL, "kt")
                W(w_dve, RW_DVE, "NT_0")
                done(gram(kp, kq, 6, 0), "A2T_0")
                W(w_dve, RW_DVE, "NT_1")
                done(gram(kp, kq, 7, 1), "A2T_1")
                W(w_dve, RW_DVE, "A2T_1")
                W(w_dve, RW_DVE, "X_1")
                for h in range(2):
                    for t in range(TT):
                        c0 = (h * TT + t) * HD
                        mm = pe.matmul(bank[4][:, c0:c0 + HD], T1[:, h, t, :], v_tok[:, t, h * HD:(h + 1) * HD],
                                       start=True, stop=True)
                done(mm, "A2v")
                G(2)
                for l in range(1, LEVELS - 1):
                    for h in range(2):
                        if l == 1:
                            W(w_act, RW_ACT, "A2v_tok")
                            W(w_pool, RW_POOL, "XT_1")
                        if l > 1:
                            W(w_dve, RW_DVE, f"X{l - 1}_{h}")
                        for t in range(TT):
                            mm = pe.matmul(bank[4 + h][:, t * P:(t + 1) * P], NT[:, h, t, :], X[:, h, t, :], start=True, stop=True)
                        done(mm, f"T{l}_{h}")
                    for h in range(2):
                        W(w_dve, RW_DVE, f"T{l}_{h}")
                        for t in range(TT):
                            mm = pe.matmul(bank[6 + h][:, t * P:(t + 1) * P], T1[:, h, t, :], XT[:, h, t, :], start=True, stop=True)
                        if l < LEVELS - 2:
                            for t in range(TT):
                                mm = pe.matmul(bank[4 + h][:, t * P:(t + 1) * P], XT[:, h, t, :], T1[:, h, t, :], start=True, stop=True)
                        done(mm, f"X{l}_{h}")
                for h in range(2):
                    W(w_dve, RW_DVE, f"XT{LEVELS - 2}_{h}")
                    for t in range(TT):
                        mm = pe.matmul(bank[4 + h][:, t * P:(t + 1) * P], XT[:, h, t, :],
                                       rhs[:, t, h, :, :].rearrange("p a c -> p (a c)"), start=True, stop=True)
                    done(mm, f"PG_{h}")
                W(w_pool, RW_POOL, "rt")
                for h in range(2):
                    done(gram(bb, r_, 6 + h, h), f"B1T_{h}")
                for h in range(2):
                    W(w_act, RW_ACT, f"PG_{h}")
                    done(gram(kp, r_, 4 + h, h), f"B2T_{h}")
                W(w_dve, RW_DVE, "B1T_1")
                W(w_dve, RW_DVE, "B2T_0")
                for h in range(2):
                    for t in range(TT):
                        mm = pe.matmul(bank[6][h * HD:(h + 1) * HD, t * P:(t + 1) * P], PG[:, h, t, 0:HD], NT[:, h, t, :],
                                       start=True, stop=True)
                done(mm, "R2")
                for par in range(2):
                    b = bank[7] if par == 0 else bank[4]
                    tok = slice(par * 64, par * 64 + 64)
                    for h in range(2):
                        hc = slice(h * HD, (h + 1) * HD)
                        for t in range(TT):
                            pe.matmul(b[hc, t * HD:(t + 1) * HD], PG[tok, h, t, 0:HD], b_tok[tok, t, hc], start=True, stop=True)
                            o = b[hc, (TT + t) * HD:(TT + t + 1) * HD]
                            pe.matmul(o, k_tok[tok, t, hc], v_tok[tok, t, hc], start=True, stop=False)
                            mm = pe.matmul(o, b_tok[tok, t, hc], PG[tok, h, t, HD:P], start=False, stop=True)
                    done(mm, f"state_{par}")

                W(w_dve, RW_DVE, "B2T_1")
                W(w_dve, RW_DVE, "MT")

                def state_step(i):
                    c = i + 1
                    if c <= C - 2:
                        W(w_dve, RW_DVE, f"Z{c}")
                        done(pe.matmul(bank[5][:, c * HD:(c + 1) * HD], MT[:, c, :], Z[:, c, :], start=True, stop=True), f"Z{c + 1}")
                G(3, state_step)
                W(w_dve, RW_DVE, f"Z{C - 1}")
                W(w_dve, RW_DVE, "R2")
                for h, b in ((0, bank[6]), (1, bank[4])):
                    hc = slice(h * HD, (h + 1) * HD)
                    for t in range(TT):
                        o = b[hc, t * P:(t + 1) * P]
                        pe.matmul(o, v_tok[:, t, hc], X[:, h, t, :], start=True, stop=False)
                        for c in (2 * t, 2 * t + 1):
                            if c:
                                pe.matmul(b[hc, c * HD:(c + 1) * HD], Z[hc, c, :], r_[hc, c * HD:(c + 1) * HD],
                                          start=False, stop=False)
                        mm = pe.matmul(o, PG[:, h, t, HD:P], NT[:, h, t, :], start=False, stop=True)
                    done(mm, f"y_{h}")
                W(w_dve, RW_DVE, "y_1")
                W(w_act, RW_ACT, "y_0")
                done(pe.matmul(bank[5][:], head_ones[:], y_[:], start=True, stop=True), "mean")
                W(w_act, RW_ACT, "y_sq")
                done(pe.matmul(bank[6][:], head_ones[:], tmp[:], start=True, stop=True), "var")
                assert order == RW_PE, order

            def hgrn_lap(L, lap):
                n = pe.snap(L * PAIRS + lap)
                order = []
                done = lambda ins, name: pe_mark(ins, h_pe, HG_PE, name, order)
                W = lambda sig, table, name: pe.wait_ge(sig.sem, sig.at(step(table, n, name)))
                G = lambda q: in_tile(L, "in_gates", lap, q, q % 4, q // 4 + 1)

                pe.wait_ge(h_act.sem, h_act.at(step(HG_ACT, n - 1, "o_sd")))
                G(0)
                W(h_act, HG_ACT, "qs")
                W(h_pool, HG_POOL, "vcur")
                for j in range(2):
                    jr = slice(j * 64, j * 64 + 64)
                    for t in range(TT):
                        o = bank[4 + 2 * j + t // 2]
                        for half in range(2):
                            kb = max(t - 1 + half, 0)
                            c0 = (t % 2) * 2 * P + half * P
                            mm = pe.matmul(o[:, c0:c0 + P], qs[jr, t * P:(t + 1) * P], kcur[jr, kb * P:(kb + 1) * P],
                                           start=True, stop=True)
                        if t % 2:
                            done(mm, f"scores_{j}{t // 2}")
                G(1)
                for j in range(2):
                    W(h_dve, HG_DVE, f"probs_{j}")
                    for t in range(TT):
                        for half in range(2):
                            mm = pe.transpose(bank[4 + 2 * j + t // 2][:, (t % 2) * 2 * P + half * P:(t % 2) * 2 * P + half * P + P],
                                              sc[:, j, t, half * P:(half + 1) * P], ident[:])
                        if t % 2:
                            done(mm, f"probT_{j}{t // 2}")
                G(2)
                for j in range(2):
                    W(h_act, HG_ACT, f"probT_{j}1")
                    for t in range(TT):
                        o = bank[4][j * 64:j * 64 + 64, t * P:(t + 1) * P]
                        if t:
                            pe.matmul(o, vcur[:, t - 1, :], pT_[:, j, t, 0, :], start=True, stop=False)
                        mm = pe.matmul(o, vcur[:, t, :], pT_[:, j, t, 1, :], start=t == 0, stop=True)
                done(mm, "att")
                for t in range(TT):
                    mm = pe.transpose(bank[5][:, t * P:(t + 1) * P], hz[:, 2, t * P:(t + 1) * P], ident[:])
                done(mm, "hv")
                for l in range(LEVELS + 1):
                    W(h_pool, HG_POOL, f"qk{min(l, LEVELS - 1)}")
                    if l >= 2:
                        W(h_dve, HG_DVE, f"att{l - 2}")
                    b = bank[6 + l % 2]
                    for t in range(TT):
                        c = slice(t * P, (t + 1) * P)
                        if l < LEVELS:
                            mm = pe.matmul(b[:, c], qk[:, l % 2, c], qk[:, l % 2, c], start=True, stop=True)
                        else:
                            mm = pe.matmul(b[:, c], key[:, c], hq[:, c], start=True, stop=True)
                    done(mm, f"att{l}")
                    if l in (2, 5):
                        G(l // 3 + 3)
                W(h_pool, HG_POOL, "kd")
                W(h_act, HG_ACT, "yatt")
                for t in range(TT):
                    mm = pe.transpose(bank[4][:, t * P:(t + 1) * P], dd[:, 1, t * P:(t + 1) * P], ident[:])
                done(mm, "hk")
                W(h_act, HG_ACT, "hk_tok")
                for t in range(TT - 1):
                    mm = pe.matmul(bank[5][:, t * P:(t + 1) * P], hk_tok[:, t, :], hv_tok[:, t, :], start=True, stop=True)
                done(mm, "dS")
                G(5)
                W(h_dve, HG_DVE, "S3")
                for t in range(TT):
                    c = slice(t * P, (t + 1) * P)
                    mm = pe.matmul(bank[6][:, c], hv_tok[:, t, :], attT[:, t, :], start=True, stop=t == 0)
                    if t:
                        mm = pe.matmul(bank[6][:, c], S[:, t, :], qb[:, c], start=False, stop=True)
                done(mm, "o")
                W(h_act, HG_ACT, "o_sq")
                done(pe.matmul(bank[7][:], ones[:], hsq[:], start=True, stop=True), "o_norm")
                assert order == HG_PE, order

            def mixer(L):
                pe.wait_ge(g_lo.sem, g_lo.at(8 * (4 * L + 1) + 8))
                norm(4 * L + 1)
                with pe.Fori(0, 10) as lap:
                    for q in range(2):
                        in_tile(L, "in_ab", lap, q, q)
                with pe.Fori(0, PAIRS) as lap:
                    rwkv_lap(L, lap)
                pe.wait_ge(kv_in, 32 * L + 32)
                pe.wait_ge(w_dve.sem, w_dve.at(step(RW_DVE, 4 * L + 3, "y_1")))
                for t in range(TT):
                    mm = pe.transpose(bank[4][:, t * P:(t + 1) * P], kvraw[:, 1, t * P:(t + 1) * P], ident[:])
                mm.then_inc(l_pe.sem, 1)
                with pe.Fori(0, PAIRS) as lap:
                    hgrn_lap(L, lap)
                with pe.Fori(0, KD // 2) as lap:
                    for q in range(6):
                        pe.wait_ge(m_lo.sem, m_lo.at(12 * L + PAIRS * (q % 3 + 1)))
                        bank_free(L, "merge", lap, q)
                        chunk(L, "merge", lap, q // 2 + 1, q % 2, PAIRS, yhi, ylo, (q % 3) * PAIRS, q, True, True)
                with pe.Fori(0, KD // 2) as lap:
                    pe.wait_ge(m_mlo.sem, m_mlo.at(8 * L + 8))
                    for q in range(2):
                        bank_free(L, "w_o", lap, q)
                        chunk(L, "w_o", lap, 1, q, KD, mhi, mlo, 0, q, True, True)

            with pe.Fori(0, DEPTH) as L:
                ffn(L, 1, 4 * L, fhi, flo)
                mixer(L)
                ffn(L, 2, 4 * L + 2, ghi, glo)
                pe.wait_ge(p_in, 16 * L + 16)
                for m in range(2):
                    for t in range(TT):
                        mm = pe.transpose(bank[4 + m][:, t * P:(t + 1) * P], praw[:, t, m * P:(m + 1) * P], ident[:])
                    mm.then_inc(p_turned.sem, 1)
                pe.wait_ge(g_lo.sem, g_lo.at(8 * (4 * L + 3) + 8))
                pe.wait_ge(p_lo.sem, p_lo.at(2 * L + 2))
                norm(4 * L + 3)
                with pe.Fori(0, KD // 2) as lap:
                    for i in range(2):
                        bank_free(L, "ple", lap, 2 * i)
                        chunk(L, "ple", lap, i + 1, 0, KD, ghi, glo, 0, 2 * i, True, True)
                        bank_free(L, "ple", lap, 2 * i + 1)
                        chunk(L, "ple", lap, i + 1, 1, 2, phi, plo, 0, 2 * i + 1, True, True)
            norm(4 * DEPTH)
            for t in range(TT):
                for g in range(2):
                    n = 2 * t + g
                    for j in range(4):
                        m = 4 * g + j
                        if t == 0:
                            pe.wait_ge(out_new.sem, m + 1)
                        if n >= 6 and j == 0:
                            pe.wait_ge(out_copied.sem, n - 5)
                        mm = pe.transpose(bank[n % 6][:, j * P:(j + 1) * P], fin[:, m, t * P:(t + 1) * P], ident[:])
                    mm.then_inc(turned.sem, 1)

        @block.scalar
        def _(act):
            for s in (*w_hi, g_hi, g_sq, n_rms, f_sig, f_hi, p_hi, p_sig, w_act, h_act, l_act, m_hi, m_sig, m_mhi):
                act.sem_inc(s.sem, s.ahead)
            act.wait_ge(const.sem, 3)
            for i, sem in enumerate((*stage_out, ya_out, yb_out, yc_out)):
                act.dma_start(primer[i], ident[:]).then_inc(sem, 16)

            def convert(L, section, lap, k, slot, n=W_BUF):
                use = SLOT.nth(L, section, lap, k)
                act.wait_ge(landed[slot], 16 * use)
                act.wait_ge(used[slot].sem, used[slot].at(use - 1))
                act.activation(whi[:, slot, 0:n], wraw[:, slot, 0:n], ACT.Copy).then_inc(w_hi[slot].sem, 1)

            def prep(e, m, i, gain, hi):
                n = 8 * e + m + 1
                act.wait_ge(g_sum.sem, g_sum.at(n - 2))
                act.activation(hi[:, m, :], x[:, m, :], ACT.Copy, scale=gain).then_inc(g_hi.sem, 1)
                act.activation(xsq[:, i, :], x[:, m, :], ACT.Square).then_inc(g_sq.sem, 1)

            def norm(e):
                act.wait_ge(n_sum.sem, n_sum.at(e + 1))
                act.wait_ge(n_rstd.sem, n_rstd.at(e))
                act.activation(rstd[:], bank[7][:], ACT.Sqrt, scale=1.0 / D, bias=eps_col[:, 0:1]).then_inc(n_rms.sem, 1)
                act.activation(table_set[:], eps_col[:, 0:1], ACT.Sigmoid)

            act.wait_ge(eps_set.sem, 1)
            act.wait_ge(lb_step.sem, 2)
            act.activation(lb[:, PAIRS:2 * PAIRS], lb_rest[:, 0:PAIRS], ACT.Sigmoid).then_inc(lb_sig.sem, 1)
            act.wait_ge(cols_ready.sem, 1)
            act.wait_ge(masks.sem, MASK_STEPS)
            for m in range(KD):
                act.wait_ge(x_new.sem, m + 1)
                prep(0, m, m % 2, cols[:, m:m + 1], fhi)

            def ffn(L, f, event, next_gain):
                done = L * (2 * sum(HALF_TILES)) + (f - 1) * sum(HALF_TILES)
                for half, tiles in zip("ab", HALF_TILES):
                    if half == "a":
                        norm(event)
                    up_, down_ = f"f{f}{half}_up", f"f{f}{half}_down"
                    with act.Fori(0, tiles) as j:
                        n = done + j + 1
                        convert(L, up_, j, 1, 1)
                        convert(L, up_, j, 2, 0)
                        act.wait_ge(read[0].sem, read[0].at(BANK[0].nth(L, up_, j)))
                        act.wait_ge(f_act.sem, f_act.at(n - 1))
                        act.activation(gate_sig[:], gate_in[:], ACT.Sigmoid).then_inc(f_sig.sem, 1)
                        act.wait_ge(f_h.sem, f_h.at(n))
                        act.activation(hhi[:, j, :], h[:], ACT.Copy).then_inc(f_hi.sem, 1)
                    nk = tiles // 2
                    with act.Fori(0, KD // 2) as lap:
                        for i in range(2):
                            convert(L, down_, lap, i + 1, 1, nk * P)
                            convert(L, down_, lap, i + 2, 0)
                            if half == "b":
                                act.wait_ge(read[i].sem, read[i].at(BANK[i].nth(L, down_, lap)))
                                m = act.snap(lap * 2 + i)
                                prep(event + 1, m, i, lc[:, bass.ds(act.snap(m + next_gain), 1)], ghi)
                    done = done + tiles

            def send(L, section, lap, b, tile, k=1):
                act.wait_ge(read[b].sem, read[b].at(BANK[b].nth(L, section, lap, k)))
                act.dma_start(zd[bass.ds(act.snap(tile), 1), :, :].rearrange("a p c -> p (a c)"), stage[:, b, :])\
                   .then_inc(stage_out[b], 16)

            def fetch(dst, tile, sem):
                act.dma_start(dst, zd[bass.ds(act.snap(tile), 1), :, :].rearrange("a p c -> p (a c)")).then_inc(sem, 16)

            def ahead(L, section, lap, q, n=W_BUF):
                convert(L, section, lap, (q + 1) // 2 + 1, (q + 1) % 2, n)

            def rwkv_lap(L, lap):
                n = act.snap(L * PAIRS + lap)
                order = []
                done = lambda ins, name: pe_mark(ins, w_act, RW_ACT, name, order)
                W = lambda sig, table, name, back=0: act.wait_ge(sig.sem, sig.at(step(table, n - back, name)))
                col = lambda name: lc[:, bass.ds(act.snap(lap + COL[name]), 1)]
                act.wait_ge(l_dve.sem, l_dve.at(step(LY_DVE, L, "g")))
                W(w_dve, RW_DVE, "v", 1)
                for i, z0 in enumerate((Z_R, Z_RK, Z_RV)):
                    fetch(zr[:, i, 1:SEQ + 1], lap + z0, rkv_in)
                act.wait_ge(yb_out, 16 * n + 16)
                W(w_pe, RW_PE, "d")
                done(act.activation(w_[:], bank[4][:], ACT.Sigmoid, bias=col("rwkv_w0")), "w")
                W(w_pe, RW_PE, "a")
                done(act.activation(a_[:], bank[5][:], ACT.Sigmoid, bias=col("rwkv_a0")), "a")
                W(w_pe, RW_PE, "g")
                W(w_pool, RW_POOL, "y", 1)
                done(act.activation(g_[:], bank[6][:], ACT.Copy), "g")
                W(w_dve, RW_DVE, "yn", 1)
                W(w_dve, RW_DVE, "k")
                done(act.activation(kk[:], k_[:], ACT.Copy, scale=col("rwkv_k_k")), "kk_raw")
                done(act.activation(tmp[:], k_[:], ACT.Square, scale=col("rwkv_k_k")), "kk_sq")
                ahead(L, "in_c", lap, 0)
                W(w_dve, RW_DVE, "cs")
                done(act.activation(dec[:], cs[:], ACT.Exp, scale=-DECAY), "dec")
                done(act.activation(inc[:], cs[:], ACT.Exp, scale=DECAY), "inc")
                W(w_dve, RW_DVE, "kmax")
                done(act.activation(tmp[:], tmp[:], ACT.Sqrt), "kk_root")
                ahead(L, "in_c", lap, 1)
                W(w_dve, RW_DVE, "kk")
                first = lambda t: t[:].rearrange("p (c s) -> p c s", s=HD)[:, :, 0]
                done(act.activation(first(kq), first(kk), ACT.Copy), "kq0")
                W(w_pool, RW_POOL, "rk")
                done(act.activation(rk[:], rk[:], ACT.Copy, scale=col("rwkv_r_k")), "rk")
                W(w_pe, RW_PE, "turn_v")
                done(act.activation(v_tok[:], bank[6][:].rearrange("p (t c) -> p t c", t=TT), ACT.Copy), "v_tok")
                W(w_pe, RW_PE, "turn_kq")
                done(act.activation(rhs[:, :, :, 0, :], bank[7][:].rearrange("p (t h c) -> p t h c", t=TT, h=2),
                                    ACT.Copy, scale=-1.0), "kq_tok")
                W(w_pe, RW_PE, "turn_bh")
                done(act.activation(b_tok[:], bank[4][:].rearrange("p (t c) -> p t c", t=TT), ACT.Copy), "b_tok")
                W(w_pe, RW_PE, "turn_kh")
                done(act.activation(k_tok[:], bank[5][:].rearrange("p (t c) -> p t c", t=TT), ACT.Copy), "k_tok")
                W(w_pe, RW_PE, "A2v")
                done(act.activation(rhs[:, :, :, 1, :], bank[4][:].rearrange("p (h t c) -> p t h c", t=TT, h=2),
                                    ACT.Copy), "A2v_tok")
                ahead(L, "in_c", lap, 2)
                send(L, "in_c", lap, 0, lap * 4 + Z_HQ)
                send(L, "in_c", lap, 1, lap * 4 + (Z_HQ + 1))
                ahead(L, "in_c", lap, 3)
                for h in range(2):
                    W(w_pe, RW_PE, f"PG_{h}")
                    done(act.activation(PG[:, h, :, :], bank[4 + h][:].rearrange("p (t c) -> p t c", t=TT), ACT.Copy), f"PG_{h}")
                send(L, "in_c", lap, 2, lap * 4 + (Z_HQ + 2))
                for par, b in ((0, bank[7]), (1, bank[4])):
                    W(w_pe, RW_PE, f"state_{par}")
                    done(act.activation(NZ[:].rearrange("p (t a) c -> p a t c", a=2)[:, par, :, :],
                                        b[:, TT * HD:2 * TT * HD].rearrange("p (t c) -> p t c", t=TT), ACT.Copy), f"NZ_{par}")
                send(L, "in_c", lap, 3, lap * 4 + (Z_HQ + 3))
                W(w_pe, RW_PE, "y_0")
                done(act.activation(y_[0:HD, :], bank[6][0:HD, :], ACT.Copy), "y_0")
                W(w_dve, RW_DVE, "yc")
                done(act.activation(tmp[:], y_[:], ACT.Square), "y_sq")
                W(w_pe, RW_PE, "var")
                done(act.activation(tmp[:], bank[6][:], ACT.Sqrt, scale=1.0 / HD, bias=gn_eps[:, 0:1]), "y_sd")
                W(w_dve, RW_DVE, "yn")
                done(act.activation(y_[:], y_[:], ACT.Identity, scale=col("rwkv_ln_w"), bias=col("rwkv_ln_b")), "y_ln")
                W(w_pool, RW_POOL, "y")
                act.dma_start(yd[bass.ds(act.snap(lap + Y_B), 1), :, :].rearrange("a p c -> p (a c)"), y_[:]).then_inc(yb_out, 16)
                assert order == RW_ACT, order

            def hgrn_lap(L, lap):
                n = act.snap(L * PAIRS + lap)
                order = []
                done = lambda ins, name: pe_mark(ins, h_act, HG_ACT, name, order)
                W = lambda sig, table, name, back=0: act.wait_ge(sig.sem, sig.at(step(table, n - back, name)))
                tokens = lambda ap: ap.rearrange("p (t c) -> p t c", t=TT)
                W(h_pe, HG_PE, "hv", 1)
                W(h_pool, HG_POOL, "hog", 1)
                for i, z0 in enumerate((Z_HQ, Z_HF, Z_HI, Z_HO)):
                    fetch(hz[:, i, :], lap + z0, hz_in)
                fetch(zq[:], lap + Z_Q, zq_in)
                act.wait_ge(hz_in, 64 * n + 64)
                done(act.activation(fg[:], hz[:, 1, :], ACT.Sigmoid), "sig_f")
                W(h_pe, HG_PE, f"att{LEVELS}", 1)
                W(h_pool, HG_POOL, "kd", 1)
                done(act.activation(hq[:], hz[:, 0, :], ACT.Sigmoid), "sig_q")
                W(h_dve, HG_DVE, "y", 1)
                done(act.activation(hog[:], hz[:, 3, :], ACT.Sigmoid), "sig_o")
                act.wait_ge(zq_in, 16 * n + 16)
                done(act.activation(qs[:], zq[:], ACT.Copy, scale=HD ** -0.5), "qs")
                ahead(L, "in_gates", lap, 0)
                W(h_dve, HG_DVE, "f")
                done(act.activation(logf[:], fg[:], ACT.Ln), "logf")
                act.wait_ge(sinks_in, 16)
                for j in range(2):
                    sink = sinks[:, bass.ds(act.snap(n * 2 + j), 1)]
                    W(h_dve, HG_DVE, f"max_{j}")
                    for t in range(TT):
                        ins = act.activation(sc[:, j, t, :], sc[:, j, t, :], ACT.Exp, bias=small[:, j, 1, t:t + 1],
                                             accum_out=small[:, j, 2, t:t + 1])
                    done(ins, f"exp_{j}")
                    done(act.activation(small[:, j, 3, :], small[:, j, 1, :], ACT.Exp, bias=sink), f"esink_{j}")
                ahead(L, "in_gates", lap, 1)
                send(L, "in_gates", lap, 0, lap * 6 + Z_GATE)
                for j in range(2):
                    for g in range(2):
                        W(h_pe, HG_PE, f"probT_{j}{g}")
                        done(act.activation(pT_[:, j, 2 * g:2 * g + 2, :, :].rearrange("p t a c -> p (t a c)"),
                                            bank[4 + 2 * j + g][:], ACT.Copy), f"probT_{j}{g}")
                send(L, "in_gates", lap, 1, lap * 6 + (Z_GATE + 1))
                ahead(L, "in_gates", lap, 2)
                act.wait_ge(ya_out, 16 * n + 16)
                W(h_pe, HG_PE, "att")
                done(act.activation(yatt[:], bank[4][:], ACT.Copy), "yatt")
                W(h_pe, HG_PE, "hv")
                done(act.activation(hv_tok[:], tokens(bank[5][:]), ACT.Copy), "hv_tok")
                act.wait_ge(h_act.sem, h_act.at(step(HG_ACT, n, "yatt")))
                act.dma_start(yd[bass.ds(act.snap(lap + Y_A), 1), :, :].rearrange("a p c -> p (a c)"), yatt[:]).then_inc(ya_out, 16)
                send(L, "in_gates", lap, 2, lap * 6 + (Z_GATE + 2))
                for l in range(LEVELS):
                    if l == LEVELS - 2:
                        done(act.activation(logf[:], bsum[:], ACT.Exp), "eb")
                    m = 1 << l
                    half = lambda t: t[:, l % 2, :].rearrange("p (b a m) -> p b a m", a=2, m=m)
                    W(h_dve, HG_DVE, f"d{l}")
                    if l >= 2:
                        W(h_pool, HG_POOL, f"qk{l - 2}")
                    act.activation(half(ex)[:, :, 0, :], half(dd)[:, :, 0, :], ACT.Exp, scale=-1.0)
                    done(act.activation(half(ex)[:, :, 1, :], half(dd)[:, :, 1, :], ACT.Exp), f"ex{l}")
                    if l in (2, 5):
                        ahead(L, "in_gates", lap, l // 3 + 3)
                W(h_dve, HG_DVE, "dend")
                W(h_pool, HG_POOL, f"qk{LEVELS - 1}")
                done(act.activation(ex[:, 1, :], dd[:, 1, :], ACT.Exp, scale=-1.0), "ed")
                send(L, "in_gates", lap, 3, lap * 6 + (Z_GATE + 3))
                send(L, "in_gates", lap, 0, lap * 6 + (Z_GATE + 4), 2)
                W(h_pe, HG_PE, "hk")
                done(act.activation(hk_tok[:], tokens(bank[4][:]), ACT.Copy), "hk_tok")
                ahead(L, "in_gates", lap, 5)
                send(L, "in_gates", lap, 1, lap * 6 + (Z_GATE + 5), 2)
                W(h_pe, HG_PE, "o")
                act.wait_ge(yc_out, 16 * n + 16)
                done(act.activation(ho[:], bank[6][:], ACT.Copy), "o")
                done(act.activation(hsq[:], bank[6][:], ACT.Square), "o_sq")
                W(h_pe, HG_PE, "o_norm")
                done(act.activation(hsq[:], bank[7][:], ACT.Sqrt, scale=1.0 / P, bias=eps_col[:, 0:1]), "o_sd")
                W(h_dve, HG_DVE, "y")
                act.dma_start(yd[bass.ds(act.snap(lap + Y_C), 1), :, :].rearrange("a p c -> p (a c)"), ho[:]).then_inc(yc_out, 16)
                assert order == HG_ACT, order

            def mixer(L):
                norm(4 * L + 1)
                with act.Fori(0, 10) as lap:
                    for q in range(2):
                        ahead(L, "in_ab", lap, q)
                        send(L, "in_ab", lap, q, lap * 2 + q)
                act.wait_ge(l_dve.sem, l_dve.at(step(LY_DVE, L, "mt_zero")))
                for b in range(2):
                    act.wait_ge(stage_out[b], 16 * STAGE[b].nth(L, "in_ab", 9) + 16)
                fetch(zr[:, 0, 1:SEQ + 1], Z_WA, wag_in)
                fetch(zr[:, 1, 1:SEQ + 1], Z_G, wag_in)
                act.wait_ge(l_dve.sem, l_dve.at(step(LY_DVE, L, "g")))
                act.activation(xwa[0:64, :], xwa[0:64, :], ACT.Tanh).then_inc(l_act.sem, 1)
                act.activation(xgs[:], xgs[:], ACT.Sigmoid).then_inc(l_act.sem, 1)
                with act.Fori(0, PAIRS) as lap:
                    rwkv_lap(L, lap)
                act.wait_ge(yb_out, 16 * (4 * L) + (64 + 16))
                for b in range(4):
                    act.wait_ge(stage_out[b], 16 * STAGE[b].nth(L, "in_c", 3) + 16)
                fetch(kvraw[:, 0, :], Z_K, kv_in)
                fetch(kvraw[:, 1, :], Z_V, kv_in)
                act.wait_ge(kv_in, 32 * L + 32)
                for kv in range(2):
                    for r in range(2):
                        act.activation(krep[r * 64:r * 64 + 64, kv, :], kvraw[kv * 64:kv * 64 + 64, 0, :], ACT.Copy)\
                           .then_inc(l_act.sem, 1)
                act.wait_ge(l_pe.sem, l_pe.at(step(LY_PE, L, "v")))
                act.activation(vtok2[:].rearrange("p k t c -> p t k c"), bank[4][:].rearrange("p (t k c) -> p t k c", t=TT, k=2),
                               ACT.Copy).then_inc(l_act.sem, 1)
                with act.Fori(0, PAIRS) as lap:
                    hgrn_lap(L, lap)
                for b in range(4):
                    act.wait_ge(stage_out[b], 16 * STAGE[b].nth(L, "in_gates", 3, 2 if b < 2 else 1) + 16)
                for sem in (ya_out, yb_out, yc_out):
                    act.wait_ge(sem, 16 * (4 * L) + (64 + 16))
                gate_view = zd[Z_GATE:Z_TILES, :, :].rearrange("(b m) p c -> m p b c", b=3)

                def gate_fetch(m, i):
                    src = gate_view[bass.ds(act.snap(m), 1), :, :, :] if not isinstance(m, int) else gate_view[m:m + 1, :, :, :]
                    act.dma_start(gates[:, i, :, :], src.rearrange("a p b c -> p (a b) c")).then_inc(gates_in[i], 16)

                with act.Fori(0, 12 // Y_RAW) as lap:
                    for i in range(Y_RAW):
                        act.wait_ge(m_lo.sem, m_lo.at(12 * L + Y_RAW * lap + (i + 1 - Y_RAW)))
                        tile = act.snap(lap * Y_RAW + i)
                        act.dma_start(yraw[:, i, :], yd[bass.ds(tile, 1), :, :].rearrange("a p c -> p (a c)")).then_inc(y_in[i], 16)
                    for i in range(Y_RAW):
                        act.wait_ge(y_in[i], 16 * (12 // Y_RAW * L + lap) + 16)
                        act.activation(yhi[:, bass.ds(act.snap(lap * Y_RAW + i), 1), :].rearrange("p a c -> p (a c)"), yraw[:, i, :],
                                       ACT.Copy).then_inc(m_hi.sem, 1)
                gate_fetch(0, 0)

                def merge_lap(lap, last):
                    for i in range(2):
                        u = 8 * L + 2 * lap + i + 1
                        act.wait_ge(m_sum.sem, m_sum.at(u - 1))
                        if not (last and i):
                            gate_fetch(lap * 2 + i + 1, 1 - i)
                        act.wait_ge(gates_in[i], 16 * (4 * L + lap) + 16)
                        act.activation(gates[:, i, :, :], gates[:, i, :, :], ACT.Sigmoid).then_inc(m_sig.sem, 1)
                        for q in range(3 * i, 3 * i + 3):
                            ahead(L, "merge", lap, q, W_BUF if q == 5 else PAIRS * P)
                        act.wait_ge(m_sum.sem, m_sum.at(u))
                        act.activation(mhi[:, bass.ds(act.snap(lap * 2 + i), 1), :].rearrange("p a c -> p (a c)") if not last
                                       else mhi[:, lap * 2 + i, :], acc[:, 0, :], ACT.Copy).then_inc(m_mhi.sem, 1)
                with act.Fori(0, KD // 2 - 1) as lap:
                    merge_lap(lap, False)
                merge_lap(KD // 2 - 1, True)
                with act.Fori(0, KD // 2) as lap:
                    for q in range(2):
                        ahead(L, "w_o", lap, q)
                        act.wait_ge(read[q].sem, read[q].at(BANK[q].nth(L, "w_o", lap)))
                        m = act.snap(lap * 2 + q)
                        prep(4 * L + 2, m, q, lc[:, bass.ds(act.snap(m + COL["ffn2_norm"]), 1)], ghi)

            with act.Fori(0, DEPTH) as L:
                act.wait_ge(lc_ready.sem, L + 1)
                convert(L, "f1a_up", 0, 1, 0)
                ffn(L, 1, 4 * L, COL["mix_norm"])
                mixer(L)
                ffn(L, 2, 4 * L + 2, COL["ple_norm"])
                for m in range(2):
                    act.wait_ge(p_copied.sem, p_copied.at(2 * L + m + 1))
                    act.activation(phi[:, m, :], pT[:, m, :], ACT.Copy).then_inc(p_hi.sem, 1)
                norm(4 * L + 3)

                def ple_lap(lap, last):
                    for i in range(2):
                        n = 8 * L + 2 * lap + i + 1
                        convert(L, "ple", lap, i + 1, 1, 2 * P)
                        if not (last and i == 1):
                            convert(L, "ple", lap, i + 2, 0)
                        act.wait_ge(read[2 * i].sem, read[2 * i].at(BANK[2 * i].nth(L, "ple", lap)))
                        act.activation(pgate[:, i, :], pgate[:, i, :], ACT.Sigmoid).then_inc(p_sig.sem, 1)
                        act.wait_ge(p_add.sem, p_add.at(n))
                        m = lap * 2 + i if last else act.snap(lap * 2 + i)
                        gain = lc[:, NEXT_GAIN + m:NEXT_GAIN + m + 1] if last else lc[:, bass.ds(act.snap(m + NEXT_GAIN), 1)]
                        prep(4 * L + 4, m, i, gain, fhi)
                with act.Fori(0, KD // 2 - 1) as lap:
                    ple_lap(lap, False)
                ple_lap(KD // 2 - 1, True)
            norm(4 * DEPTH)

        @block.gpsimd
        def _(pool):
            for s in (g_sum, f_act, f_lo, p_lo, w_pool, h_pool, m_mlo):
                pool.sem_inc(s.sem, s.ahead)
            pool.memset(ident[:], 0.0).then_inc(const.sem, 1)
            pool.memset(ones[:], 1.0).then_inc(const.sem, 1)
            pool.memset(zero[:], 0.0).then_inc(zero_set.sem, 1)
            pool.memset(eps_col[:], EPS).then_inc(eps_set.sem, 1)
            pool.wait_ge(const.sem, 2)
            pool.affine_select(out=ident[:], in_=ident[:], compare_op=ALU.not_equal, fill=1.0, base=0,
                               pattern=[[-1, P]], channel_multiplier=1).then_inc(const.sem, 1)

            masks_left = [0]

            def fill(ap, value, waits=0):
                pool.memset(ap, value).then_inc(masks.sem, 1)
                masks_left[0] += 1
                pool.wait_ge(masks.sem, masks_left[0])

            def keep(out_ap, in_ap, base, pattern, rows=1, fill_=0.0):
                pool.affine_select(out=out_ap, in_=in_ap, compare_op=ALU.is_ge, fill=fill_, base=base, pattern=pattern,
                                   channel_multiplier=rows).then_inc(masks.sem, 1)
                masks_left[0] += 1
                pool.wait_ge(masks.sem, masks_left[0])

            minus = xsq[:, 0, 0:P]
            plus = xsq[:, 0, P:2 * P]
            fill(minus, -1.0)
            fill(plus, 1.0)
            fill(low[:], 0.0)
            fill(up0[:], 0.0)
            fill(pair_mask[:], 0)
            fill(gn_eps[:], GN_EPS)
            for l in range(LEVELS):
                m = 1 << l
                halves = lambda ap: ap.rearrange("p (b a m) -> p b a m", a=2, m=m)
                nb = P // (2 * m)
                if l < LEVELS - 1:
                    t_, s_ = halves(low[:, l, :]), halves(minus if l == 0 else plus)
                    keep(t_[:, :, 0, :], s_[:, :, 0, :], -m, [[-2 * m, nb], [0, m]])
                    keep(t_[:, :, 0, :], t_[:, :, 0, :], 2 * m - 1, [[2 * m, nb], [0, m]], -1)
                t_, s_ = halves(pair_mask[:, l, :]), halves(plus)
                keep(t_[:, :, 1, :], s_[:, :, 1, :], 0, [[-2 * m, nb], [0, m]])
                keep(t_[:, :, 1, :], t_[:, :, 1, :], m - 1, [[2 * m, nb], [0, m]], -1)
                if l == 0:
                    t_ = halves(up0[:])
                    keep(t_[:, :, 1, :], s_[:, :, 1, :], 0, [[-2 * m, nb], [0, m]])
                    keep(t_[:, :, 1, :], t_[:, :, 1, :], m - 1, [[2 * m, nb], [0, m]], -1)
            pool.tensor_copy(pair_mask[:, LEVELS, :], ident[:]).then_inc(masks.sem, 1)
            masks_left[0] += 1
            chunks = [[-HD, 2], [0, HD]]
            keep(before[:], minus, -1, [[1, P]], -1)
            keep(before[:], before[:], 0, chunks)
            keep(upto[:], plus, 0, [[1, P]], -1)
            keep(upto[:], upto[:], 0, chunks)
            fill(band[:], 0.0)
            fill(band[:, 0, :], MASKED)
            keep(band[:, 2, :], band[:, 2, :], -1, [[1, P]], -1, MASKED)
            for i in (1, 3):
                keep(band[:, i, :], band[:, i, :], 0, [[-1, P]], 1, MASKED)
            fill(seg64[:], 1.0)
            fill(seg64[:].rearrange("p (c s) -> p c s", s=HD)[:, :, 0], 0.0)
            fill(seg128[:], 1.0)
            fill(seg128[:].rearrange("p (c s) -> p c s", s=P)[:, :, 0], 0.0)
            fill(head_ones[:], 0.0)
            fill(head_ones[0:64, 0:64], 1.0)
            fill(head_ones[64:P, 64:P], 1.0)
            pool.tensor_copy(eye64[0:64, :], ident[0:64, 0:64]).then_inc(masks.sem, 1)
            pool.wait_ge(masks.sem, MASK_STEPS - 1)
            pool.tensor_copy(eye64[64:P, :], ident[64:P, 64:P]).then_inc(masks.sem, 1)
            pool.wait_ge(masks.sem, MASK_STEPS)
            masks_left[0] += 2
            assert masks_left[0] == MASK_STEPS, masks_left

            def prep(e, m, i):
                n = 8 * e + m + 1
                pool.wait_ge(g_sq.sem, g_sq.at(n))
                pool.wait_ge(g_sum.sem, g_sum.at(n - 1))
                pool.wait_ge(sum_clear.sem, e + 1)
                pool.tensor_tensor(ssum[:], ssum[:], xsq[:, i, :], ALU.add).then_inc(g_sum.sem, 1)

            def clear_sum(e):
                pool.wait_ge(n_sum.sem, n_sum.at(e))
                pool.tensor_tensor(ssum[:], zero[:, 0:1].broadcast_to([P, SEQ]), zero[:, 0:1].broadcast_to([P, SEQ]),
                                   ALU.add).then_inc(sum_clear.sem, 1)

            pool.wait_ge(zero_set.sem, 1)
            pool.wait_ge(const.sem, 3)
            clear_sum(0)
            for m in range(KD):
                prep(0, m, m % 2)

            def ffn(L, f, event):
                done = L * (2 * sum(HALF_TILES)) + (f - 1) * sum(HALF_TILES)
                for half, tiles in zip("ab", HALF_TILES):
                    up_, down_ = f"f{f}{half}_up", f"f{f}{half}_down"
                    with pool.Fori(0, tiles) as j:
                        n = done + j + 1
                        pool.wait_ge(f_sig.sem, f_sig.at(n))
                        pool.wait_ge(f_h.sem, f_h.at(n - 1))
                        pool.tensor_tensor(gate_act[:], gate_in[:], gate_sig[:], ALU.mult).then_inc(f_act.sem, 1)
                        pool.wait_ge(f_hi.sem, f_hi.at(n))
                        pool.tensor_tensor(hlo[:, j, :], h[:], hhi[:, j, :].bitcast(F32), ALU.subtract).then_inc(f_lo.sem, 1)
                    nk = tiles // 2
                    if half == "b":
                        clear_sum(event + 1)
                    with pool.Fori(0, KD // 2) as lap:
                        for i in range(2):
                            if half == "b":
                                prep(event + 1, pool.snap(lap * 2 + i), i)
                    done = done + tiles

            def rwkv_lap(L, lap):
                n = pool.snap(L * PAIRS + lap)
                order = []
                done = lambda ins, name: pe_mark(ins, w_pool, RW_POOL, name, order)
                W = lambda sig, table, name, back=0: pool.wait_ge(sig.sem, sig.at(step(table, n - back, name)))
                mine = bass.ds(pool.snap(lap * P), P)
                last = lambda t: t[:].rearrange("p (c s) -> p c s", s=HD)[:, :, HD - 1:HD]
                pool.wait_ge(lora_in, 48 * L + 48)
                W(w_pe, RW_PE, "g", 1)
                done(pool.tensor_copy(lwa[:], lora_wa[:, mine]), "lora_wa")
                done(pool.tensor_copy(lg[:], lora_g[:, mine]), "lora_g")
                W(w_dve, RW_DVE, "kk")
                W(w_act, RW_ACT, "a")
                done(pool.tensor_tensor(bb[:], kk[:], a_[:], ALU.mult), "b")
                W(w_dve, RW_DVE, "kp")
                W(w_pe, RW_PE, "bonus", 1)
                done(pool.tensor_tensor(rk[:], r_[:], kp[:], ALU.mult), "rk")
                W(w_act, RW_ACT, "inc")
                W(w_pool, RW_POOL, "b")
                done(pool.tensor_tensor(bb[:], bb[:], inc[:], ALU.mult), "bt")
                W(w_pool, RW_POOL, "rk")
                done(pool.tensor_tensor(r_[:], r_[:], dec[:], ALU.mult), "rt")
                done(pool.tensor_tensor(kp[:], kp[:], inc[:], ALU.mult), "kt")
                done(pool.tensor_tensor(ediag[:], eye64[:].unsqueeze(1).broadcast_to([P, C, HD]),
                                        last(dec).broadcast_to([P, C, HD]), ALU.mult), "ediag")
                for h in range(2):
                    W(w_dve, RW_DVE, f"NT_{h}")
                    done(pool.tensor_tensor(XT[:, h, :, :], NT[:, h, :, :], up0[:].unsqueeze(1).broadcast_to([P, TT, P]),
                                            ALU.mult), f"XTm_{h}")
                eye = ident[:].unsqueeze(1).broadcast_to([P, TT, P])
                for h in range(2):
                    W(w_dve, RW_DVE, f"X_{h}")
                    done(pool.tensor_tensor(X[:, h, :, :], X[:, h, :, :], eye, ALU.add), f"X_{h}")
                for h in range(2):
                    W(w_pool, RW_POOL, f"XTm_{h}")
                    done(pool.tensor_tensor(XT[:, h, :, :], XT[:, h, :, :], eye, ALU.add), f"XT_{h}")
                W(w_act, RW_ACT, "y_ln")
                done(pool.tensor_tensor(y_[:], y_[:], bonus[:], ALU.add), "y_b")
                W(w_pool, RW_POOL, "y_b")
                done(pool.tensor_tensor(y_[:], y_[:], g_[:], ALU.mult), "y")
                assert order == RW_POOL, order

            def hgrn_lap(L, lap):
                n = pool.snap(L * PAIRS + lap)
                order = []
                done = lambda ins, name: pe_mark(ins, h_pool, HG_POOL, name, order)
                W = lambda sig, table, name, back=0: pool.wait_ge(sig.sem, sig.at(step(table, n - back, name)))
                kv = pool.snap(lap // 2)
                pool.wait_ge(l_act.sem, l_act.at(step(LY_ACT, L, "v")))
                W(h_pe, HG_PE, "att", 1)
                done(pool.tensor_copy(kcur[:], krep[:, bass.ds(kv, 1), :].rearrange("p a c -> p (a c)")), "kcur")
                done(pool.tensor_copy(vcur[:], vtok2[:, bass.ds(kv, 1), :, :].rearrange("p a t c -> p (a t) c")), "vcur")
                W(h_dve, HG_DVE, "f")
                W(h_pe, HG_PE, f"att{LEVELS}", 1)
                done(pool.tensor_tensor(key[:], ones[:, 0:1].broadcast_to([P, SEQ]), fg[:], ALU.subtract), "key")
                W(h_act, HG_ACT, "sig_q")
                done(pool.tensor_tensor(hq[:], hq[:], hz[:, 0, :], ALU.mult), "hq")
                W(h_act, HG_ACT, "sig_o")
                done(pool.tensor_tensor(hog[:], hog[:], hz[:, 3, :], ALU.mult), "hog")
                for l in range(LEVELS):
                    m = 1 << l
                    half = lambda t: t.rearrange("p (b a m) -> p b a m", a=2, m=m)
                    W(h_act, HG_ACT, f"ex{l}")
                    if l == 0:
                        W(h_pool, HG_POOL, "hq")
                    if l >= 2:
                        W(h_pe, HG_PE, f"att{l - 2}")
                    pool.tensor_tensor(half(qk[:, l % 2, :])[:, :, 0, :], half(key[:])[:, :, 0, :],
                                       half(ex[:, l % 2, :])[:, :, 0, :], ALU.mult)
                    done(pool.tensor_tensor(half(qk[:, l % 2, :])[:, :, 1, :], half(hq[:])[:, :, 1, :],
                                            half(ex[:, l % 2, :])[:, :, 1, :], ALU.mult), f"qk{l}")
                W(h_act, HG_ACT, "ed")
                done(pool.tensor_tensor(dd[:, 1, :], key[:], ex[:, 1, :], ALU.mult), "kd")
                assert order == HG_POOL, order

            def mixer(L):
                with pool.Fori(0, PAIRS) as lap:
                    rwkv_lap(L, lap)
                with pool.Fori(0, PAIRS) as lap:
                    hgrn_lap(L, lap)
                with pool.Fori(0, KD // 2) as lap:
                    for i in range(2):
                        pool.wait_ge(m_mhi.sem, m_mhi.at(8 * L + 2 * lap + (i + 1)))
                        tile = bass.ds(pool.snap(lap * 2 + i), 1)
                        pool.tensor_tensor(mlo[:, tile, :].rearrange("p a c -> p (a c)"), acc[:, 0, :],
                                           mhi[:, tile, :].rearrange("p a c -> p (a c)").bitcast(F32), ALU.subtract)\
                            .then_inc(m_mlo.sem, 1)
                clear_sum(4 * L + 2)
                with pool.Fori(0, KD // 2) as lap:
                    for q in range(2):
                        prep(4 * L + 2, pool.snap(lap * 2 + q), q)

            with pool.Fori(0, DEPTH) as L:
                ffn(L, 1, 4 * L)
                mixer(L)
                ffn(L, 2, 4 * L + 2)
                for m in range(2):
                    pool.wait_ge(p_hi.sem, p_hi.at(2 * L + m + 1))
                    pool.tensor_tensor(plo[:, m, :], pT[:, m, :], phi[:, m, :].bitcast(F32), ALU.subtract).then_inc(p_lo.sem, 1)
                clear_sum(4 * L + 4)

                def ple_lap(lap, last):
                    for i in range(2):
                        prep(4 * L + 4, lap * 2 + i if last else pool.snap(lap * 2 + i), i)
                with pool.Fori(0, KD // 2 - 1) as lap:
                    ple_lap(lap, False)
                ple_lap(KD // 2 - 1, True)

        @block.vector
        def _(dve):
            for s in (*w_lo, g_lo, m_lo, *read, n_rstd, f_h, p_copied, p_mul, p_add, w_dve, h_dve, l_dve, m_sum, acc_step):
                dve.sem_inc(s.sem, s.ahead)
            dve.wait_ge(turned.sem, DEPTH)
            for L in range(DEPTH):
                dve.tensor_copy(cols[:, L * LAYER_COLS:(L + 1) * LAYER_COLS],
                                bank[6][:, L * P:L * P + LAYER_COLS]).then_inc(col_copy.sem, 1)
            dve.tensor_copy(cols[:, DEPTH * LAYER_COLS:DEPTH * LAYER_COLS + 8],
                            bank[6][:, LAYER_COLS:LAYER_COLS + 8]).then_inc(cols_ready.sem, 1)
            for m in range(KD):
                dve.wait_ge(turned.sem, DEPTH + m + 1)
                dve.tensor_copy(x[:, m, :], bank[m % 2][:]).then_inc(x_new.sem, 1)

            def norm(e):
                dve.wait_ge(n_rms.sem, n_rms.at(e + 1))
                dve.reciprocal(rstd[:], rstd[:]).then_inc(n_rstd.sem, 1)

            def split(L, section, lap, k, slot, n=W_BUF):
                use = SLOT.nth(L, section, lap, k)
                dve.wait_ge(w_hi[slot].sem, w_hi[slot].at(use))
                dve.tensor_tensor(wlo[:, slot, 0:n], wraw[:, slot, 0:n], whi[:, slot, 0:n].bitcast(F32),
                                   ALU.subtract).then_inc(w_lo[slot].sem, 1)

            def ahead(L, section, lap, q, n=W_BUF):
                split(L, section, lap, (q + 1) // 2 + 1, (q + 1) % 2, n)

            def prep(e, m, gain, hi, lo):
                dve.wait_ge(g_hi.sem, g_hi.at(8 * e + m + 1))
                dve.scalar_tensor_tensor(lo[:, m, :], x[:, m, :], gain, hi[:, m, :].bitcast(F32), ALU.mult, ALU.subtract)\
                   .then_inc(g_lo.sem, 1)

            def take(L, e, section, lap, b, slot, k, out_ap):
                dve.wait_ge(n_rstd.sem, n_rstd.at(e + 1))
                dve.wait_ge(used[slot].sem, used[slot].at(SLOT.nth(L, section, lap, k)))
                dve.tensor_tensor(out_ap, bank[b][:], rstd[:], ALU.mult).then_inc(read[b].sem, 1)

            def ffn(L, f, event, next_gain):
                done = L * (2 * sum(HALF_TILES)) + (f - 1) * sum(HALF_TILES)
                for half, tiles in zip("ab", HALF_TILES):
                    up_, down_ = f"f{f}{half}_up", f"f{f}{half}_down"
                    if half == "a":
                        norm(event)
                    with dve.Fori(0, tiles) as j:
                        n = done + j + 1
                        dve.wait_ge(f_act.sem, f_act.at(n - 1))
                        split(L, up_, j, 1, 1)
                        take(L, event, up_, j, 0, 0, 1, gate_in[:])
                        split(L, up_, j, 2, 0)
                        dve.wait_ge(f_h.sem, f_h.at(n - 1))
                        take(L, event, up_, j, 1, 1, 1, up[:])
                        dve.wait_ge(f_act.sem, f_act.at(n))
                        dve.wait_ge(f_lo.sem, f_lo.at(n - 1))
                        dve.wait_ge(read[1].sem, read[1].at(BANK[1].nth(L, up_, j)))
                        dve.tensor_tensor(h[:], up[:], gate_act[:], ALU.mult).then_inc(f_h.sem, 1)
                    with dve.Fori(0, KD // 2) as lap:
                        for i in range(2):
                            m = dve.snap(lap * 2 + i)
                            split(L, down_, lap, i + 1, 1, tiles // 2 * P)
                            split(L, down_, lap, i + 2, 0)
                            dve.wait_ge(used[1].sem, used[1].at(SLOT.nth(L, down_, lap, i + 1)))
                            dve.wait_ge(g_sum.sem, g_sum.at(8 * event + 8))
                            dve.scalar_tensor_tensor(x[:, m, :], bank[i][:], 0.5, x[:, m, :], ALU.mult, ALU.add)\
                               .then_inc(read[i].sem, 1)
                            if half == "b":
                                prep(event + 1, m, lc[:, bass.ds(dve.snap(m + next_gain), 1)], ghi, glo)
                    done = done + tiles

            dve.wait_ge(cols_ready.sem, 1)
            lbc = lambda L: cols[:, L * LAYER_COLS + COL["hgrn_lb"]:L * LAYER_COLS + COL["hgrn_lb"] + PAIRS]
            dve.memset(lb[:, 0:PAIRS], 0.0).then_inc(lb_step.sem, 1)
            dve.tensor_tensor(lb_rest[:, 0:PAIRS], lbc(1), lbc(0), ALU.subtract).then_inc(lb_step.sem, 1)
            dve.wait_ge(lb_sig.sem, 1)
            dve.tensor_scalar(lb[:, PAIRS:2 * PAIRS], lb[:, PAIRS:2 * PAIRS], 1.0 - 1e-6, None, ALU.min).then_inc(lb_step.sem, 1)
            dve.wait_ge(lb_step.sem, 3)
            dve.tensor_scalar(lb_rest[:], lb[:], -1.0, 1.0, ALU.mult, ALU.add).then_inc(lb_ready.sem, 1)

            def stage_take(L, section, lap, q, b, k=1):
                ahead(L, section, lap, q)
                dve.wait_ge(stage_out[b], 16 * STAGE[b].nth(L, section, lap, k))
                take(L, 4 * L + 1, section, lap, b, q % 2, q // 2 + 1, stage[:, b, :])

            def rwkv_lap(L, lap):
                n = dve.snap(L * PAIRS + lap)
                order = []
                done = lambda ins, name: pe_mark(ins, w_dve, RW_DVE, name, order)
                W = lambda sig, table, name, back=0: dve.wait_ge(sig.sem, sig.at(step(table, n - back, name)))
                mine = lambda name: W(w_dve, RW_DVE, name)
                col = lambda name, i=0: lc[:, bass.ds(dve.snap(lap + (COL[name] + i)), 1)]
                chunks = lambda ap: ap.rearrange("p (c s) -> p c s", s=HD)
                tiles = lambda ap: ap.rearrange("p (t c) -> p t c", t=TT)
                bc = lambda m: m.unsqueeze(1).broadcast_to([P, TT, P])
                dve.wait_ge(rkv_in, 48 * n + 48)
                W(w_pe, RW_PE, "var", 1)
                for i, (dst, name) in enumerate(((r_, "r"), (k_, "k"), (v_, "v"))):
                    if i:
                        mine("rk"[i - 1])
                    done(dve.tensor_tensor(shift[:], zr[:, i, 0:SEQ], zr[:, i, 1:SEQ + 1], ALU.subtract), "d" + name)
                    mine("d" + name)
                    done(dve.scalar_tensor_tensor(dst[:], shift[:], col("rwkv_mu", 4 * i), zr[:, i, 1:SEQ + 1],
                                                  ALU.mult, ALU.add), name)
                W(w_act, RW_ACT, "w")
                done(dve.tensor_tensor_scan(cs[:], seg64[:], w_[:], 0.0, ALU.mult, ALU.add), "cs")
                stage_take(L, "in_c", lap, 0, 0)
                W(w_pe, RW_PE, "kk_norm")
                done(dve.tensor_scalar(tmp[:], bank[4][:], 1e-24, None, ALU.max), "kmax")
                W(w_act, RW_ACT, "kk_root")
                done(dve.reciprocal(tmp[:], tmp[:]), "krs")
                mine("krs")
                done(dve.tensor_tensor(kk[:], kk[:], tmp[:], ALU.mult), "kk")
                W(w_act, RW_ACT, "a")
                done(dve.tensor_scalar(shift[:], a_[:], 1.0, col("rwkv_k_a"), ALU.subtract, ALU.mult), "ka")
                mine("ka")
                done(dve.scalar_tensor_tensor(kp[:], shift[:], 1.0, k_[:], ALU.add, ALU.mult), "kp")
                mine("kk")
                done(dve.tensor_tensor(chunks(kq[:])[:, :, 1:HD], chunks(kk[:])[:, :, 1:HD], chunks(dec[:])[:, :, 0:HD - 1],
                                       ALU.mult), "kq")
                last = chunks(dec[:])[:, :, HD - 1:HD].broadcast_to([P, C, HD])
                W(w_pool, RW_POOL, "bt")
                done(dve.tensor_tensor(chunks(bh[:]), chunks(bb[:]), last, ALU.mult), "bh")
                W(w_pool, RW_POOL, "kt")
                done(dve.tensor_tensor(chunks(kh[:]), chunks(kp[:]), last, ALU.mult), "kh")
                stage_take(L, "in_c", lap, 1, 1)
                W(w_pe, RW_PE, "bonus")
                W(w_pool, RW_POOL, "y_b", 1)
                done(dve.tensor_tensor(bonus[:], bank[5][:], v_[:], ALU.mult), "bonus")
                for h in range(2):
                    W(w_pe, RW_PE, f"A1T_{h}")
                    done(dve.tensor_tensor(NT[:, h, :, :], tiles(bank[6 + h][:]), bc(before[:]), ALU.mult), f"NT_{h}")
                for h in range(2):
                    W(w_pe, RW_PE, f"A1_{h}")
                    done(dve.tensor_tensor(X[:, h, :, :], tiles(bank[4 + h][:]), bc(low[:, 0, :]), ALU.mult), f"X_{h}")
                for h in range(2):
                    W(w_pe, RW_PE, f"A2T_{h}")
                    done(dve.tensor_tensor(T1[:, h, :, :], tiles(bank[6 + h][:]), bc(before[:]), ALU.mult), f"A2T_{h}")
                stage_take(L, "in_c", lap, 2, 2)
                for l in range(1, LEVELS - 1):
                    for h in range(2):
                        W(w_pe, RW_PE, f"T{l}_{h}")
                        done(dve.tensor_tensor(T1[:, h, :, :], tiles(bank[4 + h][:]), bc(low[:, l, :]), ALU.mult), f"T{l}_{h}")
                    for h in range(2):
                        W(w_pe, RW_PE, f"X{l}_{h}")
                        done(dve.tensor_tensor(XT[:, h, :, :], tiles(bank[6 + h][:]), XT[:, h, :, :], ALU.add), f"XT{l}_{h}")
                    if l < LEVELS - 2:
                        for h in range(2):
                            done(dve.tensor_tensor(X[:, h, :, :], tiles(bank[4 + h][:]), X[:, h, :, :], ALU.add), f"X{l}_{h}")
                for h in range(2):
                    W(w_pe, RW_PE, f"B1T_{h}")
                    done(dve.tensor_tensor(NT[:, h, :, :], tiles(bank[6 + h][:]), bc(upto[:]), ALU.mult), f"B1T_{h}")
                for h in range(2):
                    W(w_pe, RW_PE, f"B2T_{h}")
                    done(dve.tensor_tensor(X[:, h, :, :], tiles(bank[4 + h][:]), bc(upto[:]), ALU.mult), f"B2T_{h}")
                W(w_pe, RW_PE, "R2")
                done(dve.tensor_tensor(r_[:], bank[6][:], r_[:], ALU.add), "R2")
                W(w_pool, RW_POOL, "ediag")
                for par, b in ((0, bank[7]), (1, bank[4])):
                    W(w_pe, RW_PE, f"state_{par}")
                    W(w_act, RW_ACT, f"NZ_{par}")
                    for h in range(2):
                        hc = slice(h * HD, (h + 1) * HD)
                        every = lambda ap: ap.rearrange("p (t a) c -> p a t c", a=2)[hc, par, :, :]
                        done(dve.tensor_tensor(every(MT[:])[:, :, hc], b[hc, 0:TT * HD].rearrange("p (t c) -> p t c", t=TT),
                                               every(ediag[:]), ALU.add), "MT" if par and h else f"M{par}{h}")
                done(dve.tensor_copy(Z[:, 1, :], NZ[:, 0, :]), "Z1")
                for c in range(2, C):
                    W(w_pe, RW_PE, f"Z{c}")
                    done(dve.tensor_tensor(Z[:, c, :], bank[5][:, (c - 1) * HD:c * HD], NZ[:, c - 1, :], ALU.add), f"Z{c}")
                stage_take(L, "in_c", lap, 3, 3)
                W(w_pe, RW_PE, "y_1")
                done(dve.tensor_copy(y_[HD:P, :], bank[4][HD:P, :]), "y_1")
                W(w_pe, RW_PE, "mean")
                done(dve.scalar_tensor_tensor(y_[:], bank[5][:], -1.0 / HD, y_[:], ALU.mult, ALU.add), "yc")
                W(w_act, RW_ACT, "y_sd")
                done(dve.reciprocal(tmp[:], tmp[:]), "yrs")
                mine("yrs")
                done(dve.tensor_tensor(y_[:], y_[:], tmp[:], ALU.mult), "yn")
                assert order == RW_DVE, order

            def hgrn_lap(L, lap):
                n = dve.snap(L * PAIRS + lap)
                order = []
                done = lambda ins, name: pe_mark(ins, h_dve, HG_DVE, name, order)
                W = lambda sig, table, name, back=0: dve.wait_ge(sig.sem, sig.at(step(table, n - back, name)))
                mine = lambda name: W(h_dve, HG_DVE, name)
                tiles = lambda ap: ap.rearrange("p (t c) -> p t c", t=TT)
                head = bass.ds(n, 1)
                W(h_act, HG_ACT, "sig_f")
                done(dve.tensor_scalar(fg[:], fg[:], lb_rest[:, head], lb[:, head], ALU.mult, ALU.add), "fl")
                mine("fl")
                done(dve.tensor_scalar(fg[:], fg[:], LN_MIN, None, ALU.max), "f")
                W(h_act, HG_ACT, "logf")
                done(dve.tensor_tensor_scan(bsum[:], seg128[:], logf[:], 0.0, ALU.mult, ALU.add), "bsum")
                stage_take(L, "in_gates", lap, 0, 0)
                for j in range(2):
                    sink = sinks[:, bass.ds(dve.snap(n * 2 + j), 1)]
                    pairs = lambda g: sc[:, j, 2 * g:2 * g + 2, :]
                    W(h_pe, HG_PE, f"scores_{j}0")
                    done(dve.tensor_tensor(pairs(0), bank[4 + 2 * j][:].rearrange("p (t c) -> p t c", t=2),
                                           band[:].rearrange("p (t a) c -> p t (a c)", t=2), ALU.add), f"m0_{j}")
                    W(h_pe, HG_PE, f"scores_{j}1")
                    done(dve.tensor_tensor(pairs(1), bank[5 + 2 * j][:].rearrange("p (t c) -> p t c", t=2),
                                           band[:, 2:4, :].rearrange("p a c -> p (a c)").unsqueeze(1).broadcast_to([P, 2, 2 * P]),
                                           ALU.add), f"m1_{j}")
                    mine(f"m1_{j}")
                    done(dve.tensor_reduce(small[:, j, 0, :], sc[:, j, :, :], AX.X, ALU.max), f"mx_{j}")
                    mine(f"mx_{j}")
                    done(dve.tensor_scalar(small[:, j, 1, :], small[:, j, 0, :], sink, -1.0, ALU.max, ALU.mult), f"max_{j}")
                stage_take(L, "in_gates", lap, 1, 1)
                for j in range(2):
                    W(h_act, HG_ACT, f"esink_{j}")
                    done(dve.tensor_tensor(small[:, j, 4, :], small[:, j, 2, :], small[:, j, 3, :], ALU.add), f"den_{j}")
                    mine(f"den_{j}")
                    done(dve.reciprocal(small[:, j, 5, :], small[:, j, 4, :]), f"rec_{j}")
                    mine(f"rec_{j}")
                    done(dve.tensor_tensor(sc[:, j, :, :], sc[:, j, :, :], small[:, j, 5, :].unsqueeze(2).broadcast_to([P, TT, 2 * P]),
                                           ALU.mult), f"probs_{j}")
                stage_take(L, "in_gates", lap, 2, 2)

                def rel(l):
                    m = 1 << l
                    blocks = lambda ap: ap.rearrange("p (b s) -> p b s", s=2 * m)
                    if l >= 2:
                        W(h_act, HG_ACT, f"ex{l - 2}")
                    if l == 0:
                        mine("bsum")
                        W(h_pe, HG_PE, "hk", 1)
                    done(dve.tensor_tensor(blocks(dd[:, l % 2, :]), blocks(bsum[:]),
                                           blocks(bsum[:])[:, :, m - 1:m].broadcast_to([P, SEQ // (2 * m), 2 * m]),
                                           ALU.subtract), f"d{l}")

                def place(l, between):
                    W(h_pe, HG_PE, f"att{l}")
                    if l == 0:
                        W(h_pe, HG_PE, "o", 1)
                    dve.wait_ge(l_dve.sem, l_dve.at(step(LY_DVE, L, "att_zero")))
                    if l:
                        mine(f"att{l - 1}")
                    between()
                    done(dve.copy_predicated(attT[:], pair_mask[:, l, :].unsqueeze(1).broadcast_to([P, TT, P]),
                                             tiles(bank[6 + l % 2][:])), f"att{l}")

                def from_state():
                    W(h_act, HG_ACT, "eb")
                    done(dve.tensor_tensor(qb[:], hq[:], logf[:], ALU.mult), "qb")

                def to_state():
                    W(h_act, HG_ACT, f"ex{LEVELS - 2}")
                    by_tile = lambda ap: ap.rearrange("p (b s) -> p b s", s=P)
                    done(dve.tensor_tensor(by_tile(dd[:, 1, :]), by_tile(bsum[:]),
                                           by_tile(bsum[:])[:, :, P - 1:P].broadcast_to([P, TT, P]), ALU.subtract), "dend")

                def first_state():
                    W(h_pe, HG_PE, "dS")
                    done(dve.tensor_copy(S[:, 1, :], bank[5][:, 0:P]), "S1")
                rel(0)
                rel(1)
                for l in range(LEVELS):
                    if l in (3, 6):
                        stage_take(L, "in_gates", lap, l // 3 + 2, (l // 3 + 2) % 4, (l // 3 + 2) // 4 + 1)
                    place(l, (lambda: rel(l + 2)) if l < LEVELS - 2 else from_state if l == LEVELS - 2 else to_state)
                place(LEVELS, first_state)
                for t in (2, 3):
                    mine(f"S{t - 1}")
                    done(dve.scalar_tensor_tensor(S[:, t, :], S[:, t - 1, :], logf[:, t * P - 1:t * P], bank[5][:, (t - 1) * P:t * P],
                                                  ALU.mult, ALU.add), f"S{t}")
                stage_take(L, "in_gates", lap, 5, 1, 2)
                W(h_act, HG_ACT, "o_sd")
                done(dve.reciprocal(hsq[:], hsq[:]), "orec")
                mine("orec")
                done(dve.tensor_tensor(ho[:], ho[:], hsq[:], ALU.mult), "on")
                mine("on")
                done(dve.scalar_tensor_tensor(ho[:], ho[:], lc[:, COL["hgrn_norm"]:COL["hgrn_norm"] + 1], hog[:],
                                              ALU.mult, ALU.mult), "y")
                assert order == HG_DVE, order

            def mixer(L):
                norm(4 * L + 1)
                with dve.Fori(0, 10) as lap:
                    for q in range(2):
                        stage_take(L, "in_ab", lap, q, q)
                mark = lambda ins: ins.then_inc(l_dve.sem, 1)
                mine = lambda name: dve.wait_ge(l_dve.sem, l_dve.at(step(LY_DVE, L, name)))
                mark(dve.memset(zr[:, :, 0], 0.0))
                mark(dve.memset(MT[:], 0.0))
                dve.wait_ge(wag_in, 32 * L + 32)
                for i, (dst, name) in enumerate(((xwa, "wa"), (xgs, "g"))):
                    if i:
                        mine("wa")
                    mark(dve.tensor_tensor(shift[:], zr[:, i, 0:SEQ], zr[:, i, 1:SEQ + 1], ALU.subtract))
                    mine("d" + name)
                    mark(dve.scalar_tensor_tensor(dst[:], shift[:], lc[:, COL["rwkv_mu"] + 12 + i:COL["rwkv_mu"] + 13 + i],
                                                  zr[:, i, 1:SEQ + 1], ALU.mult, ALU.add))
                dve.wait_ge(masks.sem, MASK_STEPS)
                with dve.Fori(0, PAIRS) as lap:
                    rwkv_lap(L, lap)
                dve.wait_ge(w_act.sem, w_act.at(step(RW_ACT, 4 * L + 3, "y_ln")))
                mark(dve.memset(attT[:], 0.0))
                with dve.Fori(0, PAIRS) as lap:
                    hgrn_lap(L, lap)
                with dve.Fori(0, 12 // Y_RAW) as lap:
                    for i in range(Y_RAW):
                        dve.wait_ge(m_hi.sem, m_hi.at(12 * L + Y_RAW * lap + (i + 1)))
                        tile = bass.ds(dve.snap(lap * Y_RAW + i), 1)
                        dve.tensor_tensor(ylo[:, tile, :].rearrange("p a c -> p (a c)"), yraw[:, i, :],
                                          yhi[:, tile, :].rearrange("p a c -> p (a c)").bitcast(F32), ALU.subtract)\
                           .then_inc(m_lo.sem, 1)
                with dve.Fori(0, KD // 2) as lap:
                    for i in range(2):
                        u = 8 * L + 2 * lap + (i + 1)
                        for br in range(3):
                            q = 3 * i + br
                            ahead(L, "merge", lap, q, W_BUF if q == 5 else PAIRS * P)
                            dve.wait_ge(used[q % 2].sem, used[q % 2].at(SLOT.nth(L, "merge", lap, q // 2 + 1)))
                            if br == 0:
                                dve.wait_ge(m_sig.sem, m_sig.at(u))
                                dve.wait_ge(m_mlo.sem, m_mlo.at(u - 1))
                            if br == 2:
                                dve.wait_ge(acc_step.sem, acc_step.at(u))
                            dve.tensor_tensor(acc[:, min(br, 1), :], bank[q][:], gates[:, i, br, :], ALU.mult).then_inc(read[q].sem, 1)
                            dve.wait_ge(read[q].sem, read[q].at(BANK[q].nth(L, "merge", lap)))
                            if br:
                                dve.tensor_tensor(acc[:, 0, :], acc[:, 0, :], acc[:, 1, :], ALU.add)\
                                   .then_inc((acc_step if br == 1 else m_sum).sem, 1)
                with dve.Fori(0, KD // 2) as lap:
                    for q in range(2):
                        m = dve.snap(lap * 2 + q)
                        ahead(L, "w_o", lap, q)
                        dve.wait_ge(used[q].sem, used[q].at(SLOT.nth(L, "w_o", lap)))
                        dve.tensor_tensor(x[:, m, :], bank[q][:], x[:, m, :], ALU.add).then_inc(read[q].sem, 1)
                        prep(4 * L + 2, m, lc[:, bass.ds(dve.snap(m + COL["ffn2_norm"]), 1)], ghi, glo)

            for m in range(KD):
                prep(0, m, cols[:, m:m + 1], fhi, flo)
            with dve.Fori(0, DEPTH) as L:
                dve.wait_ge(g_sq.sem, g_sq.at(8 * (4 * L) + 8))
                dve.wait_ge(g_lo.sem, g_lo.at(8 * (4 * L) + 8))
                dve.tensor_copy(lc[:, 0:LAYER_COLS], cols[:, bass.ds(dve.snap(L * LAYER_COLS), LAYER_COLS)])\
                   .then_inc(lc_copied.sem, 1)
                dve.tensor_copy(lc[:, LAYER_COLS:LAYER_COLS + 8], cols[:, bass.ds(dve.snap(L * LAYER_COLS + LAYER_COLS), 8)])\
                   .then_inc(lc_ready.sem, 1)
                split(L, "f1a_up", 0, 1, 0)
                ffn(L, 1, 4 * L, COL["mix_norm"])
                mixer(L)
                ffn(L, 2, 4 * L + 2, COL["ple_norm"])
                for m in range(2):
                    dve.wait_ge(p_turned.sem, p_turned.at(2 * L + m + 1))
                    dve.tensor_copy(pT[:, m, :], bank[4 + m][:]).then_inc(p_copied.sem, 1)
                norm(4 * L + 3)

                def ple_lap(lap, last):
                    for i in range(2):
                        n = 8 * L + 2 * lap + i + 1
                        m = lap * 2 + i if last else dve.snap(lap * 2 + i)
                        split(L, "ple", lap, i + 1, 1, 2 * P)
                        dve.wait_ge(p_add.sem, p_add.at(n - 1))
                        take(L, 4 * L + 3, "ple", lap, 2 * i, 0, i + 1, pgate[:, i, :])
                        if not (last and i == 1):
                            split(L, "ple", lap, i + 2, 0)
                        dve.wait_ge(p_sig.sem, p_sig.at(n))
                        dve.wait_ge(used[1].sem, used[1].at(SLOT.nth(L, "ple", lap, i + 1)))
                        dve.tensor_tensor(pprod[:, i, :], bank[2 * i + 1][:], pgate[:, i, :], ALU.mult).then_inc(read[2 * i + 1].sem, 1)
                        dve.wait_ge(read[2 * i + 1].sem, read[2 * i + 1].at(BANK[2 * i + 1].nth(L, "ple", lap)))
                        dve.tensor_tensor(x[:, m, :], x[:, m, :], pprod[:, i, :], ALU.add).then_inc(p_add.sem, 1)
                        gain = lc[:, NEXT_GAIN + m:NEXT_GAIN + m + 1] if last else lc[:, bass.ds(dve.snap(m + NEXT_GAIN), 1)]
                        prep(4 * L + 4, m, gain, fhi, flo)
                with dve.Fori(0, KD // 2 - 1) as lap:
                    ple_lap(lap, False)
                ple_lap(KD // 2 - 1, True)
            norm(4 * DEPTH)
            dve.wait_ge(n_rstd.sem, n_rstd.at(4 * DEPTH + 1))
            for m in range(KD):
                dve.scalar_tensor_tensor(fin[:, m, :], x[:, m, :], lc[:, NEXT_GAIN + m:NEXT_GAIN + m + 1], rstd[:],
                                         ALU.mult, ALU.mult).then_inc(out_new.sem, 1)
            for n in range(2 * TT):
                dve.wait_ge(turned.sem, DEPTH + KD + n + 1)
                dve.tensor_copy(fout[:, n // 2, (n % 2) * SEQ:(n % 2 + 1) * SEQ], bank[n % 6][:]).then_inc(out_copied.sem, 1)


_INS = ['x', 'p', 'ffn1_norm', 'ffn1_w_gate', 'ffn1_w_up', 'ffn1_w_down', 'mix_norm', 'w_in', 'attn_sinks',
        'rwkv_mu', 'rwkv_w0', 'rwkv_w_up', 'rwkv_a0', 'rwkv_a_up', 'rwkv_g_up', 'rwkv_k_k', 'rwkv_k_a', 'rwkv_r_k',
        'rwkv_ln_w', 'rwkv_ln_b', 'hgrn_lb', 'hgrn_norm', 'w_branch', 'w_o', 'ffn2_norm', 'ffn2_w_gate', 'ffn2_w_up',
        'ffn2_w_down', 'ple_norm', 'ple_w_gate', 'ple_w_proj', 'final_norm']


def kernel(**inputs):
    import concourse.bacc as _bacc
    from concourse.bass_utils import run_bass_kernel_spmd as _run

    nc = _bacc.Bacc("TRN2", target_bir_lowering=False, num_devices=1)
    arrays, args = {}, {}
    for name in _INS:
        a = np.ascontiguousarray(inputs[name])
        arrays[f"in_{name}_dram"] = a
        args[name] = nc.dram_tensor(f"in_{name}_dram", a.shape, mybir.dt.from_np(a.dtype), kind="ExternalInput").ap()
    out = nc.dram_tensor("out_0_dram", (1, SEQ, D), F32, kind="ExternalOutput").ap()
    build_trunk(nc, args, out)
    r = _run(nc, [arrays], core_ids=[0])
    return r.results[0]["out_0_dram"]
```

```python
from contextlib import ExitStack

import numpy as np
import concourse.bass as bass
from concourse import mybir

F32 = mybir.dt.float32
F32R = mybir.dt.float32r
I32 = mybir.dt.int32
ALU = mybir.AluOpType
ACT = mybir.ActivationFunctionType
AX = mybir.AxisListType

P = 128
SEQ = 512
D = 1024
DEPTH = 2
D_FF = 2816
PLE = 256
KD = D // P
TT = SEQ // P
HALF_TILES = (10, 12)
EPS = 1e-6

HD = 64
C = SEQ // HD
PAIRS = 4
Y_RAW = 6
LEVELS = 7
WIDTH = PAIRS * P
DECAY = float(np.exp(-0.5))
GN_EPS = 64e-5
MASKED = -1e30
LN_MIN = 2.0 ** -60

Z_Q, Z_K, Z_V = 0, 4, 5
Z_R, Z_RK, Z_RV, Z_WA, Z_G = 6, 10, 14, 18, 19
Z_HQ, Z_HF, Z_HI, Z_HO = 20, 24, 28, 32
Z_GATE, Z_TILES = 36, 60
Y_A, Y_B, Y_C = 0, 4, 8

W_BUF = KD * P


class Signal:

    def __init__(self, sem, ahead=1):
        self.sem, self.ahead = sem, ahead

    def at(self, n):
        return n + self.ahead


class Turns:

    def __init__(self, sections):
        self.base, self.per, self.total = {}, {}, 0
        for name, laps, uses in sections:
            self.base[name], self.per[name] = self.total, uses
            self.total += laps * uses

    def nth(self, layer, section, lap, k=1):
        return layer * self.total + lap * self.per[section] + (self.base[section] + k)


SECTIONS = [("f1a_up", HALF_TILES[0], 1, (1, 1)), ("f1a_down", 4, 2, (1, 1)), ("f1b_up", HALF_TILES[1], 1, (1, 1)), ("f1b_down", 4, 2, (1, 1)),
            ("in_ab", 10, 1, (1, 1)), ("in_c", 4, 2, (1, 1, 1, 1)), ("in_gates", 4, 3, (2, 2, 1, 1)),
            ("merge", 4, 3, (1, 1, 1, 1, 1, 1)), ("w_o", 4, 1, (1, 1)),
            ("f2a_up", HALF_TILES[0], 1, (1, 1)), ("f2a_down", 4, 2, (1, 1)), ("f2b_up", HALF_TILES[1], 1, (1, 1)), ("f2b_down", 4, 2, (1, 1)),
            ("ple", 4, 2, (1, 1, 1, 1))]
SLOT = Turns([(n, laps, u) for n, laps, u, _ in SECTIONS])
BANK = [Turns([(n, laps, (b[i] if i < len(b) else 0)) for n, laps, _, b in SECTIONS]) for i in range(6)]

STAGE = [Turns([(n, laps, b[i] if i < len(b) else 0) for n, laps, _, b in SECTIONS if n.startswith("in_")])
         for i in range(4)]

ROWS = [("ffn1_norm", 8), ("mix_norm", 8), ("ffn2_norm", 8), ("ple_norm", 8), ("rwkv_mu", 14), ("rwkv_w0", 4),
        ("rwkv_a0", 4), ("rwkv_k_k", 4), ("rwkv_k_a", 4), ("rwkv_r_k", 4), ("rwkv_ln_w", 4), ("rwkv_ln_b", 4),
        ("hgrn_lb", 4), ("hgrn_norm", 1)]
COL = {}
_at = 0
for _name, _n in ROWS:
    COL[_name] = _at
    _at += _n
LAYER_COLS = _at
NEXT_GAIN = LAYER_COLS


_LV = range(1, LEVELS - 1)
RW_PE = (["d", "a", "g", "kk_norm", "turn_v", "bonus", "turn_kq", "turn_bh", "turn_kh",
          "A1T_0", "A1T_1", "A1_0", "A1_1", "A2T_0", "A2T_1", "A2v"]
         + [f"{w}{l}_{h}" for l in _LV for w in "TX" for h in (0, 1)]
         + ["PG_0", "PG_1", "B1T_0", "B1T_1", "B2T_0", "B2T_1", "R2", "state_0", "state_1"]
         + [f"Z{c}" for c in range(2, C)] + ["y_0", "y_1", "mean", "var"])
RW_ACT = ["w", "a", "g", "lw_g", "kk_raw", "kk_sq", "kk_root", "dec", "inc", "kq0", "v_tok", "kq_tok", "b_tok", "k_tok",
          "A2v_tok", "PG_0", "PG_1", "NZ_0", "NZ_1", "bonus_b", "y_0", "y_sq", "y_sd"]
RW_POOL = ["a_inc", "kt", "rt", "ediag", "lora_wa", "lora_g", "XTm_0", "XTm_1", "X_0", "X_1", "XT_0", "XT_1",
           "bonus_g", "yg", "y"]
RW_DVE = (["dk", "k", "dr", "r", "dv", "v", "cs", "ka", "kp", "rk", "kmax", "krs", "kk", "b", "kq", "bh", "bonus", "kh",
           "NT_0", "NT_1", "X_0", "X_1", "A2T_0", "A2T_1"]
          + [f"{w}{l}_{h}" for l in _LV[:-1] for w in ("T", "XT", "X") for h in (0, 1)]
          + [f"{w}{LEVELS - 2}_{h}" for w in ("T", "XT") for h in (0, 1)]
          + ["B1T_0", "B1T_1", "B2T_0", "B2T_1", "R2", "M00", "M01", "M10", "MT"] + [f"Z{c}" for c in range(1, C)]
          + ["y_1", "yc", "yrs", "yn"])
HG_PE = (["scores_00", "scores_01", "scores_10", "scores_11", "probT_00", "probT_01", "probT_10", "probT_11", "hv", "att"]
         + [f"att{l}" for l in range(LEVELS + 1)] + ["hk", "dS", "o", "o_norm"])
HG_ACT = (["qs", "sig_f", "sig_q", "sig_o", "logf", "exp_0", "esink_0", "exp_1", "esink_1", "ex0", "ex1"]
          + ["probT_00", "probT_01", "probT_10", "probT_11", "hv_tok", "yatt"]
          + [f"ex{l}" for l in range(2, LEVELS - 2)] + ["eb", f"ex{LEVELS - 2}", f"ex{LEVELS - 1}", "ed", "hk_tok", "o", "o_sq", "o_sd"])
HG_POOL = ["kcur", "vcur", "key", "hq", "hog"] + [f"qk{l}" for l in range(LEVELS)] + ["kd"]
HG_DVE = (["fl", "f", "m0_0", "m1_0", "mx_0", "max_0", "bsum", "m0_1", "m1_1", "mx_1", "max_1", "d0", "d1"]
          + [f"{x}_{j}" for j in (0, 1) for x in ("den", "rec", "probs")]
          + [x for l in range(LEVELS) for x in (f"d{l + 2}" if l + 2 < LEVELS else ("qb", "dend")[l + 2 - LEVELS], f"att{l}")]
          + ["S1", f"att{LEVELS}", "S2", "S3", "orec", "on", "y"])
LY_DVE = ["zero", "mt_zero", "dwa", "wa", "dg", "g", "att_zero"]
LY_ACT = ["tanh", "sigmoid", "lora_wa", "lora_g", "k00", "k01", "k10", "k11", "v"]
LY_PE = ["v"]
MASK_STEPS = 53


def step(table, n, name):
    return n * len(table) + (table.index(name) + 1)


def pe_mark(ins, signal, table, name, order):
    order.append(name)
    return ins.then_inc(signal.sem, 1)


def build_trunk(nc, d, out):
    ctx = ExitStack()
    with ctx:
        def sb(name, shape, dt=F32, scope=ctx):
            return scope.enter_context(nc.sbuf_tensor(name, shape, dt))

        def signal(name, ahead=1):
            return Signal(ctx.enter_context(nc.semaphore(name)), ahead)

        def dma_signal(name):
            return ctx.enter_context(nc.semaphore(name))

        x = sb("x", [P, KD, SEQ])
        ghi = sb("ghi", [P, KD, SEQ], F32R)
        glo = sb("glo", [P, KD, SEQ], F32R)
        wraw = sb("wraw", [P, 2, W_BUF])
        whi = sb("whi", [P, 2, W_BUF], F32R)
        wlo = sb("wlo", [P, 2, W_BUF], F32R)
        ident = sb("ident", [P, P])
        ones = sb("ones", [P, P])
        rows = sb("rows", [P, DEPTH, P])
        cols = sb("cols", [P, DEPTH * LAYER_COLS + 8])
        lc = sb("lc", [P, LAYER_COLS + 8])
        xsq = sb("xsq", [P, 2, SEQ])
        ssum = sb("ssum", [P, SEQ])
        eps_col = sb("eps_col", [P, 1])
        zero = sb("zero", [P, 1])
        table_set = sb("table_set", [P, 1])
        rstd = sb("rstd", [P, SEQ])

        low = sb("low", [P, LEVELS - 1, P])
        up0 = sb("up0", [P, P])
        before = sb("before", [P, P])
        upto = sb("upto", [P, P])
        pair_mask = sb("pair_mask", [P, LEVELS + 1, P], I32)
        band = sb("band", [P, 4, P])
        seg64 = sb("seg64", [P, SEQ])
        seg128 = sb("seg128", [P, SEQ])
        head_ones = sb("head_ones", [P, P])
        eye64 = sb("eye64", [P, HD])
        sinks = sb("sinks", [P, DEPTH * 8])
        lb = sb("lb", [P, DEPTH * PAIRS])
        lb_rest = sb("lb_rest", [P, DEPTH * PAIRS])
        gn_eps = sb("gn_eps", [P, 1])

        rw = ExitStack()
        stage = sb("stage", [P, 4, SEQ], F32, rw)
        zr = sb("zr", [P, 3, SEQ + 1], F32, rw)
        lora_wa = sb("lora_wa", [P, WIDTH + P], F32, rw)
        lora_g = sb("lora_g", [P, WIDTH + P], F32, rw)
        xwa = sb("xwa", [P, SEQ], F32, rw)
        xgs = sb("xgs", [P, SEQ], F32, rw)
        lwa = sb("lwa", [P, P], F32, rw)
        lg = sb("lg", [P, P], F32, rw)
        shift = sb("shift", [P, SEQ], F32, rw)
        r_ = sb("r", [P, SEQ], F32, rw)
        k_ = sb("k", [P, SEQ], F32, rw)
        v_ = sb("v", [P, SEQ], F32, rw)
        w_ = sb("w", [P, SEQ], F32, rw)
        a_ = sb("a", [P, SEQ], F32, rw)
        g_ = sb("g", [P, SEQ], F32, rw)
        lw_g = sb("lw_g", [P, SEQ], F32, rw)
        cs = sb("cs", [P, SEQ], F32, rw)
        dec = sb("dec", [P, SEQ], F32, rw)
        inc = sb("inc", [P, SEQ], F32, rw)
        kk = sb("kk", [P, SEQ], F32, rw)
        tmp = sb("tmp", [P, SEQ], F32, rw)
        kp = sb("kp", [P, SEQ], F32, rw)
        bb = sb("bb", [P, SEQ], F32, rw)
        kq = sb("kq", [P, SEQ], F32, rw)
        rk = sb("rk", [P, SEQ], F32, rw)
        bh = sb("bh", [P, SEQ], F32, rw)
        kh = sb("kh", [P, SEQ], F32, rw)
        bonus = sb("bonus", [P, SEQ], F32, rw)
        v_tok = sb("v_tok", [P, TT, P], F32, rw)
        b_tok = sb("b_tok", [P, TT, P], F32, rw)
        k_tok = sb("k_tok", [P, TT, P], F32, rw)
        rhs = sb("rhs", [P, TT, 2, 2, HD], F32, rw)
        NT = sb("NT", [P, 2, TT, P], F32, rw)
        X = sb("X", [P, 2, TT, P], F32, rw)
        XT = sb("XT", [P, 2, TT, P], F32, rw)
        T1 = sb("T1", [P, 2, TT, P], F32, rw)
        PG = sb("PG", [P, 2, TT, P], F32, rw)
        MT = sb("MT", [P, C, P], F32, rw)
        ediag = sb("ediag", [P, C, HD], F32, rw)
        NZ = sb("NZ", [P, C, HD], F32, rw)
        Z = sb("Z", [P, C, HD], F32, rw)
        rw.close()
        y_ = cs

        hg = ExitStack()
        sb("stage_again", [P, 4, SEQ], F32, hg)
        kvraw = sb("kvraw", [P, 2, SEQ], F32, hg)
        krep = sb("krep", [P, 2, SEQ], F32, hg)
        vtok2 = sb("vtok2", [P, 2, TT, HD], F32, hg)
        kcur = sb("kcur", [P, SEQ], F32, hg)
        vcur = sb("vcur", [P, TT, HD], F32, hg)
        zq = sb("zq", [P, SEQ], F32, hg)
        qs = sb("qs", [P, SEQ], F32, hg)
        sc = sb("sc", [P, 2, TT, 2 * P], F32, hg)
        pT_ = sb("probT", [P, 2, TT, 2, P], F32, hg)
        small = sb("small", [P, 2, 6, TT], F32, hg)
        yatt = sb("yatt", [P, SEQ], F32, hg)
        hz = sb("hz", [P, 4, SEQ], F32, hg)
        fg = sb("fg", [P, SEQ], F32, hg)
        logf = sb("logf", [P, SEQ], F32, hg)
        key = sb("key", [P, SEQ], F32, hg)
        bsum = sb("bsum", [P, SEQ], F32, hg)
        hq = sb("hq", [P, SEQ], F32, hg)
        hog = sb("hog", [P, SEQ], F32, hg)
        dd = sb("dd", [P, 2, SEQ], F32, hg)
        ex = sb("ex", [P, 2, SEQ], F32, hg)
        qk = sb("qk", [P, 2, SEQ], F32, hg)
        attT = sb("attT", [P, TT, P], F32, hg)
        qb = sb("qb", [P, SEQ], F32, hg)
        hv_tok = sb("hv_tok", [P, TT, P], F32, hg)
        hk_tok = sb("hk_tok", [P, TT, P], F32, hg)
        S = sb("S", [P, TT, P], F32, hg)
        ho = sb("ho", [P, SEQ], F32, hg)
        hsq = sb("hsq", [P, SEQ], F32, hg)
        hg.close()

        mg = ExitStack()
        yhi = sb("yhi", [P, 12, SEQ], F32R, mg)
        ylo = sb("ylo", [P, 12, SEQ], F32R, mg)
        gates = sb("gates", [P, 2, 3, SEQ], F32, mg)
        mhi = sb("mhi", [P, KD, SEQ], F32R, mg)
        mlo = sb("mlo", [P, KD, SEQ], F32R, mg)
        acc = sb("acc", [P, 2, SEQ], F32, mg)
        yraw = sb("yraw", [P, Y_RAW, SEQ], F32, mg)
        mg.close()

        ffn = ExitStack()
        fhi = sb("fhi", [P, KD, SEQ], F32R, ffn)
        flo = sb("flo", [P, KD, SEQ], F32R, ffn)
        ple_scope = ExitStack()
        praw = sb("praw", [P, TT, PLE], F32, ple_scope)
        pT = sb("pT", [P, 2, SEQ], F32, ple_scope)
        phi = sb("phi", [P, 2, SEQ], F32R, ple_scope)
        plo = sb("plo", [P, 2, SEQ], F32R, ple_scope)
        pgate = sb("pgate", [P, 2, SEQ], F32, ple_scope)
        pprod = sb("pprod", [P, 2, SEQ], F32, ple_scope)
        ple_scope.close()
        hhi = sb("hhi", [P, max(HALF_TILES), SEQ], F32R, ffn)
        hlo = sb("hlo", [P, max(HALF_TILES), SEQ], F32R, ffn)
        gate_in = sb("gate_in", [P, SEQ], F32, ffn)
        gate_sig = sb("gate_sig", [P, SEQ], F32, ffn)
        gate_act = sb("gate_act", [P, SEQ], F32, ffn)
        up = sb("up", [P, SEQ], F32, ffn)
        h = sb("h", [P, SEQ], F32, ffn)
        ffn.close()
        ends = ExitStack()
        sb("fhi_flo_again", [P, 2 * KD, SEQ], F32, ends)
        xin = sb("xin", [P, TT, D], F32, ends)
        fin = sb("fin", [P, KD, SEQ], F32, ends)
        fout = sb("fout", [P, TT, D], F32, ends)
        ends.close()

        zd = nc.dram_tensor("z_scratch", (Z_TILES, P, SEQ), F32, kind="Internal").ap()
        yd = nc.dram_tensor("y_scratch", (12, P, SEQ), F32, kind="Internal").ap()
        primer = nc.dram_tensor("primer_scratch", (7, P, P), F32, kind="Internal").ap()

        bank = [ctx.enter_context(nc.psum_tensor(f"bank{i}", [P, SEQ], F32)) for i in range(8)]

        landed = [dma_signal(f"chunk_landed{s}") for s in (0, 1)]
        w_hi = [signal(f"chunk_hi{s}") for s in (0, 1)]
        w_lo = [signal(f"chunk_lo{s}") for s in (0, 1)]
        used = [signal(f"chunk_used{s}") for s in (0, 1)]
        read = [signal(f"bank_read{i}") for i in range(6)]
        rows_in = dma_signal("rows_in")
        x_in = dma_signal("x_in")
        p_in = dma_signal("p_in")
        stored = dma_signal("stored")
        const = signal("constants", 0)
        turned = signal("transposes_done", 0)
        cols_ready = signal("cols_ready", 0)
        lc_ready = signal("layer_cols_ready", 0)
        x_new = signal("x_tile_loaded", 0)
        g_hi = signal("x_gain_hi")
        g_sq = signal("x_square")
        g_lo = signal("x_gain_lo")
        g_sum = signal("squares_summed", 2)
        n_sum = signal("norm_sum")
        n_rms = signal("norm_rms")
        n_rstd = signal("norm_rstd")
        f_sig = signal("gate_sigmoid")
        f_act = signal("gate_silu")
        f_h = signal("hidden")
        f_hi = signal("hidden_hi")
        f_lo = signal("hidden_lo")
        p_turned = signal("p_turned")
        p_copied = signal("p_copied")
        p_hi = signal("p_hi")
        p_lo = signal("p_lo")
        p_sig = signal("ple_sigmoid")
        p_add = signal("ple_added")
        stage_out = [dma_signal(f"stage{i}_out") for i in range(4)]
        lora_in = dma_signal("lora_in")
        wag_in = dma_signal("wag_in")
        rkv_in = dma_signal("rkv_in")
        kv_in = dma_signal("kv_in")
        hz_in = dma_signal("hz_in")
        zq_in = dma_signal("zq_in")
        ya_out, yb_out, yc_out = dma_signal("ya_out"), dma_signal("yb_out"), dma_signal("yc_out")
        acc_step = signal("branch_sum_step")
        y_in = [dma_signal(f"y_in{i}") for i in range(Y_RAW)]
        gates_in = [dma_signal(f"gates_in{i}") for i in (0, 1)]
        sinks_in = dma_signal("sinks_in")
        lb_step = signal("lb_step", 0)
        lb_sig = signal("lb_sigmoid", 0)
        masks = signal("masks", 0)
        w_pe = signal("rwkv_products", len(RW_PE))
        w_act = signal("rwkv_scalar", len(RW_ACT))
        w_pool = signal("rwkv_pool", len(RW_POOL))
        w_dve = signal("rwkv_vector", len(RW_DVE))
        h_pe = signal("hgrn_products", len(HG_PE))
        h_act = signal("hgrn_scalar", len(HG_ACT))
        h_pool = signal("hgrn_pool", len(HG_POOL))
        h_dve = signal("hgrn_vector", len(HG_DVE))
        l_dve = signal("layer_vector", len(LY_DVE))
        l_act = signal("layer_scalar", len(LY_ACT))
        l_pe = signal("layer_products", len(LY_PE))
        m_hi = signal("y_hi")
        m_lo = signal("y_lo")
        m_lo_a = signal("y_lo_attention")
        m_sig = signal("gates_sigmoid")
        m_sum = signal("merged")
        m_mhi = signal("merged_hi")
        m_mlo = signal("merged_lo")
        sum_clear = signal("ssum_cleared", 0)
        eps_set = signal("eps_set", 0)
        zero_set = signal("zero_set", 0)
        col_copy = signal("cols_copied", 0)
        lc_copied = signal("layer_cols_copied", 0)
        out_new = signal("out_tile", 0)
        out_copied = signal("out_copied", 0)

        def kview(w, k0, nk):
            return w[k0 * P:(k0 + nk) * P, :].rearrange("(k p) n -> p k n", p=P)

        block = ctx.enter_context(nc.Block())

        @block.sync
        def _(sp):
            for L in range(DEPTH):
                for name, n in ROWS:
                    src = d[name][L] if name != "rwkv_r_k" else d[name][L].rearrange("h k -> (h k)")
                    sp.dma_start(rows[COL[name]:COL[name] + n, L, :],
                                 src.rearrange("(r c) -> r c", c=P)).then_inc(rows_in, 16)
                sp.dma_start(rows[LAYER_COLS:LAYER_COLS + 8, L, :],
                             d["final_norm"].rearrange("(r c) -> r c", c=P)).then_inc(rows_in, 16)
            sp.dma_start(sinks[:], d["attn_sinks"].rearrange("l h -> (l h)").partition_broadcast(P)).then_inc(sinks_in, 16)
            sp.dma_start(xin[:], d["x"][0].rearrange("(t p) c -> p t c", p=P)).then_inc(x_in, 16)

            def load(L, section, lap, k, slot, src, n):
                use = SLOT.nth(L, section, lap, k)
                dst = wraw[:, slot, 0:n].rearrange("p (k c) -> p k c", c=P)
                before = sp.snap(w_lo[slot].at(use - 1))
                sp.wait_ge(w_lo[slot].sem, before)
                sp.dma_start(dst, src).then_inc(landed[slot], 16)

            def ffn_loads(L, f):
                tile0 = 0
                for half, tiles in zip("ab", HALF_TILES):
                    with sp.Fori(0, tiles) as j:
                        cols_j = bass.ds(sp.snap(j * P + tile0 * P), P)
                        load(L, f"f{f}{half}_up", j, 1, 0, kview(d[f"ffn{f}_w_gate"][L], 0, KD)[:, :, cols_j], W_BUF)
                        load(L, f"f{f}{half}_up", j, 1, 1, kview(d[f"ffn{f}_w_up"][L], 0, KD)[:, :, cols_j], W_BUF)
                    nk = tiles // 2
                    with sp.Fori(0, KD // 2) as lap:
                        for i in range(2):
                            cols_m = bass.ds(sp.snap(lap * (2 * P) + i * P), P)
                            for s in (0, 1):
                                load(L, f"f{f}{half}_down", lap, i + 1, s,
                                     kview(d[f"ffn{f}_w_down"][L], tile0 + s * nk, nk)[:, :, cols_m], nk * P)
                    tile0 += tiles

            def mixer_loads(L):
                win = kview(d["w_in"][L], 0, KD)

                def in_tile(section, lap, q, tile):
                    load(L, section, lap, q // 2 + 1, q % 2, win[:, :, bass.ds(tile * P if isinstance(tile, int) else sp.snap(tile * P), P)], W_BUF)

                for q in range(2):
                    in_tile("in_ab", 0, q, Z_WA + q)
                with sp.Fori(1, 10) as lap:
                    for q in range(2):
                        in_tile("in_ab", lap, q, lap * 2 + (q - 2))
                sp.wait_ge(used[1].sem, used[1].at(SLOT.nth(L, "f1b_down", 3, 2)))
                for dst, src in ((lora_wa[0:64, :], d["rwkv_w_up"]), (lora_wa[64:P, :], d["rwkv_a_up"]), (lora_g[:], d["rwkv_g_up"])):
                    sp.dma_start(dst[:, 0:WIDTH], src[L]).then_inc(lora_in, 16)
                    sp.dma_start(dst[:, WIDTH:WIDTH + P], src[L][:, 0:P]).then_inc(lora_in, 16)

                def in_c(lap, chunks):
                    for q in chunks:
                        in_tile("in_c", lap, q, lap * 4 + (Z_HQ + q))

                def in_gates(lap, chunks):
                    for q in chunks:
                        in_tile("in_gates", lap, q, lap * 6 + (Z_GATE + q))

                def merge(lap, chunks):
                    for q in chunks:
                        first = (q // 3) * P
                        cols_m = slice(first, first + P) if isinstance(lap, int) else bass.ds(sp.snap(lap * (2 * P) + first), P)
                        load(L, "merge", lap, q // 2 + 1, q % 2, kview(d["w_branch"][L, q % 3], 0, PAIRS)[:, :, cols_m], PAIRS * P)

                def fetch(dst, tile, sem):
                    tile = tile if isinstance(tile, int) else sp.snap(tile)
                    sp.dma_start(dst, zd[bass.ds(tile, 1), :, :].rearrange("a p c -> p (a c)")).then_inc(sem, 16)

                def next_pair(lap):
                    sp.wait_ge(w_dve.sem, w_dve.at(step(RW_DVE, sp.snap(L * PAIRS + lap), "v")))
                    for i, z0 in enumerate((Z_R, Z_RK, Z_RV)):
                        fetch(zr[:, i, 1:SEQ + 1], lap + (z0 + 1), rkv_in)

                def next_head(lap):
                    n = sp.snap(L * PAIRS + lap)
                    for sig, table, name in ((h_act, HG_ACT, "sig_o"), (h_pool, HG_POOL, "hog"), (h_pe, HG_PE, "hv")):
                        sp.wait_ge(sig.sem, sig.at(step(table, n, name)))
                    for i, z0 in enumerate((Z_HQ, Z_HF, Z_HI, Z_HO)):
                        fetch(hz[:, i, :], lap + (z0 + 1), hz_in)
                    fetch(zq[:], lap + (Z_Q + 1), zq_in)
                    sp.wait_ge(h_act.sem, h_act.at(step(HG_ACT, n, "yatt")))
                    tile = lap + Y_A if isinstance(lap, int) else sp.snap(lap + Y_A)
                    sp.dma_start(yd[bass.ds(tile, 1), :, :].rearrange("a p c -> p (a c)"), yatt[:]).then_inc(ya_out, 16)

                def store_y(tile, lap, src, sig, table, sem):
                    sp.wait_ge(sig.sem, sig.at(step(table, sp.snap(L * PAIRS + lap), "y")))
                    tile = tile + lap if isinstance(lap, int) else sp.snap(lap + tile)
                    sp.dma_start(yd[bass.ds(tile, 1), :, :].rearrange("a p c -> p (a c)"), src).then_inc(sem, 16)

                in_c(0, (0, 1))
                with sp.Fori(0, PAIRS - 1) as lap:
                    in_c(lap, (2,))
                    next_pair(lap)
                    in_c(lap, (3,))
                    in_c(sp.snap(lap + 1), (0, 1))
                    store_y(Y_B, lap, y_[:], w_pool, RW_POOL, yb_out)
                in_c(PAIRS - 1, (2,))
                next_pair(PAIRS - 1)
                pairs_in = sp.snap(48 * (5 * L) + 5 * 48)
                gate_used = sp.snap(w_pe.at(step(RW_PE, 4 * L + 3, "g")))
                sent = [sp.snap(16 * STAGE[b].nth(L, "in_c", 3) + 16) for b in range(4)]
                sp.wait_ge(rkv_in, pairs_in)
                fetch(kvraw[:, 0, :], Z_K, kv_in)
                fetch(kvraw[:, 1, :], Z_V, kv_in)
                sp.wait_ge(w_pe.sem, gate_used)
                fetch(zq[:], Z_Q, zq_in)
                in_c(PAIRS - 1, (3,))
                in_gates(0, (0, 1))
                store_y(Y_B, PAIRS - 1, y_[:], w_pool, RW_POOL, yb_out)
                for b in range(4):
                    sp.wait_ge(stage_out[b], sent[b])
                for i, z0 in enumerate((Z_HQ, Z_HF, Z_HI, Z_HO)):
                    fetch(hz[:, i, :], z0, hz_in)
                with sp.Fori(0, PAIRS - 1) as lap:
                    in_gates(lap, (2, 3, 4))
                    next_head(lap)
                    in_gates(lap, (5,))
                    in_gates(sp.snap(lap + 1), (0, 1))
                    store_y(Y_C, lap, ho[:], h_dve, HG_DVE, yc_out)
                in_gates(PAIRS - 1, (2, 3, 4))
                next_head(PAIRS - 1)
                in_gates(PAIRS - 1, (5,))
                merge(0, (0, 1))

                def load_y(tile, after=None):
                    i = tile % Y_RAW
                    if tile >= Y_RAW:
                        sig, n = (m_lo_a, 4 * L + (i + 1)) if i < PAIRS else (m_lo, 8 * L + (i + 1 - PAIRS))
                        is_split = sp.snap(sig.at(n))
                        sp.wait_ge(sig.sem, is_split)
                    if after is not None:
                        sp.wait_ge(after, all_out)
                    sp.dma_start(yraw[:, i, :], yd[tile]).then_inc(y_in[i], 16)

                all_out = sp.snap(16 * (4 * L) + (64 + 16))
                heads_in = sp.snap(64 * (5 * L) + 5 * 64)
                sp.wait_ge(hz_in, heads_in)
                for sem in (ya_out, yb_out):
                    sp.wait_ge(sem, all_out)
                for tile in range(Y_RAW):
                    load_y(tile)
                sent = [sp.snap(16 * STAGE[b].nth(L, "in_gates", 3, 2 if b < 2 else 1) + 16) for b in range(4)]
                for sig, table, name in ((h_pe, HG_PE, "o"), (h_dve, HG_DVE, "S3")):
                    sp.wait_ge(sig.sem, sig.at(step(table, 4 * L + 3, name)))
                for b in range(4):
                    sp.wait_ge(stage_out[b], sent[b])
                for m in range(2):
                    sp.dma_start(gates[:, m, :, :], zd[Z_GATE:Z_TILES, :, :].rearrange("(b m) p c -> p m b c", b=3)[:, m])\
                      .then_inc(gates_in[m], 16)
                store_y(Y_C, PAIRS - 1, ho[:], h_dve, HG_DVE, yc_out)
                load_y(6)
                load_y(7)
                merge(0, (2,))
                load_y(8, yc_out)
                for tile in range(9, 12):
                    load_y(tile)
                merge(0, (3, 4, 5))
                with sp.Fori(1, KD // 2) as lap:
                    merge(lap, range(6))
                with sp.Fori(0, KD // 2) as lap:
                    for q in range(2):
                        cols_m = bass.ds(sp.snap(lap * (2 * P) + q * P), P)
                        load(L, "w_o", lap, 1, q, kview(d["w_o"][L], 0, KD)[:, :, cols_m], W_BUF)

            with sp.Fori(0, DEPTH) as L:
                ffn_loads(L, 1)
                mixer_loads(L)
                ffn_loads(L, 2)
                sp.wait_ge(used[1].sem, used[1].at(SLOT.nth(L, "f2b_down", 3, 2)))
                sp.dma_start(praw[:], d["p"][L, 0].rearrange("(t p) c -> p t c", p=P)).then_inc(p_in, 16)
                with sp.Fori(0, KD // 2) as lap:
                    for i in range(2):
                        cols_m = bass.ds(sp.snap(lap * (2 * P) + i * P), P)
                        load(L, "ple", lap, i + 1, 0, kview(d["ple_w_gate"][L], 0, KD)[:, :, cols_m], W_BUF)
                        load(L, "ple", lap, i + 1, 1, kview(d["ple_w_proj"][L], 0, 2)[:, :, cols_m], 2 * P)

            for t in range(TT):
                sp.wait_ge(out_copied.sem, 2 * t + 2)
                sp.dma_start(out[0, t * P:(t + 1) * P, :], fout[:, t, :]).then_inc(stored, 16)
            sp.wait_ge(stored, 16 * TT)

        @block.tensor
        def _(pe):
            for s in (*used, n_sum, p_turned, w_pe, h_pe, l_pe):
                pe.sem_inc(s.sem, s.ahead)
            pe.wait_ge(const.sem, 3)
            pe.wait_ge(rows_in, 16 * DEPTH * (len(ROWS) + 1))
            for L in range(DEPTH):
                pe.transpose(bank[6][:, L * P:L * P + LAYER_COLS + 8], rows[0:LAYER_COLS + 8, L, :],
                             ident[0:LAYER_COLS + 8, 0:LAYER_COLS + 8]).then_inc(turned.sem, 1)
            pe.wait_ge(x_in, 16)
            for m in range(KD):
                if m >= 2:
                    pe.wait_ge(x_new.sem, m - 1)
                for t in range(TT):
                    mm = pe.transpose(bank[m % 2][:, t * P:(t + 1) * P], xin[:, t, m * P:(m + 1) * P], ident[:])
                mm.then_inc(turned.sem, 1)

            def norm(e):
                pe.wait_ge(g_sum.sem, g_sum.at(8 * e + 8))
                pe.wait_ge(n_rms.sem, n_rms.at(e))
                pe.matmul(bank[7][:], ones[:], ssum[:], start=True, stop=True).then_inc(n_sum.sem, 1)

            def chunk(L, section, lap, k, slot, nk, hi, lo, k0, b, first, last, between=None, event=None,
                      span=None):
                use = SLOT.nth(L, section, lap, k)
                k_from, k_to = span or (0, nk)
                if k_from == 0:
                    pe.wait_ge(w_lo[slot].sem, w_lo[slot].at(use))
                for i in range(k_from, k_to):
                    if event is not None:
                        pe.wait_ge(g_lo.sem, g_lo.at(8 * event + i + 1))
                    wh = whi[:, slot, i * P:(i + 1) * P]
                    wl = wlo[:, slot, i * P:(i + 1) * P]
                    pe.matmul(bank[b][:], wh, hi[:, k0 + i, :], start=first and i == 0, stop=False)
                    pe.matmul(bank[b][:], wh, lo[:, k0 + i, :], start=False, stop=False)
                    mm = pe.matmul(bank[b][:], wl, hi[:, k0 + i, :], start=False, stop=last and i == nk - 1)
                    if between is not None and i < nk - 1:
                        between(i - k_from)
                if k_to == nk:
                    mm.then_inc(used[slot].sem, 1)

            def bank_free(L, section, lap, b, k=1):
                pe.wait_ge(read[b].sem, read[b].at(BANK[b].nth(L, section, lap, k) - 1))

            def ffn(L, f, event, hi, lo):
                done = L * (2 * sum(HALF_TILES)) + (f - 1) * sum(HALF_TILES)
                for half, tiles in zip("ab", HALF_TILES):
                    def up_lap(j, first):
                        for s in (0, 1):
                            bank_free(L, f"f{f}{half}_up", j, s)
                            chunk(L, f"f{f}{half}_up", j, 1, s, KD, hi, lo, 0, s, True, True,
                                  event=event if first and s == 0 else None)
                            if first and s == 0:
                                norm(event)
                    if half == "a":
                        up_lap(0, True)
                    with pe.Fori(1 if half == "a" else 0, tiles) as j:
                        up_lap(j, False)
                    nk = tiles // 2
                    with pe.Fori(0, KD // 2) as lap:
                        for i in range(2):
                            bank_free(L, f"f{f}{half}_down", lap, i)
                            for s in (0, 1):
                                pe.wait_ge(f_lo.sem, f_lo.at(done + (s + 1) * nk))
                                chunk(L, f"f{f}{half}_down", lap, i + 1, s, nk, hhi, hlo, s * nk, i, s == 0, s == 1)
                    done = done + tiles

            def in_tile(L, section, lap, q, b, k=1, between=None, event=None, span=None):
                if span is None or span[0] == 0:
                    bank_free(L, section, lap, b, k)
                chunk(L, section, lap, q // 2 + 1, q % 2, KD, ghi, glo, 0, b, True, True, between, event, span)

            def rwkv_lap(L, lap):
                n = pe.snap(L * PAIRS + lap)
                done = lambda ins, name: pe_mark(ins, w_pe, RW_PE, name, order)
                order = []
                G = lambda q, k0, k1, between=None: in_tile(L, "in_c", lap, q, q, 1, between, None, (k0, k1))
                W = lambda sig, table, name: pe.wait_ge(sig.sem, sig.at(step(table, n, name)))

                def turn(src, b, name):
                    for t in range(TT):
                        mm = pe.transpose(bank[b][:, t * P:(t + 1) * P], src[:, t * P:(t + 1) * P], ident[:])
                    done(mm, "turn_" + name)

                G(0, 0, 6)
                pe.wait_ge(l_act.sem, l_act.at(step(LY_ACT, L, "lora_g")))
                pe.wait_ge(w_pool.sem, w_pool.at(step(RW_POOL, n - 1, "lora_g")))
                pe.wait_ge(w_dve.sem, w_dve.at(step(RW_DVE, n - 1, "yc")))
                pe.wait_ge(w_act.sem, w_act.at(step(RW_ACT, n - 1, "y_sd")))
                for b, w, x_, name in ((4, lwa[0:64, :], xwa[0:64, :], "d"), (5, lwa[64:P, :], xwa[64:P, :], "a"),
                                       (6, lg[:], xgs[:], "g")):
                    done(pe.matmul(bank[b][:], w, x_, start=True, stop=True), name)
                G(0, 6, 8)
                W(w_act, RW_ACT, "kk_sq")
                done(pe.matmul(bank[4][:], head_ones[:], tmp[:], start=True, stop=True), "kk_norm")
                G(1, 0, 4)
                W(w_dve, RW_DVE, "rk")
                turn(v_, 6, "v")
                done(pe.matmul(bank[5][:], head_ones[:], rk[:], start=True, stop=True), "bonus")
                G(1, 4, 8)
                G(2, 0, 2)
                W(w_act, RW_ACT, "kq0")
                W(w_dve, RW_DVE, "kq")
                turn(kq, 7, "kq")
                W(w_dve, RW_DVE, "bh")
                turn(bh, 4, "bh")
                W(w_dve, RW_DVE, "kh")
                turn(kh, 5, "kh")

                def gram(l_, r__, b, h):
                    for t in range(TT):
                        mm = pe.matmul(bank[b][:, t * P:(t + 1) * P], l_[h * 64:h * 64 + 64, t * P:(t + 1) * P],
                                       r__[h * 64:h * 64 + 64, t * P:(t + 1) * P], start=True, stop=True)
                    return mm

                W(w_act, RW_ACT, "v_tok")
                done(gram(bb, kq, 6, 0), "A1T_0")
                W(w_act, RW_ACT, "kq_tok")
                done(gram(bb, kq, 7, 1), "A1T_1")
                W(w_act, RW_ACT, "b_tok")
                done(gram(kq, bb, 4, 0), "A1_0")
                W(w_act, RW_ACT, "k_tok")
                done(gram(kq, bb, 5, 1), "A1_1")
                W(w_pool, RW_POOL, "kt")
                W(w_dve, RW_DVE, "NT_0")
                done(gram(kp, kq, 6, 0), "A2T_0")
                W(w_dve, RW_DVE, "NT_1")
                done(gram(kp, kq, 7, 1), "A2T_1")
                G(2, 2, 3)
                W(w_dve, RW_DVE, "A2T_1")
                W(w_dve, RW_DVE, "X_1")
                for h in range(2):
                    for t in range(TT):
                        c0 = (h * TT + t) * HD
                        mm = pe.matmul(bank[4][:, c0:c0 + HD], T1[:, h, t, :], v_tok[:, t, h * HD:(h + 1) * HD],
                                       start=True, stop=True)
                done(mm, "A2v")
                fill = {2: (2, 3, 5), 3: (2, 5, 7), 4: (2, 7, 8), 5: (3, 0, 1)}
                for l in range(1, LEVELS - 1):
                    if l in fill:
                        G(*fill[l])
                    for h in range(2):
                        if l == 1:
                            W(w_act, RW_ACT, "A2v_tok")
                            W(w_pool, RW_POOL, "XT_1")
                        if l > 1:
                            W(w_dve, RW_DVE, f"X{l - 1}_{h}")
                        for t in range(TT):
                            mm = pe.matmul(bank[4 + h][:, t * P:(t + 1) * P], NT[:, h, t, :], X[:, h, t, :], start=True, stop=True)
                        done(mm, f"T{l}_{h}")
                    for h in range(2):
                        W(w_dve, RW_DVE, f"T{l}_{h}")
                        for t in range(TT):
                            mm = pe.matmul(bank[6 + h][:, t * P:(t + 1) * P], T1[:, h, t, :], XT[:, h, t, :], start=True, stop=True)
                        if l < LEVELS - 2:
                            for t in range(TT):
                                mm = pe.matmul(bank[4 + h][:, t * P:(t + 1) * P], XT[:, h, t, :], T1[:, h, t, :], start=True, stop=True)
                        done(mm, f"X{l}_{h}")
                for h in range(2):
                    W(w_dve, RW_DVE, f"XT{LEVELS - 2}_{h}")
                    for t in range(TT):
                        mm = pe.matmul(bank[4 + h][:, t * P:(t + 1) * P], XT[:, h, t, :],
                                       rhs[:, t, h, :, :].rearrange("p a c -> p (a c)"), start=True, stop=True)
                    done(mm, f"PG_{h}")
                W(w_pool, RW_POOL, "rt")
                for h in range(2):
                    done(gram(bb, r_, 6 + h, h), f"B1T_{h}")
                for h in range(2):
                    W(w_act, RW_ACT, f"PG_{h}")
                    done(gram(kp, r_, 4 + h, h), f"B2T_{h}")
                W(w_dve, RW_DVE, "B1T_1")
                W(w_dve, RW_DVE, "B2T_0")
                for h in range(2):
                    for t in range(TT):
                        mm = pe.matmul(bank[6][h * HD:(h + 1) * HD, t * P:(t + 1) * P], PG[:, h, t, 0:HD], NT[:, h, t, :],
                                       start=True, stop=True)
                done(mm, "R2")
                for par in range(2):
                    b = bank[7] if par == 0 else bank[4]
                    tok = slice(par * 64, par * 64 + 64)
                    for h in range(2):
                        hc = slice(h * HD, (h + 1) * HD)
                        for t in range(TT):
                            pe.matmul(b[hc, t * HD:(t + 1) * HD], PG[tok, h, t, 0:HD], b_tok[tok, t, hc], start=True, stop=True)
                            o = b[hc, (TT + t) * HD:(TT + t + 1) * HD]
                            pe.matmul(o, k_tok[tok, t, hc], v_tok[tok, t, hc], start=True, stop=False)
                            mm = pe.matmul(o, b_tok[tok, t, hc], PG[tok, h, t, HD:P], start=False, stop=True)
                    done(mm, f"state_{par}")

                W(w_dve, RW_DVE, "B2T_1")
                W(w_dve, RW_DVE, "MT")

                def state_step(i):
                    c = i + 1
                    if c <= C - 2:
                        W(w_dve, RW_DVE, f"Z{c}")
                        done(pe.matmul(bank[5][:, c * HD:(c + 1) * HD], MT[:, c, :], Z[:, c, :], start=True, stop=True), f"Z{c + 1}")
                G(3, 1, 8, state_step)
                W(w_dve, RW_DVE, f"Z{C - 1}")
                W(w_dve, RW_DVE, "R2")
                for h, b in ((0, bank[6]), (1, bank[4])):
                    hc = slice(h * HD, (h + 1) * HD)
                    for t in range(TT):
                        o = b[hc, t * P:(t + 1) * P]
                        pe.matmul(o, v_tok[:, t, hc], X[:, h, t, :], start=True, stop=False)
                        for c in (2 * t, 2 * t + 1):
                            if c:
                                pe.matmul(b[hc, c * HD:(c + 1) * HD], Z[hc, c, :], r_[hc, c * HD:(c + 1) * HD],
                                          start=False, stop=False)
                        mm = pe.matmul(o, PG[:, h, t, HD:P], NT[:, h, t, :], start=False, stop=True)
                    done(mm, f"y_{h}")
                W(w_dve, RW_DVE, "y_1")
                W(w_act, RW_ACT, "y_0")
                done(pe.matmul(bank[5][:], head_ones[:], y_[:], start=True, stop=True), "mean")
                W(w_act, RW_ACT, "y_sq")
                done(pe.matmul(bank[6][:], head_ones[:], tmp[:], start=True, stop=True), "var")
                assert order == RW_PE, order

            def hgrn_lap(L, lap):
                n = pe.snap(L * PAIRS + lap)
                order = []
                done = lambda ins, name: pe_mark(ins, h_pe, HG_PE, name, order)
                W = lambda sig, table, name: pe.wait_ge(sig.sem, sig.at(step(table, n, name)))
                G = lambda q, k0=0, k1=KD: in_tile(L, "in_gates", lap, q, q % 4, q // 4 + 1, span=(k0, k1))

                G(0)
                pe.wait_ge(h_act.sem, h_act.at(step(HG_ACT, n - 1, "o_sd")))
                W(h_act, HG_ACT, "qs")
                W(h_pool, HG_POOL, "vcur")
                for j in range(2):
                    jr = slice(j * 64, j * 64 + 64)
                    for t in range(TT):
                        o = bank[4 + 2 * j + t // 2]
                        for half in range(2):
                            kb = max(t - 1 + half, 0)
                            c0 = (t % 2) * 2 * P + half * P
                            mm = pe.matmul(o[:, c0:c0 + P], qs[jr, t * P:(t + 1) * P], kcur[jr, kb * P:(kb + 1) * P],
                                           start=True, stop=True)
                        if t % 2:
                            done(mm, f"scores_{j}{t // 2}")
                G(1)
                G(2)
                for j in range(2):
                    W(h_dve, HG_DVE, f"probs_{j}")
                    for t in range(TT):
                        for half in range(2):
                            mm = pe.transpose(bank[4 + 2 * j + t // 2][:, (t % 2) * 2 * P + half * P:(t % 2) * 2 * P + half * P + P],
                                              sc[:, j, t, half * P:(half + 1) * P], ident[:])
                        if t % 2:
                            done(mm, f"probT_{j}{t // 2}")
                W(h_act, HG_ACT, "probT_01")
                for t in range(TT):
                    mm = pe.transpose(bank[5][:, t * P:(t + 1) * P], hz[:, 2, t * P:(t + 1) * P], ident[:])
                done(mm, "hv")
                for j in range(2):
                    W(h_act, HG_ACT, f"probT_{j}1")
                    for t in range(TT):
                        o = bank[4][j * 64:j * 64 + 64, t * P:(t + 1) * P]
                        if t:
                            pe.matmul(o, vcur[:, t - 1, :], pT_[:, j, t, 0, :], start=True, stop=False)
                        mm = pe.matmul(o, vcur[:, t, :], pT_[:, j, t, 1, :], start=t == 0, stop=True)
                done(mm, "att")
                for l in range(LEVELS + 1):
                    W(h_pool, HG_POOL, f"qk{min(l, LEVELS - 1)}")
                    if l >= 2:
                        W(h_dve, HG_DVE, f"att{l - 2}")
                    b = bank[6 + l % 2]
                    for t in range(TT):
                        c = slice(t * P, (t + 1) * P)
                        if l < LEVELS:
                            mm = pe.matmul(b[:, c], qk[:, l % 2, c], qk[:, l % 2, c], start=True, stop=True)
                        else:
                            mm = pe.matmul(b[:, c], key[:, c], hq[:, c], start=True, stop=True)
                    done(mm, f"att{l}")
                    G(3 + l // 4, l % 4 * 2, l % 4 * 2 + 2)
                W(h_pool, HG_POOL, "kd")
                W(h_act, HG_ACT, "yatt")
                for t in range(TT):
                    mm = pe.transpose(bank[4][:, t * P:(t + 1) * P], dd[:, 1, t * P:(t + 1) * P], ident[:])
                done(mm, "hk")
                W(h_act, HG_ACT, "hk_tok")
                for t in range(TT - 1):
                    mm = pe.matmul(bank[5][:, t * P:(t + 1) * P], hk_tok[:, t, :], hv_tok[:, t, :], start=True, stop=True)
                done(mm, "dS")
                G(5)
                W(h_dve, HG_DVE, "S3")
                for t in range(TT):
                    c = slice(t * P, (t + 1) * P)
                    mm = pe.matmul(bank[6][:, c], hv_tok[:, t, :], attT[:, t, :], start=True, stop=t == 0)
                    if t:
                        mm = pe.matmul(bank[6][:, c], S[:, t, :], qb[:, c], start=False, stop=True)
                done(mm, "o")
                W(h_act, HG_ACT, "o_sq")
                done(pe.matmul(bank[7][:], ones[:], hsq[:], start=True, stop=True), "o_norm")
                assert order == HG_PE, order

            def mixer(L):
                in_tile(L, "in_ab", 0, 0, 0, event=4 * L + 1)
                norm(4 * L + 1)
                in_tile(L, "in_ab", 0, 1, 1)
                with pe.Fori(1, 10) as lap:
                    for q in range(2):
                        in_tile(L, "in_ab", lap, q, q)
                with pe.Fori(0, PAIRS) as lap:
                    rwkv_lap(L, lap)
                pe.wait_ge(kv_in, 32 * L + 32)
                pe.wait_ge(w_dve.sem, w_dve.at(step(RW_DVE, 4 * L + 3, "y_1")))
                for t in range(TT):
                    mm = pe.transpose(bank[4][:, t * P:(t + 1) * P], kvraw[:, 1, t * P:(t + 1) * P], ident[:])
                mm.then_inc(l_pe.sem, 1)
                with pe.Fori(0, PAIRS) as lap:
                    hgrn_lap(L, lap)
                with pe.Fori(0, KD // 2) as lap:
                    for q in range(6):
                        if q % 3:
                            pe.wait_ge(m_lo.sem, m_lo.at(8 * L + PAIRS * (q % 3)))
                        else:
                            pe.wait_ge(m_lo_a.sem, m_lo_a.at(4 * L + PAIRS))
                        bank_free(L, "merge", lap, q)
                        chunk(L, "merge", lap, q // 2 + 1, q % 2, PAIRS, yhi, ylo, (q % 3) * PAIRS, q, True, True)
                with pe.Fori(0, KD // 2) as lap:
                    pe.wait_ge(m_mlo.sem, m_mlo.at(8 * L + 8))
                    for q in range(2):
                        bank_free(L, "w_o", lap, q)
                        chunk(L, "w_o", lap, 1, q, KD, mhi, mlo, 0, q, True, True)

            with pe.Fori(0, DEPTH) as L:
                ffn(L, 1, 4 * L, fhi, flo)
                mixer(L)
                ffn(L, 2, 4 * L + 2, ghi, glo)
                pe.wait_ge(p_in, 16 * L + 16)
                for m in range(2):
                    for t in range(TT):
                        mm = pe.transpose(bank[4 + m][:, t * P:(t + 1) * P], praw[:, t, m * P:(m + 1) * P], ident[:])
                    mm.then_inc(p_turned.sem, 1)

                def ple_lap(lap, first):
                    for i in range(2):
                        bank_free(L, "ple", lap, 2 * i)
                        event = 4 * L + 3 if first and i == 0 else None
                        chunk(L, "ple", lap, i + 1, 0, KD, ghi, glo, 0, 2 * i, True, True, event=event)
                        if first and i == 0:
                            norm(4 * L + 3)
                            pe.wait_ge(p_lo.sem, p_lo.at(2 * L + 2))
                        bank_free(L, "ple", lap, 2 * i + 1)
                        chunk(L, "ple", lap, i + 1, 1, 2, phi, plo, 0, 2 * i + 1, True, True)
                ple_lap(0, True)
                with pe.Fori(1, KD // 2) as lap:
                    ple_lap(lap, False)
            norm(4 * DEPTH)
            for t in range(TT):
                for g in range(2):
                    n = 2 * t + g
                    for j in range(4):
                        m = 4 * g + j
                        if t == 0:
                            pe.wait_ge(out_new.sem, m + 1)
                        if n >= 6 and j == 0:
                            pe.wait_ge(out_copied.sem, n - 5)
                        mm = pe.transpose(bank[n % 6][:, j * P:(j + 1) * P], fin[:, m, t * P:(t + 1) * P], ident[:])
                    mm.then_inc(turned.sem, 1)

        @block.scalar
        def _(act):
            for s in (*w_hi, g_hi, g_sq, n_rms, f_sig, f_hi, p_hi, p_sig, w_act, h_act, l_act, m_hi, m_sig, m_mhi):
                act.sem_inc(s.sem, s.ahead)
            act.wait_ge(const.sem, 3)
            for i, sem in enumerate((*stage_out, ya_out, yb_out, yc_out)):
                act.dma_start(primer[i], ident[:]).then_inc(sem, 16)

            def convert(L, section, lap, k, slot, n=W_BUF):
                use = SLOT.nth(L, section, lap, k)
                act.wait_ge(landed[slot], 16 * use)
                act.wait_ge(used[slot].sem, used[slot].at(use - 1))
                act.activation(whi[:, slot, 0:n], wraw[:, slot, 0:n], ACT.Copy).then_inc(w_hi[slot].sem, 1)

            def prep(e, m, i, gain, hi):
                n = 8 * e + m + 1
                act.wait_ge(g_sum.sem, g_sum.at(n - 2))
                act.activation(hi[:, m, :], x[:, m, :], ACT.Copy, scale=gain).then_inc(g_hi.sem, 1)
                act.activation(xsq[:, i, :], x[:, m, :], ACT.Square).then_inc(g_sq.sem, 1)

            def norm(e):
                act.wait_ge(n_sum.sem, n_sum.at(e + 1))
                act.wait_ge(n_rstd.sem, n_rstd.at(e))
                act.activation(rstd[:], bank[7][:], ACT.Sqrt, scale=1.0 / D, bias=eps_col[:, 0:1]).then_inc(n_rms.sem, 1)
                act.activation(table_set[:], eps_col[:, 0:1], ACT.Sigmoid)

            act.wait_ge(eps_set.sem, 1)
            act.wait_ge(lb_step.sem, 2)
            act.activation(lb[:, PAIRS:2 * PAIRS], lb_rest[:, 0:PAIRS], ACT.Sigmoid).then_inc(lb_sig.sem, 1)
            act.wait_ge(cols_ready.sem, 1)
            act.wait_ge(masks.sem, MASK_STEPS)
            for m in range(KD):
                act.wait_ge(x_new.sem, m + 1)
                prep(0, m, m % 2, cols[:, m:m + 1], fhi)

            def ffn(L, f, event, next_gain):
                done = L * (2 * sum(HALF_TILES)) + (f - 1) * sum(HALF_TILES)
                for half, tiles in zip("ab", HALF_TILES):
                    if half == "a":
                        norm(event)
                    up_, down_ = f"f{f}{half}_up", f"f{f}{half}_down"
                    with act.Fori(0, tiles) as j:
                        n = done + j + 1
                        convert(L, up_, j, 1, 1)
                        convert(L, up_, j, 2, 0)
                        act.wait_ge(read[0].sem, read[0].at(BANK[0].nth(L, up_, j)))
                        act.wait_ge(f_act.sem, f_act.at(n - 1))
                        act.activation(gate_sig[:], gate_in[:], ACT.Sigmoid).then_inc(f_sig.sem, 1)
                        act.wait_ge(f_h.sem, f_h.at(n))
                        act.activation(hhi[:, j, :], h[:], ACT.Copy).then_inc(f_hi.sem, 1)
                    nk = tiles // 2
                    with act.Fori(0, KD // 2) as lap:
                        for i in range(2):
                            convert(L, down_, lap, i + 1, 1, nk * P)
                            convert(L, down_, lap, i + 2, 0)
                            if half == "b":
                                act.wait_ge(read[i].sem, read[i].at(BANK[i].nth(L, down_, lap)))
                                m = act.snap(lap * 2 + i)
                                prep(event + 1, m, i, lc[:, bass.ds(act.snap(m + next_gain), 1)], ghi)
                    done = done + tiles

            def send(L, section, lap, b, tile, k=1):
                act.wait_ge(read[b].sem, read[b].at(BANK[b].nth(L, section, lap, k)))
                tile = tile if isinstance(tile, int) else act.snap(tile)
                act.dma_start(zd[bass.ds(tile, 1), :, :].rearrange("a p c -> p (a c)"), stage[:, b, :])\
                   .then_inc(stage_out[b], 16)

            def fetch(dst, tile, sem):
                tile = tile if isinstance(tile, int) else act.snap(tile)
                act.dma_start(dst, zd[bass.ds(tile, 1), :, :].rearrange("a p c -> p (a c)")).then_inc(sem, 16)

            def ahead(L, section, lap, q, n=W_BUF):
                convert(L, section, lap, (q + 1) // 2 + 1, (q + 1) % 2, n)

            def rwkv_lap(L, lap):
                n = act.snap(L * PAIRS + lap)
                order = []
                done = lambda ins, name: pe_mark(ins, w_act, RW_ACT, name, order)
                W = lambda sig, table, name, back=0: act.wait_ge(sig.sem, sig.at(step(table, n - back, name)))
                col = lambda name: lc[:, bass.ds(act.snap(lap + COL[name]), 1)]
                ahead(L, "in_c", lap, 0)
                W(w_pe, RW_PE, "d")
                done(act.activation(w_[:], bank[4][:], ACT.Sigmoid, bias=col("rwkv_w0")), "w")
                W(w_pe, RW_PE, "a")
                done(act.activation(a_[:], bank[5][:], ACT.Sigmoid, bias=col("rwkv_a0")), "a")
                W(w_pe, RW_PE, "g")
                W(w_pool, RW_POOL, "y", 1)
                done(act.activation(g_[:], bank[6][:], ACT.Copy), "g")
                done(act.activation(lw_g[:], bank[6][:], ACT.Copy, scale=col("rwkv_ln_w")), "lw_g")
                W(w_dve, RW_DVE, "yn", 1)
                W(w_dve, RW_DVE, "k")
                done(act.activation(kk[:], k_[:], ACT.Copy, scale=col("rwkv_k_k")), "kk_raw")
                done(act.activation(tmp[:], k_[:], ACT.Square, scale=col("rwkv_k_k")), "kk_sq")
                W(w_dve, RW_DVE, "kmax")
                done(act.activation(tmp[:], tmp[:], ACT.Sqrt), "kk_root")
                W(w_dve, RW_DVE, "cs")
                done(act.activation(dec[:], cs[:], ACT.Exp, scale=-DECAY), "dec")
                done(act.activation(inc[:], cs[:], ACT.Exp, scale=DECAY), "inc")
                ahead(L, "in_c", lap, 1)
                W(w_dve, RW_DVE, "kk")
                first = lambda t: t[:].rearrange("p (c s) -> p c s", s=HD)[:, :, 0]
                done(act.activation(first(kq), first(kk), ACT.Copy), "kq0")
                W(w_pe, RW_PE, "turn_v")
                done(act.activation(v_tok[:], bank[6][:].rearrange("p (t c) -> p t c", t=TT), ACT.Copy), "v_tok")
                ahead(L, "in_c", lap, 2)
                W(w_pe, RW_PE, "turn_kq")
                done(act.activation(rhs[:, :, :, 0, :], bank[7][:].rearrange("p (t h c) -> p t h c", t=TT, h=2),
                                    ACT.Copy, scale=-1.0), "kq_tok")
                W(w_pe, RW_PE, "turn_bh")
                done(act.activation(b_tok[:], bank[4][:].rearrange("p (t c) -> p t c", t=TT), ACT.Copy), "b_tok")
                W(w_pe, RW_PE, "turn_kh")
                done(act.activation(k_tok[:], bank[5][:].rearrange("p (t c) -> p t c", t=TT), ACT.Copy), "k_tok")
                W(w_pe, RW_PE, "A2v")
                done(act.activation(rhs[:, :, :, 1, :], bank[4][:].rearrange("p (h t c) -> p t h c", t=TT, h=2),
                                    ACT.Copy), "A2v_tok")
                send(L, "in_c", lap, 0, lap * 4 + Z_HQ)
                send(L, "in_c", lap, 1, lap * 4 + (Z_HQ + 1))
                for h in range(2):
                    W(w_pe, RW_PE, f"PG_{h}")
                    done(act.activation(PG[:, h, :, :], bank[4 + h][:].rearrange("p (t c) -> p t c", t=TT), ACT.Copy), f"PG_{h}")
                ahead(L, "in_c", lap, 3)
                for par, b in ((0, bank[7]), (1, bank[4])):
                    W(w_pe, RW_PE, f"state_{par}")
                    done(act.activation(NZ[:].rearrange("p (t a) c -> p a t c", a=2)[:, par, :, :],
                                        b[:, TT * HD:2 * TT * HD].rearrange("p (t c) -> p t c", t=TT), ACT.Copy), f"NZ_{par}")
                W(w_dve, RW_DVE, "bonus")
                done(act.activation(bonus[:], bonus[:], ACT.Identity, bias=col("rwkv_ln_b")), "bonus_b")
                send(L, "in_c", lap, 2, lap * 4 + (Z_HQ + 2))
                send(L, "in_c", lap, 3, lap * 4 + (Z_HQ + 3))
                W(w_pe, RW_PE, "y_0")
                done(act.activation(y_[0:HD, :], bank[6][0:HD, :], ACT.Copy), "y_0")
                W(w_dve, RW_DVE, "yc")
                done(act.activation(tmp[:], y_[:], ACT.Square), "y_sq")
                W(w_pe, RW_PE, "var")
                done(act.activation(tmp[:], bank[6][:], ACT.Sqrt, scale=1.0 / HD, bias=gn_eps[:, 0:1]), "y_sd")
                assert order == RW_ACT, order

            def hgrn_lap(L, lap):
                n = act.snap(L * PAIRS + lap)
                order = []
                done = lambda ins, name: pe_mark(ins, h_act, HG_ACT, name, order)
                W = lambda sig, table, name, back=0: act.wait_ge(sig.sem, sig.at(step(table, n - back, name)))
                tokens = lambda ap: ap.rearrange("p (t c) -> p t c", t=TT)
                W(h_pe, HG_PE, "hv", 1)
                act.wait_ge(zq_in, 16 * (n + L) + 16)
                done(act.activation(qs[:], zq[:], ACT.Copy, scale=HD ** -0.5), "qs")
                act.wait_ge(hz_in, 64 * (n + L) + 64)
                done(act.activation(fg[:], hz[:, 1, :], ACT.Sigmoid), "sig_f")
                W(h_pe, HG_PE, f"att{LEVELS}", 1)
                W(h_pool, HG_POOL, "kd", 1)
                done(act.activation(hq[:], hz[:, 0, :], ACT.Sigmoid), "sig_q")
                W(h_dve, HG_DVE, "y", 1)
                done(act.activation(hog[:], hz[:, 3, :], ACT.Sigmoid), "sig_o")
                ahead(L, "in_gates", lap, 0)
                W(h_dve, HG_DVE, "f")
                done(act.activation(logf[:], fg[:], ACT.Ln), "logf")
                ahead(L, "in_gates", lap, 1)
                act.wait_ge(sinks_in, 16)
                for j in range(2):
                    sink = sinks[:, bass.ds(act.snap(n * 2 + j), 1)]
                    W(h_dve, HG_DVE, f"max_{j}")
                    for t in range(TT):
                        ins = act.activation(sc[:, j, t, :], sc[:, j, t, :], ACT.Exp, bias=small[:, j, 1, t:t + 1],
                                             accum_out=small[:, j, 2, t:t + 1])
                    done(ins, f"exp_{j}")
                    done(act.activation(small[:, j, 3, :], small[:, j, 1, :], ACT.Exp, bias=sink), f"esink_{j}")

                def level(l):
                    m = 1 << l
                    half = lambda t: t[:, l % 2, :].rearrange("p (b a m) -> p b a m", a=2, m=m)
                    W(h_dve, HG_DVE, f"d{l}")
                    if l < 2:
                        W(h_pool, HG_POOL, "kd", 1)
                    else:
                        W(h_pool, HG_POOL, f"qk{l - 2}")
                    act.activation(half(ex)[:, :, 0, :], half(dd)[:, :, 0, :], ACT.Exp, scale=-1.0)
                    done(act.activation(half(ex)[:, :, 1, :], half(dd)[:, :, 1, :], ACT.Exp), f"ex{l}")

                level(0)
                level(1)
                send(L, "in_gates", lap, 0, lap * 6 + Z_GATE)
                for j in range(2):
                    for g in range(2):
                        W(h_pe, HG_PE, f"probT_{j}{g}")
                        done(act.activation(pT_[:, j, 2 * g:2 * g + 2, :, :].rearrange("p t a c -> p (t a c)"),
                                            bank[4 + 2 * j + g][:], ACT.Copy), f"probT_{j}{g}")
                send(L, "in_gates", lap, 1, lap * 6 + (Z_GATE + 1))
                ahead(L, "in_gates", lap, 2)
                W(h_pe, HG_PE, "hv")
                done(act.activation(hv_tok[:], tokens(bank[5][:]), ACT.Copy), "hv_tok")
                act.wait_ge(ya_out, 16 * n + 16)
                W(h_pe, HG_PE, "att")
                done(act.activation(yatt[:], bank[4][:], ACT.Copy), "yatt")
                send(L, "in_gates", lap, 2, lap * 6 + (Z_GATE + 2))
                for l in range(2, LEVELS):
                    if l == LEVELS - 2:
                        done(act.activation(logf[:], bsum[:], ACT.Exp), "eb")
                    level(l)
                    if l in (2, 5):
                        ahead(L, "in_gates", lap, l // 3 + 3)
                W(h_dve, HG_DVE, "dend")
                W(h_pool, HG_POOL, f"qk{LEVELS - 1}")
                done(act.activation(ex[:, 1, :], dd[:, 1, :], ACT.Exp, scale=-1.0), "ed")
                send(L, "in_gates", lap, 3, lap * 6 + (Z_GATE + 3))
                W(h_pe, HG_PE, "hk")
                done(act.activation(hk_tok[:], tokens(bank[4][:]), ACT.Copy), "hk_tok")
                ahead(L, "in_gates", lap, 5)
                send(L, "in_gates", lap, 0, lap * 6 + (Z_GATE + 4), 2)
                send(L, "in_gates", lap, 1, lap * 6 + (Z_GATE + 5), 2)
                W(h_pe, HG_PE, "o")
                act.wait_ge(yc_out, 16 * n + 16)
                done(act.activation(ho[:], bank[6][:], ACT.Copy), "o")
                done(act.activation(hsq[:], bank[6][:], ACT.Square), "o_sq")
                W(h_pe, HG_PE, "o_norm")
                done(act.activation(hsq[:], bank[7][:], ACT.Sqrt, scale=1.0 / P, bias=eps_col[:, 0:1]), "o_sd")
                assert order == HG_ACT, order

            def mixer(L):
                norm(4 * L + 1)
                def in_lap(lap, tile):
                    for q in range(2):
                        ahead(L, "in_ab", lap, q)
                        send(L, "in_ab", lap, q, tile + q)
                in_lap(0, Z_WA)
                act.wait_ge(l_dve.sem, l_dve.at(step(LY_DVE, L, "mt_zero")))
                for b in range(2):
                    act.wait_ge(stage_out[b], 16 * STAGE[b].nth(L, "in_ab", 0) + 16)
                fetch(zr[:, 0, 1:SEQ + 1], Z_WA, wag_in)
                fetch(zr[:, 1, 1:SEQ + 1], Z_G, wag_in)
                with act.Fori(1, 5) as lap:
                    in_lap(lap, act.snap(lap * 2 - 2))
                act.wait_ge(l_dve.sem, l_dve.at(step(LY_DVE, L, "g")))
                act.activation(xwa[0:64, :], xwa[0:64, :], ACT.Tanh).then_inc(l_act.sem, 1)
                act.activation(xgs[:], xgs[:], ACT.Sigmoid).then_inc(l_act.sem, 1)
                with act.Fori(5, 10) as lap:
                    in_lap(lap, act.snap(lap * 2 - 2))
                for b in range(2):
                    act.wait_ge(stage_out[b], 16 * STAGE[b].nth(L, "in_ab", 9) + 16)
                act.wait_ge(lora_in, 96 * L + 96)
                act.activation(lwa[:], lora_wa[:, 0:P], ACT.Copy).then_inc(l_act.sem, 1)
                act.activation(lg[:], lora_g[:, 0:P], ACT.Copy).then_inc(l_act.sem, 1)
                act.wait_ge(l_dve.sem, l_dve.at(step(LY_DVE, L, "g")))
                for i, z0 in enumerate((Z_R, Z_RK, Z_RV)):
                    fetch(zr[:, i, 1:SEQ + 1], z0, rkv_in)
                with act.Fori(0, PAIRS) as lap:
                    rwkv_lap(L, lap)
                act.wait_ge(kv_in, 32 * L + 32)
                for kv in range(2):
                    for r in range(2):
                        act.activation(krep[r * 64:r * 64 + 64, kv, :], kvraw[kv * 64:kv * 64 + 64, 0, :], ACT.Copy)\
                           .then_inc(l_act.sem, 1)
                act.wait_ge(l_pe.sem, l_pe.at(step(LY_PE, L, "v")))
                act.activation(vtok2[:].rearrange("p k t c -> p t k c"), bank[4][:].rearrange("p (t k c) -> p t k c", t=TT, k=2),
                               ACT.Copy).then_inc(l_act.sem, 1)
                with act.Fori(0, PAIRS) as lap:
                    hgrn_lap(L, lap)
                act.wait_ge(hz_in, 64 * (5 * L) + 5 * 64)
                act.wait_ge(zq_in, 16 * (5 * L) + 5 * 16)
                for b in range(4):
                    act.wait_ge(stage_out[b], 16 * STAGE[b].nth(L, "in_gates", 3, 2 if b < 2 else 1) + 16)
                gate_view = zd[Z_GATE:Z_TILES, :, :].rearrange("(b m) p c -> m p b c", b=3)

                def gate_fetch(m, i):
                    src = gate_view[bass.ds(act.snap(m), 1), :, :, :] if not isinstance(m, int) else gate_view[m:m + 1, :, :, :]
                    act.dma_start(gates[:, i, :, :], src.rearrange("a p b c -> p (a b) c")).then_inc(gates_in[i], 16)

                def gate_sigmoid(u, i):
                    act.wait_ge(gates_in[i], 16 * u)
                    act.activation(gates[:, i, :, :], gates[:, i, :, :], ACT.Sigmoid).then_inc(m_sig.sem, 1)

                for tile in range(12):
                    i = tile % Y_RAW
                    if tile == Y_RAW:
                        gate_sigmoid(4 * L + 1, 0)
                    act.wait_ge(y_in[i], 32 * L + 16 * (tile // Y_RAW + 1))
                    act.activation(yhi[:, tile, :], yraw[:, i, :], ACT.Copy).then_inc(m_hi.sem, 1)

                def merge_lap(lap, last):
                    for i in range(2):
                        u = 8 * L + 2 * lap + i + 1
                        ahead(L, "merge", lap, 3 * i + 1, PAIRS * P)
                        if not (last and i):
                            gate_sigmoid(4 * L + lap + (i + 1), 1 - i)
                        ahead(L, "merge", lap, 3 * i + 2, W_BUF if i else PAIRS * P)
                        if i == 0:
                            ahead(L, "merge", lap, 3, PAIRS * P)
                        elif not last:
                            ahead(L, "merge", act.snap(lap + 1), 0, PAIRS * P)
                        act.wait_ge(m_sum.sem, m_sum.at(u))
                        act.activation(mhi[:, bass.ds(act.snap(lap * 2 + i), 1), :].rearrange("p a c -> p (a c)") if not last
                                       else mhi[:, lap * 2 + i, :], acc[:, 0, :], ACT.Copy).then_inc(m_mhi.sem, 1)
                        if not last:
                            gate_fetch(lap * 2 + i + 2, i)
                ahead(L, "merge", 0, 0, PAIRS * P)
                with act.Fori(0, KD // 2 - 1) as lap:
                    merge_lap(lap, False)
                merge_lap(KD // 2 - 1, True)
                with act.Fori(0, KD // 2) as lap:
                    for q in range(2):
                        ahead(L, "w_o", lap, q)
                        act.wait_ge(read[q].sem, read[q].at(BANK[q].nth(L, "w_o", lap)))
                        m = act.snap(lap * 2 + q)
                        prep(4 * L + 2, m, q, lc[:, bass.ds(act.snap(m + COL["ffn2_norm"]), 1)], ghi)

            with act.Fori(0, DEPTH) as L:
                act.wait_ge(lc_ready.sem, L + 1)
                convert(L, "f1a_up", 0, 1, 0)
                ffn(L, 1, 4 * L, COL["mix_norm"])
                mixer(L)
                ffn(L, 2, 4 * L + 2, COL["ple_norm"])
                for m in range(2):
                    act.wait_ge(p_copied.sem, p_copied.at(2 * L + m + 1))
                    act.activation(phi[:, m, :], pT[:, m, :], ACT.Copy).then_inc(p_hi.sem, 1)
                norm(4 * L + 3)

                def ple_lap(lap, last):
                    for i in range(2):
                        n = 8 * L + 2 * lap + i + 1
                        convert(L, "ple", lap, i + 1, 1, 2 * P)
                        if not (last and i == 1):
                            convert(L, "ple", lap, i + 2, 0)
                        act.wait_ge(read[2 * i].sem, read[2 * i].at(BANK[2 * i].nth(L, "ple", lap)))
                        act.activation(pgate[:, i, :], pgate[:, i, :], ACT.Sigmoid).then_inc(p_sig.sem, 1)
                        act.wait_ge(p_add.sem, p_add.at(n))
                        m = lap * 2 + i if last else act.snap(lap * 2 + i)
                        gain = lc[:, NEXT_GAIN + m:NEXT_GAIN + m + 1] if last else lc[:, bass.ds(act.snap(m + NEXT_GAIN), 1)]
                        prep(4 * L + 4, m, i, gain, fhi)
                with act.Fori(0, KD // 2 - 1) as lap:
                    ple_lap(lap, False)
                ple_lap(KD // 2 - 1, True)
            norm(4 * DEPTH)

        @block.gpsimd
        def _(pool):
            for s in (g_sum, f_act, f_lo, p_lo, w_pool, h_pool, m_lo_a, m_mlo):
                pool.sem_inc(s.sem, s.ahead)
            pool.memset(ident[:], 0.0).then_inc(const.sem, 1)
            pool.memset(ones[:], 1.0).then_inc(const.sem, 1)
            pool.memset(zero[:], 0.0).then_inc(zero_set.sem, 1)
            pool.memset(eps_col[:], EPS).then_inc(eps_set.sem, 1)
            pool.wait_ge(const.sem, 2)
            pool.affine_select(out=ident[:], in_=ident[:], compare_op=ALU.not_equal, fill=1.0, base=0,
                               pattern=[[-1, P]], channel_multiplier=1).then_inc(const.sem, 1)

            masks_left = [0]

            def fill(ap, value, waits=0):
                pool.memset(ap, value).then_inc(masks.sem, 1)
                masks_left[0] += 1
                pool.wait_ge(masks.sem, masks_left[0])

            def keep(out_ap, in_ap, base, pattern, rows=1, fill_=0.0):
                pool.affine_select(out=out_ap, in_=in_ap, compare_op=ALU.is_ge, fill=fill_, base=base, pattern=pattern,
                                   channel_multiplier=rows).then_inc(masks.sem, 1)
                masks_left[0] += 1
                pool.wait_ge(masks.sem, masks_left[0])

            minus = xsq[:, 0, 0:P]
            plus = xsq[:, 0, P:2 * P]
            fill(minus, -1.0)
            fill(plus, 1.0)
            fill(low[:], 0.0)
            fill(up0[:], 0.0)
            fill(pair_mask[:], 0)
            fill(gn_eps[:], GN_EPS)
            for l in range(LEVELS):
                m = 1 << l
                halves = lambda ap: ap.rearrange("p (b a m) -> p b a m", a=2, m=m)
                nb = P // (2 * m)
                if l < LEVELS - 1:
                    t_, s_ = halves(low[:, l, :]), halves(minus if l == 0 else plus)
                    keep(t_[:, :, 0, :], s_[:, :, 0, :], -m, [[-2 * m, nb], [0, m]])
                    keep(t_[:, :, 0, :], t_[:, :, 0, :], 2 * m - 1, [[2 * m, nb], [0, m]], -1)
                t_, s_ = halves(pair_mask[:, l, :]), halves(plus)
                keep(t_[:, :, 1, :], s_[:, :, 1, :], 0, [[-2 * m, nb], [0, m]])
                keep(t_[:, :, 1, :], t_[:, :, 1, :], m - 1, [[2 * m, nb], [0, m]], -1)
                if l == 0:
                    t_ = halves(up0[:])
                    keep(t_[:, :, 1, :], s_[:, :, 1, :], 0, [[-2 * m, nb], [0, m]])
                    keep(t_[:, :, 1, :], t_[:, :, 1, :], m - 1, [[2 * m, nb], [0, m]], -1)
            pool.tensor_copy(pair_mask[:, LEVELS, :], ident[:]).then_inc(masks.sem, 1)
            masks_left[0] += 1
            chunks = [[-HD, 2], [0, HD]]
            keep(before[:], minus, -1, [[1, P]], -1)
            keep(before[:], before[:], 0, chunks)
            keep(upto[:], plus, 0, [[1, P]], -1)
            keep(upto[:], upto[:], 0, chunks)
            fill(band[:], 0.0)
            fill(band[:, 0, :], MASKED)
            keep(band[:, 2, :], band[:, 2, :], -1, [[1, P]], -1, MASKED)
            for i in (1, 3):
                keep(band[:, i, :], band[:, i, :], 0, [[-1, P]], 1, MASKED)
            fill(seg64[:], 1.0)
            fill(seg64[:].rearrange("p (c s) -> p c s", s=HD)[:, :, 0], 0.0)
            fill(seg128[:], 1.0)
            fill(seg128[:].rearrange("p (c s) -> p c s", s=P)[:, :, 0], 0.0)
            fill(head_ones[:], 0.0)
            fill(head_ones[0:64, 0:64], 1.0)
            fill(head_ones[64:P, 64:P], 1.0)
            pool.tensor_copy(eye64[0:64, :], ident[0:64, 0:64]).then_inc(masks.sem, 1)
            pool.wait_ge(masks.sem, MASK_STEPS - 1)
            pool.tensor_copy(eye64[64:P, :], ident[64:P, 64:P]).then_inc(masks.sem, 1)
            pool.wait_ge(masks.sem, MASK_STEPS)
            masks_left[0] += 2
            assert masks_left[0] == MASK_STEPS, masks_left

            def prep(e, m, i):
                n = 8 * e + m + 1
                pool.wait_ge(g_sq.sem, g_sq.at(n))
                pool.wait_ge(g_sum.sem, g_sum.at(n - 1))
                pool.wait_ge(sum_clear.sem, e + 1)
                pool.tensor_tensor(ssum[:], ssum[:], xsq[:, i, :], ALU.add).then_inc(g_sum.sem, 1)

            def clear_sum(e):
                pool.wait_ge(n_sum.sem, n_sum.at(e))
                pool.tensor_tensor(ssum[:], zero[:, 0:1].broadcast_to([P, SEQ]), zero[:, 0:1].broadcast_to([P, SEQ]),
                                   ALU.add).then_inc(sum_clear.sem, 1)

            pool.wait_ge(zero_set.sem, 1)
            pool.wait_ge(const.sem, 3)
            clear_sum(0)
            for m in range(KD):
                prep(0, m, m % 2)

            def ffn(L, f, event):
                done = L * (2 * sum(HALF_TILES)) + (f - 1) * sum(HALF_TILES)
                for half, tiles in zip("ab", HALF_TILES):
                    up_, down_ = f"f{f}{half}_up", f"f{f}{half}_down"
                    with pool.Fori(0, tiles) as j:
                        n = done + j + 1
                        pool.wait_ge(f_sig.sem, f_sig.at(n))
                        pool.wait_ge(f_h.sem, f_h.at(n - 1))
                        pool.tensor_tensor(gate_act[:], gate_in[:], gate_sig[:], ALU.mult).then_inc(f_act.sem, 1)
                        pool.wait_ge(f_hi.sem, f_hi.at(n))
                        pool.tensor_tensor(hlo[:, j, :], h[:], hhi[:, j, :].bitcast(F32), ALU.subtract).then_inc(f_lo.sem, 1)
                    nk = tiles // 2
                    if half == "b":
                        clear_sum(event + 1)
                    with pool.Fori(0, KD // 2) as lap:
                        for i in range(2):
                            if half == "b":
                                prep(event + 1, pool.snap(lap * 2 + i), i)
                    done = done + tiles

            def rwkv_lap(L, lap):
                n = pool.snap(L * PAIRS + lap)
                order = []
                done = lambda ins, name: pe_mark(ins, w_pool, RW_POOL, name, order)
                W = lambda sig, table, name, back=0: pool.wait_ge(sig.sem, sig.at(step(table, n - back, name)))
                last = lambda t: t[:].rearrange("p (c s) -> p c s", s=HD)[:, :, HD - 1:HD]
                W(w_act, RW_ACT, "inc")
                W(w_dve, RW_DVE, "ka")
                done(pool.tensor_tensor(a_[:], a_[:], inc[:], ALU.mult), "a_inc")
                W(w_dve, RW_DVE, "rk")
                done(pool.tensor_tensor(kp[:], kp[:], inc[:], ALU.mult), "kt")
                done(pool.tensor_tensor(r_[:], r_[:], dec[:], ALU.mult), "rt")
                done(pool.tensor_tensor(ediag[:], eye64[:].unsqueeze(1).broadcast_to([P, C, HD]),
                                        last(dec).broadcast_to([P, C, HD]), ALU.mult), "ediag")
                mine = bass.ds(pool.snap(lap * P + P), P)
                W(w_pe, RW_PE, "g")
                done(pool.tensor_copy(lwa[:], lora_wa[:, mine]), "lora_wa")
                done(pool.tensor_copy(lg[:], lora_g[:, mine]), "lora_g")
                for h in range(2):
                    W(w_dve, RW_DVE, f"NT_{h}")
                    done(pool.tensor_tensor(XT[:, h, :, :], NT[:, h, :, :], up0[:].unsqueeze(1).broadcast_to([P, TT, P]),
                                            ALU.mult), f"XTm_{h}")
                eye = ident[:].unsqueeze(1).broadcast_to([P, TT, P])
                for h in range(2):
                    W(w_dve, RW_DVE, f"X_{h}")
                    done(pool.tensor_tensor(X[:, h, :, :], X[:, h, :, :], eye, ALU.add), f"X_{h}")
                for h in range(2):
                    W(w_pool, RW_POOL, f"XTm_{h}")
                    done(pool.tensor_tensor(XT[:, h, :, :], XT[:, h, :, :], eye, ALU.add), f"XT_{h}")
                W(w_act, RW_ACT, "bonus_b")
                done(pool.tensor_tensor(bonus[:], bonus[:], g_[:], ALU.mult), "bonus_g")
                W(w_dve, RW_DVE, "yn")
                done(pool.tensor_tensor(y_[:], y_[:], lw_g[:], ALU.mult), "yg")
                W(w_pool, RW_POOL, "yg")
                done(pool.tensor_tensor(y_[:], y_[:], bonus[:], ALU.add), "y")
                assert order == RW_POOL, order

            def hgrn_lap(L, lap):
                n = pool.snap(L * PAIRS + lap)
                order = []
                done = lambda ins, name: pe_mark(ins, h_pool, HG_POOL, name, order)
                W = lambda sig, table, name, back=0: pool.wait_ge(sig.sem, sig.at(step(table, n - back, name)))
                kv = pool.snap(lap // 2)
                pool.wait_ge(l_act.sem, l_act.at(step(LY_ACT, L, "v")))
                W(h_pe, HG_PE, "att", 1)
                done(pool.tensor_copy(kcur[:], krep[:, bass.ds(kv, 1), :].rearrange("p a c -> p (a c)")), "kcur")
                done(pool.tensor_copy(vcur[:], vtok2[:, bass.ds(kv, 1), :, :].rearrange("p a t c -> p (a t) c")), "vcur")
                W(h_dve, HG_DVE, "f")
                W(h_pe, HG_PE, f"att{LEVELS}", 1)
                done(pool.tensor_tensor(key[:], ones[:, 0:1].broadcast_to([P, SEQ]), fg[:], ALU.subtract), "key")
                W(h_act, HG_ACT, "sig_q")
                done(pool.tensor_tensor(hq[:], hq[:], hz[:, 0, :], ALU.mult), "hq")
                W(h_act, HG_ACT, "sig_o")
                done(pool.tensor_tensor(hog[:], hog[:], hz[:, 3, :], ALU.mult), "hog")
                for l in range(LEVELS):
                    m = 1 << l
                    half = lambda t: t.rearrange("p (b a m) -> p b a m", a=2, m=m)
                    W(h_act, HG_ACT, f"ex{l}")
                    if l == 0:
                        W(h_pool, HG_POOL, "hq")
                    if l >= 2:
                        W(h_pe, HG_PE, f"att{l - 2}")
                    pool.tensor_tensor(half(qk[:, l % 2, :])[:, :, 0, :], half(key[:])[:, :, 0, :],
                                       half(ex[:, l % 2, :])[:, :, 0, :], ALU.mult)
                    done(pool.tensor_tensor(half(qk[:, l % 2, :])[:, :, 1, :], half(hq[:])[:, :, 1, :],
                                            half(ex[:, l % 2, :])[:, :, 1, :], ALU.mult), f"qk{l}")
                W(h_act, HG_ACT, "ed")
                done(pool.tensor_tensor(dd[:, 1, :], key[:], ex[:, 1, :], ALU.mult), "kd")
                assert order == HG_POOL, order

            def mixer(L):
                with pool.Fori(0, PAIRS) as lap:
                    rwkv_lap(L, lap)
                with pool.Fori(0, PAIRS) as lap:
                    hgrn_lap(L, lap)
                for tile in range(PAIRS):
                    pool.wait_ge(m_hi.sem, m_hi.at(12 * L + tile + 1))
                    pool.tensor_tensor(ylo[:, tile, :], yraw[:, tile, :], yhi[:, tile, :].bitcast(F32), ALU.subtract)\
                        .then_inc(m_lo_a.sem, 1)
                with pool.Fori(0, KD // 2) as lap:
                    for i in range(2):
                        pool.wait_ge(m_mhi.sem, m_mhi.at(8 * L + 2 * lap + (i + 1)))
                        tile = bass.ds(pool.snap(lap * 2 + i), 1)
                        pool.tensor_tensor(mlo[:, tile, :].rearrange("p a c -> p (a c)"), acc[:, 0, :],
                                           mhi[:, tile, :].rearrange("p a c -> p (a c)").bitcast(F32), ALU.subtract)\
                            .then_inc(m_mlo.sem, 1)
                clear_sum(4 * L + 2)
                with pool.Fori(0, KD // 2) as lap:
                    for q in range(2):
                        prep(4 * L + 2, pool.snap(lap * 2 + q), q)

            with pool.Fori(0, DEPTH) as L:
                ffn(L, 1, 4 * L)
                mixer(L)
                ffn(L, 2, 4 * L + 2)
                for m in range(2):
                    pool.wait_ge(p_hi.sem, p_hi.at(2 * L + m + 1))
                    pool.tensor_tensor(plo[:, m, :], pT[:, m, :], phi[:, m, :].bitcast(F32), ALU.subtract).then_inc(p_lo.sem, 1)
                clear_sum(4 * L + 4)

                def ple_lap(lap, last):
                    for i in range(2):
                        prep(4 * L + 4, lap * 2 + i if last else pool.snap(lap * 2 + i), i)
                with pool.Fori(0, KD // 2 - 1) as lap:
                    ple_lap(lap, False)
                ple_lap(KD // 2 - 1, True)

        @block.vector
        def _(dve):
            for s in (*w_lo, g_lo, m_lo, *read, n_rstd, f_h, p_copied, p_add, w_dve, h_dve, l_dve, m_sum, acc_step):
                dve.sem_inc(s.sem, s.ahead)
            dve.wait_ge(turned.sem, DEPTH)
            for L in range(DEPTH):
                dve.tensor_copy(cols[:, L * LAYER_COLS:(L + 1) * LAYER_COLS],
                                bank[6][:, L * P:L * P + LAYER_COLS]).then_inc(col_copy.sem, 1)
            dve.tensor_copy(cols[:, DEPTH * LAYER_COLS:DEPTH * LAYER_COLS + 8],
                            bank[6][:, LAYER_COLS:LAYER_COLS + 8]).then_inc(cols_ready.sem, 1)
            for m in range(KD):
                dve.wait_ge(turned.sem, DEPTH + m + 1)
                dve.tensor_copy(x[:, m, :], bank[m % 2][:]).then_inc(x_new.sem, 1)

            def norm(e):
                dve.wait_ge(n_rms.sem, n_rms.at(e + 1))
                dve.reciprocal(rstd[:], rstd[:]).then_inc(n_rstd.sem, 1)

            def split(L, section, lap, k, slot, n=W_BUF):
                use = SLOT.nth(L, section, lap, k)
                dve.wait_ge(w_hi[slot].sem, w_hi[slot].at(use))
                dve.tensor_tensor(wlo[:, slot, 0:n], wraw[:, slot, 0:n], whi[:, slot, 0:n].bitcast(F32),
                                   ALU.subtract).then_inc(w_lo[slot].sem, 1)

            def ahead(L, section, lap, q, n=W_BUF):
                split(L, section, lap, (q + 1) // 2 + 1, (q + 1) % 2, n)

            def prep(e, m, gain, hi, lo):
                dve.wait_ge(g_hi.sem, g_hi.at(8 * e + m + 1))
                dve.scalar_tensor_tensor(lo[:, m, :], x[:, m, :], gain, hi[:, m, :].bitcast(F32), ALU.mult, ALU.subtract)\
                   .then_inc(g_lo.sem, 1)

            def take(L, e, section, lap, b, slot, k, out_ap):
                dve.wait_ge(n_rstd.sem, n_rstd.at(e + 1))
                dve.wait_ge(used[slot].sem, used[slot].at(SLOT.nth(L, section, lap, k)))
                dve.tensor_tensor(out_ap, bank[b][:], rstd[:], ALU.mult).then_inc(read[b].sem, 1)

            def ffn(L, f, event, next_gain):
                done = L * (2 * sum(HALF_TILES)) + (f - 1) * sum(HALF_TILES)
                for half, tiles in zip("ab", HALF_TILES):
                    up_, down_ = f"f{f}{half}_up", f"f{f}{half}_down"
                    if half == "a":
                        norm(event)
                    with dve.Fori(0, tiles) as j:
                        n = done + j + 1
                        dve.wait_ge(f_act.sem, f_act.at(n - 1))
                        split(L, up_, j, 1, 1)
                        take(L, event, up_, j, 0, 0, 1, gate_in[:])
                        split(L, up_, j, 2, 0)
                        dve.wait_ge(f_h.sem, f_h.at(n - 1))
                        take(L, event, up_, j, 1, 1, 1, up[:])
                        dve.wait_ge(f_act.sem, f_act.at(n))
                        dve.wait_ge(f_lo.sem, f_lo.at(n - 1))
                        dve.wait_ge(read[1].sem, read[1].at(BANK[1].nth(L, up_, j)))
                        dve.tensor_tensor(h[:], up[:], gate_act[:], ALU.mult).then_inc(f_h.sem, 1)
                    with dve.Fori(0, KD // 2) as lap:
                        for i in range(2):
                            m = dve.snap(lap * 2 + i)
                            split(L, down_, lap, i + 1, 1, tiles // 2 * P)
                            split(L, down_, lap, i + 2, 0)
                            dve.wait_ge(used[1].sem, used[1].at(SLOT.nth(L, down_, lap, i + 1)))
                            dve.wait_ge(g_sum.sem, g_sum.at(8 * event + 8))
                            dve.scalar_tensor_tensor(x[:, m, :], bank[i][:], 0.5, x[:, m, :], ALU.mult, ALU.add)\
                               .then_inc(read[i].sem, 1)
                            if half == "b":
                                prep(event + 1, m, lc[:, bass.ds(dve.snap(m + next_gain), 1)], ghi, glo)
                    done = done + tiles

            dve.wait_ge(cols_ready.sem, 1)
            lbc = lambda L: cols[:, L * LAYER_COLS + COL["hgrn_lb"]:L * LAYER_COLS + COL["hgrn_lb"] + PAIRS]
            dve.memset(lb[:, 0:PAIRS], 0.0).then_inc(lb_step.sem, 1)
            dve.tensor_tensor(lb_rest[:, 0:PAIRS], lbc(1), lbc(0), ALU.subtract).then_inc(lb_step.sem, 1)
            dve.wait_ge(lb_sig.sem, 1)
            dve.tensor_scalar(lb[:, PAIRS:2 * PAIRS], lb[:, PAIRS:2 * PAIRS], 1.0 - 1e-6, None, ALU.min).then_inc(lb_step.sem, 1)
            dve.wait_ge(lb_step.sem, 3)
            dve.tensor_scalar(lb_rest[:], lb[:], -1.0, 1.0, ALU.mult, ALU.add)

            def stage_take(L, section, lap, q, b, k=1, split_before=False):
                if section != "in_c" and not split_before:
                    ahead(L, section, lap, q)
                dve.wait_ge(stage_out[b], 16 * STAGE[b].nth(L, section, lap, k))
                take(L, 4 * L + 1, section, lap, b, q % 2, q // 2 + 1, stage[:, b, :])

            def rwkv_lap(L, lap):
                n = dve.snap(L * PAIRS + lap)
                order = []
                done = lambda ins, name: pe_mark(ins, w_dve, RW_DVE, name, order)
                W = lambda sig, table, name, back=0: dve.wait_ge(sig.sem, sig.at(step(table, n - back, name)))
                mine = lambda name: W(w_dve, RW_DVE, name)
                col = lambda name, i=0: lc[:, bass.ds(dve.snap(lap + (COL[name] + i)), 1)]
                chunks = lambda ap: ap.rearrange("p (c s) -> p c s", s=HD)
                tiles = lambda ap: ap.rearrange("p (t c) -> p t c", t=TT)
                bc = lambda m: m.unsqueeze(1).broadcast_to([P, TT, P])
                ahead(L, "in_c", lap, 0)
                dve.wait_ge(rkv_in, 48 * (n + L) + 48)
                W(w_pe, RW_PE, "var", 1)
                for after, i, dst, name in ((None, 1, k_, "k"), ("k", 0, r_, "r"), ("r", 2, v_, "v")):
                    if after:
                        mine(after)
                    done(dve.tensor_tensor(shift[:], zr[:, i, 0:SEQ], zr[:, i, 1:SEQ + 1], ALU.subtract), "d" + name)
                    mine("d" + name)
                    done(dve.scalar_tensor_tensor(dst[:], shift[:], col("rwkv_mu", 4 * i), zr[:, i, 1:SEQ + 1],
                                                  ALU.mult, ALU.add), name)
                W(w_act, RW_ACT, "w")
                dve.wait_ge(yb_out, 16 * n + 16)
                done(dve.tensor_tensor_scan(cs[:], seg64[:], w_[:], 0.0, ALU.mult, ALU.add), "cs")
                W(w_act, RW_ACT, "a")
                mine("v")
                done(dve.tensor_scalar(shift[:], a_[:], 1.0, col("rwkv_k_a"), ALU.subtract, ALU.mult), "ka")
                mine("ka")
                done(dve.scalar_tensor_tensor(kp[:], shift[:], 1.0, k_[:], ALU.add, ALU.mult), "kp")
                mine("kp")
                done(dve.scalar_tensor_tensor(rk[:], r_[:], col("rwkv_r_k"), kp[:], ALU.mult, ALU.mult), "rk")
                W(w_pe, RW_PE, "kk_norm")
                done(dve.tensor_scalar(tmp[:], bank[4][:], 1e-24, None, ALU.max), "kmax")
                stage_take(L, "in_c", lap, 0, 0)
                W(w_act, RW_ACT, "kk_root")
                done(dve.reciprocal(tmp[:], tmp[:]), "krs")
                ahead(L, "in_c", lap, 1)
                mine("krs")
                done(dve.tensor_tensor(kk[:], kk[:], tmp[:], ALU.mult), "kk")
                mine("kk")
                W(w_pool, RW_POOL, "a_inc")
                done(dve.tensor_tensor(bb[:], kk[:], a_[:], ALU.mult), "b")
                W(w_act, RW_ACT, "dec")
                done(dve.tensor_tensor(chunks(kq[:])[:, :, 1:HD], chunks(kk[:])[:, :, 1:HD], chunks(dec[:])[:, :, 0:HD - 1],
                                       ALU.mult), "kq")
                last = chunks(dec[:])[:, :, HD - 1:HD].broadcast_to([P, C, HD])
                mine("b")
                done(dve.tensor_tensor(chunks(bh[:]), chunks(bb[:]), last, ALU.mult), "bh")
                W(w_pe, RW_PE, "bonus")
                done(dve.tensor_tensor(bonus[:], bank[5][:], v_[:], ALU.mult), "bonus")
                W(w_pool, RW_POOL, "kt")
                done(dve.tensor_tensor(chunks(kh[:]), chunks(kp[:]), last, ALU.mult), "kh")
                ahead(L, "in_c", lap, 2)
                stage_take(L, "in_c", lap, 1, 1)
                for h in range(2):
                    W(w_pe, RW_PE, f"A1T_{h}")
                    done(dve.tensor_tensor(NT[:, h, :, :], tiles(bank[6 + h][:]), bc(before[:]), ALU.mult), f"NT_{h}")
                for h in range(2):
                    W(w_pe, RW_PE, f"A1_{h}")
                    done(dve.tensor_tensor(X[:, h, :, :], tiles(bank[4 + h][:]), bc(low[:, 0, :]), ALU.mult), f"X_{h}")
                for h in range(2):
                    W(w_pe, RW_PE, f"A2T_{h}")
                    done(dve.tensor_tensor(T1[:, h, :, :], tiles(bank[6 + h][:]), bc(before[:]), ALU.mult), f"A2T_{h}")
                for l in range(1, LEVELS - 1):
                    for h in range(2):
                        W(w_pe, RW_PE, f"T{l}_{h}")
                        done(dve.tensor_tensor(T1[:, h, :, :], tiles(bank[4 + h][:]), bc(low[:, l, :]), ALU.mult), f"T{l}_{h}")
                    for h in range(2):
                        W(w_pe, RW_PE, f"X{l}_{h}")
                        done(dve.tensor_tensor(XT[:, h, :, :], tiles(bank[6 + h][:]), XT[:, h, :, :], ALU.add), f"XT{l}_{h}")
                    if l < LEVELS - 2:
                        for h in range(2):
                            done(dve.tensor_tensor(X[:, h, :, :], tiles(bank[4 + h][:]), X[:, h, :, :], ALU.add), f"X{l}_{h}")
                for h in range(2):
                    W(w_pe, RW_PE, f"B1T_{h}")
                    done(dve.tensor_tensor(NT[:, h, :, :], tiles(bank[6 + h][:]), bc(upto[:]), ALU.mult), f"B1T_{h}")
                for h in range(2):
                    W(w_pe, RW_PE, f"B2T_{h}")
                    done(dve.tensor_tensor(X[:, h, :, :], tiles(bank[4 + h][:]), bc(upto[:]), ALU.mult), f"B2T_{h}")
                ahead(L, "in_c", lap, 3)
                W(w_pe, RW_PE, "R2")
                done(dve.tensor_tensor(r_[:], bank[6][:], r_[:], ALU.add), "R2")
                W(w_pool, RW_POOL, "ediag")
                for par, b in ((0, bank[7]), (1, bank[4])):
                    W(w_pe, RW_PE, f"state_{par}")
                    W(w_act, RW_ACT, f"NZ_{par}")
                    for h in range(2):
                        hc = slice(h * HD, (h + 1) * HD)
                        every = lambda ap: ap.rearrange("p (t a) c -> p a t c", a=2)[hc, par, :, :]
                        done(dve.tensor_tensor(every(MT[:])[:, :, hc], b[hc, 0:TT * HD].rearrange("p (t c) -> p t c", t=TT),
                                               every(ediag[:]), ALU.add), "MT" if par and h else f"M{par}{h}")
                done(dve.tensor_copy(Z[:, 1, :], NZ[:, 0, :]), "Z1")
                for c in range(2, C):
                    W(w_pe, RW_PE, f"Z{c}")
                    done(dve.tensor_tensor(Z[:, c, :], bank[5][:, (c - 1) * HD:c * HD], NZ[:, c - 1, :], ALU.add), f"Z{c}")
                stage_take(L, "in_c", lap, 2, 2)
                stage_take(L, "in_c", lap, 3, 3)
                W(w_pe, RW_PE, "y_1")
                done(dve.tensor_copy(y_[HD:P, :], bank[4][HD:P, :]), "y_1")
                W(w_pe, RW_PE, "mean")
                done(dve.scalar_tensor_tensor(y_[:], bank[5][:], -1.0 / HD, y_[:], ALU.mult, ALU.add), "yc")
                W(w_act, RW_ACT, "y_sd")
                done(dve.reciprocal(tmp[:], tmp[:]), "yrs")
                mine("yrs")
                done(dve.tensor_tensor(y_[:], y_[:], tmp[:], ALU.mult), "yn")
                assert order == RW_DVE, order

            def hgrn_lap(L, lap):
                n = dve.snap(L * PAIRS + lap)
                order = []
                done = lambda ins, name: pe_mark(ins, h_dve, HG_DVE, name, order)
                W = lambda sig, table, name, back=0: dve.wait_ge(sig.sem, sig.at(step(table, n - back, name)))
                mine = lambda name: W(h_dve, HG_DVE, name)
                tiles = lambda ap: ap.rearrange("p (t c) -> p t c", t=TT)
                head = bass.ds(n, 1)
                W(h_act, HG_ACT, "sig_f")
                done(dve.tensor_scalar(fg[:], fg[:], lb_rest[:, head], lb[:, head], ALU.mult, ALU.add), "fl")
                mine("fl")
                done(dve.tensor_scalar(fg[:], fg[:], LN_MIN, None, ALU.max), "f")
                ahead(L, "in_gates", lap, 0)

                def rel(l):
                    m = 1 << l
                    blocks = lambda ap: ap.rearrange("p (b s) -> p b s", s=2 * m)
                    if l >= 2:
                        W(h_act, HG_ACT, f"ex{l - 2}")
                    if l == 0:
                        mine("bsum")
                        W(h_pe, HG_PE, "hk", 1)
                    done(dve.tensor_tensor(blocks(dd[:, l % 2, :]), blocks(bsum[:]),
                                           blocks(bsum[:])[:, :, m - 1:m].broadcast_to([P, SEQ // (2 * m), 2 * m]),
                                           ALU.subtract), f"d{l}")

                def peaks(j):
                    sink = sinks[:, bass.ds(dve.snap(n * 2 + j), 1)]
                    pairs = lambda g: sc[:, j, 2 * g:2 * g + 2, :]
                    W(h_pe, HG_PE, f"scores_{j}0")
                    done(dve.tensor_tensor(pairs(0), bank[4 + 2 * j][:].rearrange("p (t c) -> p t c", t=2),
                                           band[:].rearrange("p (t a) c -> p t (a c)", t=2), ALU.add), f"m0_{j}")
                    W(h_pe, HG_PE, f"scores_{j}1")
                    done(dve.tensor_tensor(pairs(1), bank[5 + 2 * j][:].rearrange("p (t c) -> p t c", t=2),
                                           band[:, 2:4, :].rearrange("p a c -> p (a c)").unsqueeze(1).broadcast_to([P, 2, 2 * P]),
                                           ALU.add), f"m1_{j}")
                    mine(f"m1_{j}")
                    done(dve.tensor_reduce(small[:, j, 0, :], sc[:, j, :, :], AX.X, ALU.max), f"mx_{j}")
                    mine(f"mx_{j}")
                    done(dve.tensor_scalar(small[:, j, 1, :], small[:, j, 0, :], sink, -1.0, ALU.max, ALU.mult), f"max_{j}")

                def probabilities(j):
                    W(h_act, HG_ACT, f"esink_{j}")
                    done(dve.tensor_tensor(small[:, j, 4, :], small[:, j, 2, :], small[:, j, 3, :], ALU.add), f"den_{j}")
                    mine(f"den_{j}")
                    done(dve.reciprocal(small[:, j, 5, :], small[:, j, 4, :]), f"rec_{j}")
                    mine(f"rec_{j}")
                    done(dve.tensor_tensor(sc[:, j, :, :], sc[:, j, :, :], small[:, j, 5, :].unsqueeze(2).broadcast_to([P, TT, 2 * P]),
                                           ALU.mult), f"probs_{j}")

                peaks(0)
                W(h_act, HG_ACT, "logf")
                done(dve.tensor_tensor_scan(bsum[:], seg128[:], logf[:], 0.0, ALU.mult, ALU.add), "bsum")
                stage_take(L, "in_gates", lap, 0, 0, split_before=True)
                ahead(L, "in_gates", lap, 1)
                peaks(1)
                rel(0)
                rel(1)
                probabilities(0)
                stage_take(L, "in_gates", lap, 1, 1, split_before=True)
                probabilities(1)
                stage_take(L, "in_gates", lap, 2, 2)

                def place(l, between):
                    W(h_pe, HG_PE, f"att{l}")
                    if l == 0:
                        W(h_pe, HG_PE, "o", 1)
                    dve.wait_ge(l_dve.sem, l_dve.at(step(LY_DVE, L, "att_zero")))
                    if l:
                        mine(f"att{l - 1}")
                    between()
                    done(dve.copy_predicated(attT[:], pair_mask[:, l, :].unsqueeze(1).broadcast_to([P, TT, P]),
                                             tiles(bank[6 + l % 2][:])), f"att{l}")

                def from_state():
                    W(h_act, HG_ACT, "eb")
                    done(dve.tensor_tensor(qb[:], hq[:], logf[:], ALU.mult), "qb")

                def to_state():
                    W(h_act, HG_ACT, f"ex{LEVELS - 2}")
                    by_tile = lambda ap: ap.rearrange("p (b s) -> p b s", s=P)
                    done(dve.tensor_tensor(by_tile(dd[:, 1, :]), by_tile(bsum[:]),
                                           by_tile(bsum[:])[:, :, P - 1:P].broadcast_to([P, TT, P]), ALU.subtract), "dend")

                def first_state():
                    W(h_pe, HG_PE, "dS")
                    done(dve.tensor_copy(S[:, 1, :], bank[5][:, 0:P]), "S1")
                for l in range(LEVELS):
                    if l == 4:
                        stage_take(L, "in_gates", lap, 3, 3)
                    if l == 6:
                        ahead(L, "in_gates", lap, 4)
                    place(l, (lambda: rel(l + 2)) if l < LEVELS - 2 else from_state if l == LEVELS - 2 else to_state)
                place(LEVELS, first_state)
                for t in (2, 3):
                    mine(f"S{t - 1}")
                    done(dve.scalar_tensor_tensor(S[:, t, :], S[:, t - 1, :], logf[:, t * P - 1:t * P], bank[5][:, (t - 1) * P:t * P],
                                                  ALU.mult, ALU.add), f"S{t}")
                stage_take(L, "in_gates", lap, 4, 0, 2, split_before=True)
                stage_take(L, "in_gates", lap, 5, 1, 2)
                W(h_act, HG_ACT, "o_sd")
                done(dve.reciprocal(hsq[:], hsq[:]), "orec")
                mine("orec")
                done(dve.tensor_tensor(ho[:], ho[:], hsq[:], ALU.mult), "on")
                mine("on")
                done(dve.scalar_tensor_tensor(ho[:], ho[:], lc[:, COL["hgrn_norm"]:COL["hgrn_norm"] + 1], hog[:],
                                              ALU.mult, ALU.mult), "y")
                assert order == HG_DVE, order

            def mixer(L):
                norm(4 * L + 1)
                mark = lambda ins: ins.then_inc(l_dve.sem, 1)
                mine = lambda name: dve.wait_ge(l_dve.sem, l_dve.at(step(LY_DVE, L, name)))

                def in_lap(lap):
                    for q in range(2):
                        stage_take(L, "in_ab", lap, q, q)
                in_lap(0)
                mark(dve.memset(zr[:, :, 0], 0.0))
                mark(dve.memset(MT[:], 0.0))
                with dve.Fori(1, 4) as lap:
                    in_lap(lap)
                dve.wait_ge(wag_in, 32 * L + 32)
                for i, (dst, name) in enumerate(((xwa, "wa"), (xgs, "g"))):
                    if i:
                        mine("wa")
                    mark(dve.tensor_tensor(shift[:], zr[:, i, 0:SEQ], zr[:, i, 1:SEQ + 1], ALU.subtract))
                    mine("d" + name)
                    mark(dve.scalar_tensor_tensor(dst[:], shift[:], lc[:, COL["rwkv_mu"] + 12 + i:COL["rwkv_mu"] + 13 + i],
                                                  zr[:, i, 1:SEQ + 1], ALU.mult, ALU.add))
                with dve.Fori(4, 10) as lap:
                    in_lap(lap)
                dve.wait_ge(masks.sem, MASK_STEPS)
                with dve.Fori(0, PAIRS) as lap:
                    rwkv_lap(L, lap)
                dve.wait_ge(w_act.sem, w_act.at(step(RW_ACT, 4 * L + 3, "y_sd")))
                dve.wait_ge(yb_out, 16 * (4 * L) + (64 + 16))
                mark(dve.memset(attT[:], 0.0))
                with dve.Fori(0, PAIRS) as lap:
                    hgrn_lap(L, lap)
                for tile in range(PAIRS, 12):
                    dve.wait_ge(m_hi.sem, m_hi.at(12 * L + tile + 1))
                    dve.tensor_tensor(ylo[:, tile, :], yraw[:, tile % Y_RAW, :], yhi[:, tile, :].bitcast(F32), ALU.subtract)\
                       .then_inc(m_lo.sem, 1)
                with dve.Fori(0, KD // 2) as lap:
                    for i in range(2):
                        u = 8 * L + 2 * lap + (i + 1)
                        for br in range(3):
                            q = 3 * i + br
                            ahead(L, "merge", lap, q, W_BUF if q == 5 else PAIRS * P)
                            dve.wait_ge(used[q % 2].sem, used[q % 2].at(SLOT.nth(L, "merge", lap, q // 2 + 1)))
                            if br == 0:
                                dve.wait_ge(m_sig.sem, m_sig.at(u))
                                dve.wait_ge(m_mlo.sem, m_mlo.at(u - 1))
                            if br == 2:
                                dve.wait_ge(acc_step.sem, acc_step.at(u))
                            dve.tensor_tensor(acc[:, min(br, 1), :], bank[q][:], gates[:, i, br, :], ALU.mult).then_inc(read[q].sem, 1)
                            dve.wait_ge(read[q].sem, read[q].at(BANK[q].nth(L, "merge", lap)))
                            if br:
                                dve.tensor_tensor(acc[:, 0, :], acc[:, 0, :], acc[:, 1, :], ALU.add)\
                                   .then_inc((acc_step if br == 1 else m_sum).sem, 1)
                with dve.Fori(0, KD // 2) as lap:
                    for q in range(2):
                        m = dve.snap(lap * 2 + q)
                        ahead(L, "w_o", lap, q)
                        dve.wait_ge(used[q].sem, used[q].at(SLOT.nth(L, "w_o", lap)))
                        dve.tensor_tensor(x[:, m, :], bank[q][:], x[:, m, :], ALU.add).then_inc(read[q].sem, 1)
                        prep(4 * L + 2, m, lc[:, bass.ds(dve.snap(m + COL["ffn2_norm"]), 1)], ghi, glo)

            for m in range(KD):
                prep(0, m, cols[:, m:m + 1], fhi, flo)
            with dve.Fori(0, DEPTH) as L:
                dve.wait_ge(g_sq.sem, g_sq.at(8 * (4 * L) + 8))
                dve.wait_ge(g_lo.sem, g_lo.at(8 * (4 * L) + 8))
                dve.tensor_copy(lc[:, 0:LAYER_COLS], cols[:, bass.ds(dve.snap(L * LAYER_COLS), LAYER_COLS)])\
                   .then_inc(lc_copied.sem, 1)
                dve.tensor_copy(lc[:, LAYER_COLS:LAYER_COLS + 8], cols[:, bass.ds(dve.snap(L * LAYER_COLS + LAYER_COLS), 8)])\
                   .then_inc(lc_ready.sem, 1)
                split(L, "f1a_up", 0, 1, 0)
                ffn(L, 1, 4 * L, COL["mix_norm"])
                mixer(L)
                ffn(L, 2, 4 * L + 2, COL["ple_norm"])
                for m in range(2):
                    dve.wait_ge(p_turned.sem, p_turned.at(2 * L + m + 1))
                    dve.tensor_copy(pT[:, m, :], bank[4 + m][:]).then_inc(p_copied.sem, 1)
                norm(4 * L + 3)

                def ple_lap(lap, last):
                    for i in range(2):
                        n = 8 * L + 2 * lap + i + 1
                        m = lap * 2 + i if last else dve.snap(lap * 2 + i)
                        split(L, "ple", lap, i + 1, 1, 2 * P)
                        dve.wait_ge(p_add.sem, p_add.at(n - 1))
                        take(L, 4 * L + 3, "ple", lap, 2 * i, 0, i + 1, pgate[:, i, :])
                        if not (last and i == 1):
                            split(L, "ple", lap, i + 2, 0)
                        dve.wait_ge(p_sig.sem, p_sig.at(n))
                        dve.wait_ge(used[1].sem, used[1].at(SLOT.nth(L, "ple", lap, i + 1)))
                        dve.tensor_tensor(pprod[:, i, :], bank[2 * i + 1][:], pgate[:, i, :], ALU.mult).then_inc(read[2 * i + 1].sem, 1)
                        dve.wait_ge(read[2 * i + 1].sem, read[2 * i + 1].at(BANK[2 * i + 1].nth(L, "ple", lap)))
                        dve.tensor_tensor(x[:, m, :], x[:, m, :], pprod[:, i, :], ALU.add).then_inc(p_add.sem, 1)
                        gain = lc[:, NEXT_GAIN + m:NEXT_GAIN + m + 1] if last else lc[:, bass.ds(dve.snap(m + NEXT_GAIN), 1)]
                        prep(4 * L + 4, m, gain, fhi, flo)
                with dve.Fori(0, KD // 2 - 1) as lap:
                    ple_lap(lap, False)
                ple_lap(KD // 2 - 1, True)
            norm(4 * DEPTH)
            dve.wait_ge(n_rstd.sem, n_rstd.at(4 * DEPTH + 1))
            for m in range(KD):
                dve.scalar_tensor_tensor(fin[:, m, :], x[:, m, :], lc[:, NEXT_GAIN + m:NEXT_GAIN + m + 1], rstd[:],
                                         ALU.mult, ALU.mult).then_inc(out_new.sem, 1)
            for n in range(2 * TT):
                dve.wait_ge(turned.sem, DEPTH + KD + n + 1)
                dve.tensor_copy(fout[:, n // 2, (n % 2) * SEQ:(n % 2 + 1) * SEQ], bank[n % 6][:]).then_inc(out_copied.sem, 1)


_INS = ['x', 'p', 'ffn1_norm', 'ffn1_w_gate', 'ffn1_w_up', 'ffn1_w_down', 'mix_norm', 'w_in', 'attn_sinks',
        'rwkv_mu', 'rwkv_w0', 'rwkv_w_up', 'rwkv_a0', 'rwkv_a_up', 'rwkv_g_up', 'rwkv_k_k', 'rwkv_k_a', 'rwkv_r_k',
        'rwkv_ln_w', 'rwkv_ln_b', 'hgrn_lb', 'hgrn_norm', 'w_branch', 'w_o', 'ffn2_norm', 'ffn2_w_gate', 'ffn2_w_up',
        'ffn2_w_down', 'ple_norm', 'ple_w_gate', 'ple_w_proj', 'final_norm']


def kernel(**inputs):
    import concourse.bacc as _bacc
    from concourse.bass_utils import run_bass_kernel_spmd as _run

    nc = _bacc.Bacc("TRN2", target_bir_lowering=False, num_devices=1)
    arrays, args = {}, {}
    for name in _INS:
        a = np.ascontiguousarray(inputs[name])
        arrays[f"in_{name}_dram"] = a
        args[name] = nc.dram_tensor(f"in_{name}_dram", a.shape, mybir.dt.from_np(a.dtype), kind="ExternalInput").ap()
    out = nc.dram_tensor("out_0_dram", (1, SEQ, D), F32, kind="ExternalOutput").ap()
    build_trunk(nc, args, out)
    r = _run(nc, [arrays], core_ids=[0])
    return r.results[0]["out_0_dram"]
```
